# Optimizing a Trainium2 kernel written in Bass

```python
import math
import jax
import jax.numpy as jnp
from jax import lax
import numpy as np

D_MODEL = 1024
BATCH = 1
SEQ = 256
DEPTH = 2
DEC_BATCH = 8
DEC_SEQ = 8
PAST_LEN = 2048
PAGE_SIZE = 128

N_AB_LAYERS = (DEPTH + 1) // 2
N_C_LAYERS = DEPTH // 2
CONV_W = 4
CHUNK = 64
EPS = 1e-6
GDN_HEADS = D_MODEL // 256
GDN_DK = 128
GDN_DV = 128
GDN_QK = GDN_HEADS * GDN_DK
GDN_V = GDN_HEADS * GDN_DV
GDN_CONV_DIM = 2 * GDN_QK + GDN_V
HG_HEADS = D_MODEL // 256
HG_DK = 128
HG_DV = 128
HG_K = HG_HEADS * HG_DK
HG_V = HG_HEADS * HG_DV
AB_SPLIT = (GDN_CONV_DIM, GDN_V, GDN_HEADS, GDN_HEADS, HG_K, HG_K, HG_V, HG_V)
AB_IN = GDN_CONV_DIM + GDN_V + 2 * GDN_HEADS + 2 * HG_K + 2 * HG_V
AB_OUT = GDN_V + HG_V
SSD_DINNER = 2 * D_MODEL
SSD_HEADDIM = 64
SSD_HEADS = SSD_DINNER // SSD_HEADDIM
SSD_GROUPS = 4
SSD_HPG = SSD_HEADS // SSD_GROUPS
SSD_STATE = 128
SSD_BC = SSD_GROUPS * SSD_STATE
SSD_CONV_DIM = SSD_DINNER + 2 * SSD_BC
SSD_IN = SSD_DINNER + SSD_CONV_DIM + SSD_HEADS
N_EXPERTS = 16
N_EXPERT_GROUPS = 4
EXPERTS_PER_GROUP = N_EXPERTS // N_EXPERT_GROUPS
TOP_K = 2
D_EXPERT = D_MODEL // 2

kernel_name = 'hybrid_gdn_hgrn2_ssd_moe_step'

def _rmsnorm(x, gain):
    xf = x.astype(jnp.float32)
    xf = xf * lax.rsqrt(jnp.mean(xf * xf, axis=-1, keepdims=True) + EPS)
    return (xf * gain.astype(jnp.float32)).astype(x.dtype)

def _l2norm(x):
    return x * lax.rsqrt(jnp.sum(x * x, axis=-1, keepdims=True) + EPS)

def _split(a, sizes):
    return jnp.split(a, np.cumsum(sizes)[:-1].tolist(), axis=-1)

def _causal_conv(u, buf, w):
    length = u.shape[1]
    up = jnp.concatenate([buf.astype(u.dtype), u], axis=1)
    out = up[:, 0:length] * w[0]
    for j in range(1, CONV_W):
        out = out + up[:, j:j + length] * w[j]
    return out, up[:, length:]

def _to_chunks(a, c):
    b, length = a.shape[:2]
    return jnp.swapaxes(a.reshape((b, length // c, c) + a.shape[2:]), 0, 1)

def _from_chunks(a):
    a = jnp.swapaxes(a, 0, 1)
    return a.reshape((a.shape[0], a.shape[1] * a.shape[2]) + a.shape[3:])

def _gated_delta_rule(q, k, v, g, beta, s0):
    c = math.gcd(q.shape[1], CHUNK)
    incl = jnp.tril(jnp.ones((c, c), dtype=bool))
    strict = jnp.tril(jnp.ones((c, c), dtype=bool), -1)
    eye = jnp.eye(c, dtype=jnp.float32)

    def step(s, inp):
        qc, kc, vc, gc, bc = inp
        gam = jnp.cumsum(gc, axis=1)
        gam_h = jnp.swapaxes(gam, 1, 2)
        decay = jnp.exp(jnp.where(incl, gam_h[..., :, None] - gam_h[..., None, :], -jnp.inf))
        kk = jnp.einsum('bthk,bshk->bhts', kc, kc)
        lower = jnp.where(strict, jnp.swapaxes(bc, 1, 2)[..., :, None] * kk * decay, 0.0)
        rhs = jnp.concatenate([bc[..., None] * vc, (bc * jnp.exp(gam))[..., None] * kc], axis=-1)
        sol = lax.linalg.triangular_solve(eye + lower, jnp.swapaxes(rhs, 1, 2), left_side=True,
                                          lower=True, unit_diagonal=True)
        u, w = sol[..., :GDN_DV], sol[..., GDN_DV:]
        v_new = u - jnp.einsum('bhsk,bhkv->bhsv', w, s)
        qk = jnp.einsum('bthk,bshk->bhts', qc, kc) * decay
        o = (jnp.einsum('bthk,bhkv->bhtv', qc * jnp.exp(gam)[..., None], s)
             + jnp.einsum('bhts,bhsv->bhtv', qk, v_new))
        k_end = kc * jnp.exp(gam[:, -1:] - gam)[..., None]
        s = jnp.exp(gam_h[..., -1])[..., None, None] * s + jnp.einsum('bshk,bhsv->bhkv', k_end, v_new)
        return s, jnp.swapaxes(o, 1, 2)

    xs = (_to_chunks(q, c), _to_chunks(k, c), _to_chunks(v, c), _to_chunks(g, c), _to_chunks(beta, c))
    s, o = lax.scan(step, s0, xs)
    return _from_chunks(o), s

def _gla_recurrence(q, k, v, log_f, s0):
    c = math.gcd(q.shape[1], CHUNK)
    incl = jnp.tril(jnp.ones((c, c), dtype=bool))[:, :, None, None]

    def step(s, inp):
        qc, kc, vc, fc = inp
        cum = jnp.cumsum(fc, axis=1)
        decay = jnp.exp(jnp.where(incl, cum[:, :, None] - cum[:, None, :], -jnp.inf))
        att = jnp.einsum('bthk,btshk->btsh', qc, decay * kc[:, None])
        o = (jnp.einsum('bthk,bhkv->bthv', qc * jnp.exp(cum), s)
             + jnp.einsum('btsh,bshv->bthv', att, vc))
        k_end = kc * jnp.exp(cum[:, -1:] - cum)
        s = jnp.exp(cum[:, -1])[..., None] * s + jnp.einsum('bshk,bshv->bhkv', k_end, vc)
        return s, o

    xs = (_to_chunks(q, c), _to_chunks(k, c), _to_chunks(v, c), _to_chunks(log_f, c))
    s, o = lax.scan(step, s0, xs)
    return _from_chunks(o), s

def _ssd_scan(x, dt, a, bm, cm, s0):
    c = math.gcd(x.shape[1], CHUNK)
    incl = jnp.tril(jnp.ones((c, c), dtype=bool))[:, :, None, None]

    def step(s, inp):
        xc, dtc, bc, cc = inp
        cum = jnp.cumsum(dtc * a, axis=1)
        seg = jnp.exp(jnp.where(incl, cum[:, :, None] - cum[:, None, :], -jnp.inf))
        cb = jnp.einsum('btgn,bsgn->btsg', cc, bc)
        y = jnp.einsum('btsgr,bsgrp->btgrp', cb[..., None] * seg * dtc[:, None], xc)
        y = y + jnp.einsum('btgn,bgrpn->btgrp', cc, s) * jnp.exp(cum)[..., None]
        x_end = xc * (jnp.exp(cum[:, -1:] - cum) * dtc)[..., None]
        s = jnp.exp(cum[:, -1])[..., None, None] * s + jnp.einsum('bsgn,bsgrp->bgrpn', bc, x_end)
        return s, y

    xs = (_to_chunks(x, c), _to_chunks(dt, c), _to_chunks(bm, c), _to_chunks(cm, c))
    s, y = lax.scan(step, s0, xs)
    return _from_chunks(y), s

def _mixer_ab(h, p, i, lb, s_gdn, conv_gdn, s_hg):
    b, length, _ = h.shape
    f32 = jnp.float32
    conv_in, z, beta_pre, a_pre, hq, hf, hi, hgate = _split(h @ p['ab_w_in'][i], AB_SPLIT)
    conv_out, conv_new = _causal_conv(conv_in, conv_gdn, p['ab_conv_w'][i])
    q, k, v = _split(jax.nn.silu(conv_out).astype(f32), (GDN_QK, GDN_QK, GDN_V))
    q = _l2norm(q.reshape(b, length, GDN_HEADS, GDN_DK)) * (GDN_DK ** -0.5)
    k = _l2norm(k.reshape(b, length, GDN_HEADS, GDN_DK))
    v = v.reshape(b, length, GDN_HEADS, GDN_DV)
    beta = jax.nn.sigmoid(beta_pre.astype(f32))
    g = -jnp.exp(p['gdn_a_log'][i].astype(f32)) * jax.nn.softplus(a_pre.astype(f32) + p['gdn_dt_bias'][i].astype(f32))
    o_a, s_gdn_new = _gated_delta_rule(q, k, v, g, beta, s_gdn.astype(f32))
    o_a = _rmsnorm(o_a, p['gdn_norm'][i]) * jax.nn.silu(z.astype(f32)).reshape(b, length, GDN_HEADS, GDN_DV)
    lb = lb.reshape(HG_HEADS, HG_DK)
    log_f = jnp.logaddexp(jnp.log(lb), jnp.log1p(-lb) + jax.nn.log_sigmoid(hf.astype(f32).reshape(b, length, HG_HEADS, HG_DK)))
    k_b = -jnp.expm1(log_f)
    q_b = hq.astype(f32).reshape(b, length, HG_HEADS, HG_DK) * (HG_DK ** -0.5)
    v_b = hi.astype(f32).reshape(b, length, HG_HEADS, HG_DV)
    o_b, s_hg_new = _gla_recurrence(q_b, k_b, v_b, log_f, s_hg.astype(f32))
    o_b = _rmsnorm(o_b, p['hgrn_norm'][i]) * jax.nn.silu(hgate.astype(f32)).reshape(b, length, HG_HEADS, HG_DV)
    mixed = jnp.concatenate([o_a.reshape(b, length, GDN_V), o_b.reshape(b, length, HG_V)], axis=-1).astype(h.dtype)
    out = mixed @ p['ab_w_out'][i]
    return out, s_gdn_new.astype(s_gdn.dtype), conv_new.astype(conv_gdn.dtype), s_hg_new.astype(s_hg.dtype)

def _mixer_ssd(h, p, i, s_ssd, conv_ssd):
    b, length, _ = h.shape
    f32 = jnp.float32
    z, xbc, dt_pre = _split(h @ p['ssd_w_in'][i], (SSD_DINNER, SSD_CONV_DIM, SSD_HEADS))
    xbc, conv_new = _causal_conv(xbc, conv_ssd, p['ssd_conv_w'][i])
    xbc = jax.nn.silu(xbc + p['ssd_conv_b'][i]).astype(f32)
    xs, bm, cm = _split(xbc, (SSD_DINNER, SSD_BC, SSD_BC))
    xs = xs.reshape(b, length, SSD_GROUPS, SSD_HPG, SSD_HEADDIM)
    bm = bm.reshape(b, length, SSD_GROUPS, SSD_STATE)
    cm = cm.reshape(b, length, SSD_GROUPS, SSD_STATE)
    dt = jax.nn.softplus(dt_pre.astype(f32) + p['ssd_dt_bias'][i].astype(f32)).reshape(b, length, SSD_GROUPS, SSD_HPG)
    a = -jnp.exp(p['ssd_a_log'][i].astype(f32)).reshape(SSD_GROUPS, SSD_HPG)
    s0 = s_ssd.astype(f32).reshape(b, SSD_GROUPS, SSD_HPG, SSD_HEADDIM, SSD_STATE)
    y, s_new = _ssd_scan(xs, dt, a, bm, cm, s0)
    y = y + p['ssd_d'][i].astype(f32).reshape(SSD_GROUPS, SSD_HPG, 1) * xs
    y = y.reshape(b, length, SSD_DINNER) * jax.nn.silu(z.astype(f32))
    y = _rmsnorm(y.reshape(b, length, SSD_GROUPS, SSD_DINNER // SSD_GROUPS),
                 p['ssd_norm'][i].reshape(SSD_GROUPS, SSD_DINNER // SSD_GROUPS)).reshape(b, length, SSD_DINNER)
    out = y.astype(h.dtype) @ p['ssd_w_out'][i]
    return out, s_new.reshape(s_ssd.shape).astype(s_ssd.dtype), conv_new.astype(conv_ssd.dtype)

def _moe(h, p, layer):
    b, length, d = h.shape
    t = h.reshape(b * length, d)
    scores = jax.nn.sigmoid((t @ p['router_w']).astype(jnp.float32))
    biased = (scores + p['router_b'].astype(jnp.float32)).reshape(-1, N_EXPERT_GROUPS, EXPERTS_PER_GROUP)
    top_val, top_idx = lax.top_k(biased, TOP_K)
    group = jnp.argmax(jnp.sum(top_val, axis=-1), axis=-1)
    local = jnp.take_along_axis(top_idx, group[:, None, None], axis=1)[:, 0]
    expert = group[:, None] * EXPERTS_PER_GROUP + local
    w_sel = jnp.take_along_axis(scores, expert, axis=-1)
    w_sel = w_sel / jnp.sum(w_sel, axis=-1, keepdims=True)
    combine = jnp.einsum('tk,tke->te', w_sel, jax.nn.one_hot(expert, N_EXPERTS, dtype=jnp.float32)).astype(h.dtype)
    act = jax.nn.silu(jnp.einsum('td,edf->tef', t, p['moe_w_gate'][layer])) * jnp.einsum('td,edf->tef', t, p['moe_w_up'][layer])
    y = jnp.einsum('tef,efd->td', act * combine[..., None], p['moe_w_down'][layer])
    return y.reshape(b, length, d)

def _trunk(x, c, s_gdn, c_gdn, s_hg, s_ssd, c_ssd, p):
    lb_all = jnp.cumsum(jax.nn.softmax(p['hgrn_lb_logits'].astype(jnp.float32), axis=0), axis=0)
    n_gdn, n_gconv, n_hg, n_ssd, n_sconv = [], [], [], [], []
    for layer in range(DEPTH):
        i = layer // 2
        mod = jax.nn.silu(c) @ p['w_ada'][layer] + p['b_ada'][layer]
        sh_m, sc_m, g_m, sh_f, sc_f, g_f = jnp.split(mod[:, None, :], 6, axis=-1)
        h = _rmsnorm(x, p['norm_mix'][layer]) * (1 + sc_m) + sh_m
        if layer % 2 == 0:
            out, a1, a2, a3 = _mixer_ab(h, p, i, lb_all[layer], s_gdn[i], c_gdn[i], s_hg[i])
            n_gdn.append(a1)
            n_gconv.append(a2)
            n_hg.append(a3)
        else:
            out, a4, a5 = _mixer_ssd(h, p, i, s_ssd[i], c_ssd[i])
            n_ssd.append(a4)
            n_sconv.append(a5)
        x = x + g_m * out
        h = _rmsnorm(x, p['norm_ffn'][layer]) * (1 + sc_f) + sh_f
        x = x + g_f * _moe(h, p, layer)
    y = _rmsnorm(x, p['norm_final'])
    return y, jnp.stack(n_gdn), jnp.stack(n_gconv), jnp.stack(n_hg), jnp.stack(n_ssd), jnp.stack(n_sconv)

def setup_inputs(seed: int = 0) -> dict:
    key = jax.random.key(seed)
    keys = list(jax.random.split(key, 40))

    def nrm(shape, scale):
        return scale * jax.random.normal(keys.pop(), shape, jnp.float32)

    def unif(shape, lo, hi):
        return jax.random.uniform(keys.pop(), shape, jnp.float32, lo, hi)

    def dt_bias(shape):
        dt = jnp.exp(unif(shape, math.log(1e-3), math.log(1e-1)))
        return dt + jnp.log(-jnp.expm1(-dt))

    d = D_MODEL
    return {
        'x_prompt': nrm((BATCH, SEQ, d), 1.0),
        'x_sample': nrm((DEC_BATCH, DEC_SEQ, d), 1.0),
        'c_prompt': nrm((BATCH, d), 1.0),
        'c_sample': nrm((DEC_BATCH, d), 1.0),
        'state_gdn': nrm((N_AB_LAYERS, DEC_BATCH, GDN_HEADS, GDN_DK, GDN_DV), 0.1),
        'state_gdn_conv': nrm((N_AB_LAYERS, DEC_BATCH, CONV_W - 1, GDN_CONV_DIM), 1.0),
        'state_hgrn': nrm((N_AB_LAYERS, DEC_BATCH, HG_HEADS, HG_DK, HG_DV), 0.5),
        'state_ssd': nrm((N_C_LAYERS, DEC_BATCH, SSD_HEADS, SSD_HEADDIM, SSD_STATE), 0.1),
        'state_ssd_conv': nrm((N_C_LAYERS, DEC_BATCH, CONV_W - 1, SSD_CONV_DIM), 1.0),
        'w_ada': nrm((DEPTH, d, 6 * d), 0.5 * d ** -0.5),
        'b_ada': nrm((DEPTH, 6 * d), 0.02),
        'norm_mix': 1.0 + nrm((DEPTH, d), 0.05),
        'norm_ffn': 1.0 + nrm((DEPTH, d), 0.05),
        'norm_final': 1.0 + nrm((d,), 0.05),
        'ab_w_in': nrm((N_AB_LAYERS, d, AB_IN), d ** -0.5),
        'ab_conv_w': nrm((N_AB_LAYERS, CONV_W, GDN_CONV_DIM), CONV_W ** -0.5),
        'gdn_a_log': jnp.log(unif((N_AB_LAYERS, GDN_HEADS), 1.0, 16.0)),
        'gdn_dt_bias': dt_bias((N_AB_LAYERS, GDN_HEADS)),
        'gdn_norm': 1.0 + nrm((N_AB_LAYERS, GDN_DV), 0.05),
        'hgrn_lb_logits': nrm((DEPTH + 1, HG_K), 1.0),
        'hgrn_norm': 1.0 + nrm((N_AB_LAYERS, HG_DV), 0.05),
        'ab_w_out': nrm((N_AB_LAYERS, AB_OUT, d), AB_OUT ** -0.5),
        'ssd_w_in': nrm((N_C_LAYERS, d, SSD_IN), d ** -0.5),
        'ssd_conv_w': nrm((N_C_LAYERS, CONV_W, SSD_CONV_DIM), CONV_W ** -0.5),
        'ssd_conv_b': nrm((N_C_LAYERS, SSD_CONV_DIM), 0.02),
        'ssd_dt_bias': dt_bias((N_C_LAYERS, SSD_HEADS)),
        'ssd_a_log': jnp.log(unif((N_C_LAYERS, SSD_HEADS), 1.0, 16.0)),
        'ssd_d': 1.0 + nrm((N_C_LAYERS, SSD_HEADS), 0.1),
        'ssd_norm': 1.0 + nrm((N_C_LAYERS, SSD_DINNER), 0.05),
        'ssd_w_out': nrm((N_C_LAYERS, SSD_DINNER, d), SSD_DINNER ** -0.5),
        'router_w': nrm((d, N_EXPERTS), d ** -0.5),
        'router_b': nrm((N_EXPERTS,), 0.01),
        'moe_w_gate': nrm((DEPTH, N_EXPERTS, d, D_EXPERT), d ** -0.5),
        'moe_w_up': nrm((DEPTH, N_EXPERTS, d, D_EXPERT), d ** -0.5),
        'moe_w_down': nrm((DEPTH, N_EXPERTS, D_EXPERT, d), D_EXPERT ** -0.5),
    }

def reference(x_prompt, x_sample, c_prompt, c_sample,
              state_gdn, state_gdn_conv, state_hgrn, state_ssd, state_ssd_conv,
              w_ada, b_ada, norm_mix, norm_ffn, norm_final,
              ab_w_in, ab_conv_w, gdn_a_log, gdn_dt_bias, gdn_norm, hgrn_lb_logits, hgrn_norm, ab_w_out,
              ssd_w_in, ssd_conv_w, ssd_conv_b, ssd_dt_bias, ssd_a_log, ssd_d, ssd_norm, ssd_w_out,
              router_w, router_b, moe_w_gate, moe_w_up, moe_w_down):
    p = {
        'w_ada': w_ada, 'b_ada': b_ada, 'norm_mix': norm_mix, 'norm_ffn': norm_ffn, 'norm_final': norm_final,
        'ab_w_in': ab_w_in, 'ab_conv_w': ab_conv_w, 'gdn_a_log': gdn_a_log, 'gdn_dt_bias': gdn_dt_bias,
        'gdn_norm': gdn_norm, 'hgrn_lb_logits': hgrn_lb_logits, 'hgrn_norm': hgrn_norm, 'ab_w_out': ab_w_out,
        'ssd_w_in': ssd_w_in, 'ssd_conv_w': ssd_conv_w, 'ssd_conv_b': ssd_conv_b, 'ssd_dt_bias': ssd_dt_bias,
        'ssd_a_log': ssd_a_log, 'ssd_d': ssd_d, 'ssd_norm': ssd_norm, 'ssd_w_out': ssd_w_out,
        'router_w': router_w, 'router_b': router_b,
        'moe_w_gate': moe_w_gate, 'moe_w_up': moe_w_up, 'moe_w_down': moe_w_down,
    }
    bp = x_prompt.shape[0]
    dt = x_prompt.dtype
    y_prompt, p_gdn, p_gconv, p_hg, p_ssd, p_sconv = _trunk(
        x_prompt, c_prompt,
        jnp.zeros((N_AB_LAYERS, bp) + state_gdn.shape[2:], dt),
        jnp.zeros((N_AB_LAYERS, bp) + state_gdn_conv.shape[2:], dt),
        jnp.zeros((N_AB_LAYERS, bp) + state_hgrn.shape[2:], dt),
        jnp.zeros((N_C_LAYERS, bp) + state_ssd.shape[2:], dt),
        jnp.zeros((N_C_LAYERS, bp) + state_ssd_conv.shape[2:], dt),
        p)
    y_sample, s_gdn, s_gconv, s_hg, s_ssd, s_sconv = _trunk(
        x_sample, c_sample, state_gdn, state_gdn_conv, state_hgrn, state_ssd, state_ssd_conv, p)
    return (y_prompt, y_sample, p_gdn, p_gconv, p_hg, p_ssd, p_sconv, s_gdn, s_gconv, s_hg, s_ssd, s_sconv)


_drawn_inputs = setup_inputs


def setup_inputs(seed=0):
    import zlib

    import numpy as np

    out = dict(_drawn_inputs(seed))
    spreads = {}
    factors = {'gdn_norm': 3.064, 'ssd_norm': 2.787}
    for name, (base, spread) in spreads.items():
        noise = np.random.default_rng([zlib.crc32(name.encode()), seed]).standard_normal(out[name].shape)
        drawn = base * np.exp(spread * noise) if base else spread * noise
        out[name] = jnp.asarray(drawn.astype(out[name].dtype))
    for name, factor in factors.items():
        out[name] = (out[name] * factor).astype(out[name].dtype)
    return out
```

```python
from contextlib import ExitStack, contextmanager

import numpy as np

import concourse.bass as bass
from concourse import mybir

ALU = mybir.AluOpType
ACT = mybir.ActivationFunctionType
AX = mybir.AxisListType
F32 = mybir.dt.float32
U32 = mybir.dt.uint32

P = 128
D = 1024
DK = D // P
PROMPT = 256
SEQS, SEQ_LEN = 8, 8
T = PROMPT + SEQS * SEQ_LEN
C = 64
PC = PROMPT // C
CHUNKS = PC + 1
MODS = 1 + SEQS
TAPS = 4
PAD = TAPS - 1
UPW = PAD + PROMPT + SEQS * (PAD + SEQ_LEN)
CVW = UPW - PAD
EPS = 1e-6

HEADS = 4
BLOCKS = HEADS * CHUNKS
AB_CONV = 12
AB_TAIL = 2 * HEADS
AB_TAIL_AT = 2048
AB_IN = 4104

SX = 16
SG = 4
SHPG = 8
SH = SG * SHPG
SXBC = 24
SSD_IN = 5152

E = 16
EG, EPG = 4, 4
FT = 4
FE = FT * P

SLOT = 2048
SLOTS = 8
BANKS = 4
BANK = 512
N_AB = 2 * 12 + 2 * 8
N_SSD = N_AB + 2 * 2 + 6 * E + 2 * 12 + 2 * 10
EXPERTS_A_TURN = 4

SMALL = {}
_at = 0
for _name, _n in (("norm_mix", 16), ("norm_ffn", 16), ("norm_final", 8), ("b_ada", 96),
                  ("ab_conv_w", 48), ("gdn_norm", 1), ("hgrn_norm", 1), ("lb_logits", 12),
                  ("ssd_conv_w", 96), ("ssd_conv_b", 24), ("ssd_norm", 16), ("ssd_d", 16),
                  ("gdn_a_log", 4), ("gdn_dt_bias", 4), ("ssd_a_log", 32), ("ssd_dt_bias", 32),
                  ("router_b", 16)):
    SMALL[_name] = (_at, _n)
    _at += _n
SMALL_COLS = _at

LEVELS = (32, 16, 8, 4, 2, 1)
CONST = {}
_at = 0
for _name, _n in (("ones", P), ("ident", P), ("incl", CHUNKS * C), ("after", 2 * C), ("seq", SEQS),
                  ("restart", T), ("eps", 1)):
    CONST[_name] = (_at, _n)
    _at += _n
CONST_COLS = _at


class Count:

    def __init__(self):
        self.n, self.turn = {}, {}

    def at(self, sem, more=0):
        v = self.n.get(id(sem), 0) + more
        if id(sem) in self.turn:
            i, per = self.turn[id(sem)]
            v = i * per + v
        return v

    def up(self, sem, k=1):
        self.n[id(sem)] = self.n.get(id(sem), 0) + k
        return self.at(sem)

    @contextmanager
    def repeat(self, i, turns, per):
        start = {id(s): self.n.get(id(s), 0) for s in per}
        self.turn = {id(s): (i, k) for s, k in per.items()}
        yield
        for s, k in per.items():
            assert self.n[id(s)] - start[id(s)] == k, (self.n[id(s)] - start[id(s)], k)
            self.n[id(s)] = start[id(s)] + turns * k
        self.turn = {}


def spread(ap, axis, n):
    ap = ap.unsqueeze(axis)
    shape = list(ap.shape)
    shape[axis] = n
    return ap.to_broadcast(shape)


def trunk_program(nc, a, out):
    with ExitStack() as ctx:
        def sb(name, cols, parts=P):
            return ctx.enter_context(nc.sbuf_tensor(name, [parts, cols], F32))

        def sem(name):
            return ctx.enter_context(nc.semaphore(name))

        const = sb("const", CONST_COLS)
        small = sb("small", SMALL_COLS)
        x = sb("x", DK * T)
        h = sb("h", DK * T)
        cs = sb("cs", DK * MODS)
        mod = sb("mod", 48 * MODS)
        router = sb("router", DK * E)
        ab_tail = sb("ab_tail", DK * AB_TAIL)
        dt_tail = sb("dt_tail", DK * SH)
        convst = sb("convst", SXBC * SEQS * PAD)
        convnew = sb("convnew", SXBC * MODS * PAD)
        rs = sb("rs", T)
        pool_cols = (nc.sbuf_usable_end - nc.sbuf_base) // 4 - 64
        pool = sb("pool", pool_cols)
        RING = pool_cols - SLOTS * SLOT

        def K(name, parts=P):
            at, n = CONST[name]
            return const[0:parts, at:at + n]

        def W(name):
            at, n = SMALL[name]
            return small[:, at:at + n]

        ones, ident = K("ones"), K("ident")
        ident64 = const[0:C, CONST["ident"][0]:CONST["ident"][0] + C]
        ones64 = const[0:C, CONST["ones"][0]:CONST["ones"][0] + P]
        incl = K("incl", C)
        incl_p, incl_s = incl[:, 0:C], incl[:, PC * C:CHUNKS * C]
        after = K("after", C)
        after_p, after_s = after[:, 0:C], after[:, C:2 * C]
        seq = K("seq", C)
        restart = K("restart")
        eps = K("eps")
        one_col = ones[:, 0:1]

        psum = [ctx.enter_context(nc.psum_tensor(f"bank{i}", [P, BANK], F32)) for i in range(2 * BANKS)]

        def area(at, cols, parts=P):
            return pool[0:parts, at:at + cols]

        def slot(n):
            at = RING + (n % SLOTS) * SLOT
            return pool[:, at:at + SLOT]

        class Plan:
            def __init__(self, *free):
                self.free = [list(f) for f in free]

            def __call__(self, cols, parts=P):
                for f in self.free:
                    if f[1] - f[0] >= cols:
                        f[0] += cols
                        return area(f[0] - cols, cols, parts)
                raise MemoryError((cols, self.free, pool_cols, RING))

        lo = Plan((0, RING))
        UP0 = lo(AB_CONV * UPW)
        CV0 = lo(4 * 348)
        ab_free = AB_CONV * UPW + 4 * 348
        CO0 = lo(AB_CONV * T)
        zs, hq, hk, hf, hv, hg = (lo(HEADS * T) for _ in range(6))
        ab_lo_end = lo.free[0][0]
        B = BLOCKS * C
        g = Plan((0, ab_free), (ab_lo_end, pool_cols))
        levels = g(len(LEVELS) * CHUNKS * C, C)
        SQ = g(2 * HEADS * T)
        UT, WT = SQ[:, 0:B], SQ[:, B:2 * B]
        BK, KEND, BV, VTOK = (g(BLOCKS * P, C) for _ in range(4))
        EDEC, U, QKE = (g(B, C) for _ in range(3))
        MM = g(4 * B)
        M, MT, PROD, CT = (MM[0:C, i * B:(i + 1) * B] for i in range(4))
        BR = CT
        KENDM = MM[0:C, 0:SEQS * HEADS * P]
        GR, EGR = g(B), g(B)
        SS = g(SEQS * HEADS * P)
        OI = CO0[:, 2 * B:3 * B]
        VN = g(HEADS * C)
        S = g(HEADS * P)
        sc = g(400, C)
        k = Plan((0, ab_free), (ab_lo_end, pool_cols))
        assert k(len(LEVELS) * CHUNKS * C, C).offset == levels.offset
        LFC, CUM, ED, EC, KE, OIH = (k(B) for _ in range(6))
        ATT = k(B, C)
        Z = [k(B), k(B)]
        KENDH, VTOKH = k(BLOCKS * P, C), k(BLOCKS * P, C)
        SSH = k(SEQS * HEADS * P)
        KENDMH = k(SEQS * HEADS * P, C)
        SHG = k(HEADS * P)
        LB = k(40)
        lo = Plan((0, RING))
        UP1 = lo(SXBC * UPW)
        CV1 = lo(4 * 348)
        ssd_free = lo.free[0][0]
        CO1 = lo(SXBC * T)
        zs1 = lo(SX * T)
        s = Plan((0, ssd_free), (lo.free[0][0], pool_cols))
        ST = s(SH * C)
        SSS = [s(SEQS * SHPG * C), s(SEQS * SHPG * C)]
        XDT, XEND = s(CHUNKS * SHPG * C, C), s(CHUNKS * SHPG * C, C)
        BTOK, BM, CBM = s(CHUNKS * P, C), s(SEQS * P, C), s(CHUNKS * C, C)
        EG1, GM1, GBC = (s(SHPG * T, C) for _ in range(3))
        ER, YI, SQ1 = s(4 * T), s(4 * T), s(4 * T)
        DEC = s((PC + SEQS) * SH)
        sc1 = s(1800, C)
        GS = GBC[:, 0:SEQS * SH]
        m = Plan((0, RING))
        COMB = m(E * T)
        ACTV = [m(FT * T), m(FT * T)]
        SIL = m(2 * T)
        YACC = m(DK * T)
        R = m(2600, C)

        consts_in = sem("consts_in")
        cond_in = sem("cond_in")
        tails_in = sem("tails_in")
        conv_state_in = sem("conv_state_in")
        levels_in = sem("levels_in")
        gdn_state_in = sem("gdn_state_in")
        hgrn_state_in = sem("hgrn_state_in")
        ssd_state_in = [sem("ssd_state_in0"), sem("ssd_state_in1")]
        weights_in = [sem(f"weights_in{i}") for i in range(SLOTS)]
        weights_used = sem("weights_used")
        act_full, act_free = sem("act_full"), sem("act_free")
        dve_full, dve_free = sem("dve_full"), sem("dve_free")
        act_step, dve_step = sem("act_step"), sem("dve_step")
        mixer_done = sem("mixer_done")
        to_act = sem("to_act")
        to_dve = sem("to_dve")
        pe_from_dve = sem("pe_from_dve")
        pe_from_act = sem("pe_from_act")
        conv_in_ready = sem("conv_in_ready")
        conv_ready = sem("conv_ready")
        conv_silu = sem("conv_silu")
        gate_silu = sem("gate_silu")
        gate_free = sem("gate_free")
        act_ready = sem("act_ready")
        out_ready = sem("out_ready")
        stored = sem("stored")
        stored_state = [sem("stored_state0"), sem("stored_state1")]

        block = ctx.enter_context(nc.Block())

        @block.sync
        def _(sp):
            n = Count()

            def load(src):
                i = n.n.get(id(weights_used), 0)
                if i >= SLOTS:
                    sp.wait_ge(weights_used, n.at(weights_used, 1 - SLOTS))
                n.up(weights_used)
                sp.dma_start(slot(i).rearrange("p (k n) -> p k n", n=src.shape[-1]), src) \
                    .then_inc(weights_in[i % SLOTS], 16)

            def load_square(w, cols, nk, n_groups):
                wk = w.rearrange("(k p) n -> p k n", p=P)
                for c0 in cols[:n_groups]:
                    for k0 in range(0, nk, 4):
                        load(wk[:, k0:k0 + 4, c0:c0 + BANK])

            def experts(layer):
                wg, wu, wd = a["moe_w_gate"][layer], a["moe_w_up"][layer], a["moe_w_down"][layer]
                turns = E // EXPERTS_A_TURN
                with sp.Fori(0, turns) as i:
                    with n.repeat(i, turns, {weights_used: 6 * EXPERTS_A_TURN}):
                        for j in range(EXPERTS_A_TURN):
                            e = bass.ds(i * EXPERTS_A_TURN + j, 1)
                            for w in (wg, wu):
                                wk = w[e].rearrange("o (k p) n -> p (o k) n", p=P)
                                for k0 in (0, 4):
                                    load(wk[:, k0:k0 + 4, :])
                            wk = w_down = wd[e].rearrange("o (k p) n -> p (o k) n", p=P)
                            for k0 in (0, 2):
                                load(wk[:, k0:k0 + 2, :])

            sp.dma_start(cs[:, :].rearrange("p (k n) -> p k n", k=DK), a["c_t"].rearrange("(k p) n -> p k n", p=P)).then_inc(cond_in, 16)
            for dst, src in ((const, a["consts"]), (small, a["small"])):
                sp.dma_start(dst[:, :], src).then_inc(consts_in, 16)
            sp.dma_start(x[:, :].rearrange("p (k n) -> p k n", k=DK), a["x_t"].rearrange("(k p) n -> p k n", p=P)).then_inc(consts_in, 16)
            for dst, src, k_ in ((router, a["router_w"], DK), (ab_tail, a["ab_w_in"][0][:, AB_TAIL_AT:AB_TAIL_AT + AB_TAIL], DK),
                                 (dt_tail, a["ssd_w_in"][0][:, SSD_IN - SH:SSD_IN], DK)):
                sp.dma_start(dst[:, :].rearrange("p (k n) -> p k n", k=k_), src.rearrange("(k p) n -> p k n", p=P)).then_inc(tails_in, 16)
            every = [BANK * i for i in range(12)]
            load_square(a["w_ada"][0], every, DK, 12)
            load_square(a["ab_w_in"][0], [0, 512, 1024, 1536] + [AB_TAIL_AT + AB_TAIL + BANK * i for i in range(4)], DK, 8)
            sp.wait_ge(mixer_done, 1)
            load_square(a["ab_w_out"][0], every, DK, 2)
            experts(0)
            load_square(a["w_ada"][1], every, DK, 12)
            load_square(a["ssd_w_in"][0], [BANK * i for i in range(4, 10)] + [BANK * i for i in range(4)], DK, 10)
            sp.wait_ge(mixer_done, 2)
            load_square(a["ssd_w_out"][0], every, SX, 2)
            experts(1)

        @block.gpsimd
        def _(pool_eng):
            n = Count()

            def store(dst, src):
                pool_eng.wait_ge(out_ready, n.up(out_ready))
                n.up(stored, 16)
                pool_eng.dma_start(dst, src).then_inc(stored, 16)

            pool_eng.dma_start(convst[:, 0:AB_CONV * SEQS * PAD], a["gdn_conv_t"]).then_inc(conv_state_in, 16)
            store(out["gdn_conv"], convnew[:, 0:AB_CONV * MODS * PAD])
            pool_eng.dma_start(convst[:, :], a["ssd_conv_t"]).then_inc(conv_state_in, 16)
            pool_eng.wait_ge(weights_used, N_AB)
            pool_eng.wait_ge(conv_silu, AB_CONV)
            pool_eng.dma_start(levels, a["levels"]).then_inc(levels_in, 16)
            pool_eng.dma_start(SS.rearrange("p (b n) -> p b n", b=SEQS), a["gdn_state"].rearrange("p (b n) -> p b n", b=SEQS)).then_inc(gdn_state_in, 16)
            store(out["gdn_p"], S)
            store(out["gdn_s"], SS)
            pool_eng.wait_ge(out_ready, n.up(out_ready))
            pool_eng.wait_ge(stored, n.at(stored))
            pool_eng.dma_start(SSH.rearrange("p (b n) -> p b n", b=SEQS), a["hgrn_state"].rearrange("p (b n) -> p b n", b=SEQS)).then_inc(hgrn_state_in, 16)
            store(out["hgrn_p"], SHG)
            store(out["hgrn_s"], SSH)
            pool_eng.wait_ge(stored, n.at(stored))
            store(out["ssd_conv"], convnew[:, :])
            pool_eng.wait_ge(weights_used, N_SSD)
            pool_eng.wait_ge(conv_silu, AB_CONV + SXBC)
            for gi in range(SG):
                if gi >= 2:
                    pool_eng.wait_ge(stored_state[gi % 2], 16 * (gi // 2))
                pool_eng.dma_start(SSS[gi % 2].rearrange("p (b n) -> p b n", b=SEQS),
                                   a["ssd_state"][:, :, gi * SHPG * C:(gi + 1) * SHPG * C]).then_inc(ssd_state_in[gi % 2], 16)
                if gi >= 1:
                    q = gi - 1
                    pool_eng.wait_ge(out_ready, n.up(out_ready))
                    pool_eng.dma_start(out["ssd_s"][:, :, q * SHPG * C:(q + 1) * SHPG * C],
                                       SSS[q % 2].rearrange("p (b n) -> p b n", b=SEQS)).then_inc(stored_state[q % 2], 16)
            q = SG - 1
            pool_eng.wait_ge(out_ready, n.up(out_ready))
            pool_eng.dma_start(out["ssd_s"][:, :, q * SHPG * C:(q + 1) * SHPG * C],
                               SSS[q % 2].rearrange("p (b n) -> p b n", b=SEQS)).then_inc(stored_state[q % 2], 16)
            store(out["ssd_p"], ST)
            store(out["y"].rearrange("(k p) n -> p k n", p=P), h[:, :].rearrange("p (k n) -> p k n", k=DK))
            pool_eng.wait_ge(stored, n.at(stored))
            for i in range(2):
                pool_eng.wait_ge(stored_state[i], 16 * SG // 2)

        @block.tensor
        def _(pe):
            n = Count()

            def bank_for_act():
                i = n.n.get(id(act_full), 0)
                if i >= BANKS:
                    pe.wait_ge(act_free, n.at(act_full, 1 - BANKS))
                n.up(act_full)
                return psum[i % BANKS]

            def bank_for_dve():
                i = n.n.get(id(dve_full), 0)
                if i >= BANKS:
                    pe.wait_ge(dve_free, n.at(dve_full, 1 - BANKS))
                n.up(dve_full)
                return psum[BANKS + i % BANKS]

            def slot_read(full):
                pe.wait_ge(full, n.at(full))
                pe.sem_inc(weights_used, 1)

            def next_slot():
                i = n.n.get(id(weights_used), 0)
                n.up(weights_used)
                n.up(weights_in[i % SLOTS], 16)
                pe.wait_ge(weights_in[i % SLOTS], n.at(weights_in[i % SLOTS]))
                return slot(i)

            def from_dve():
                pe.wait_ge(pe_from_dve, n.up(pe_from_dve))

            def from_act():
                pe.wait_ge(pe_from_act, n.up(pe_from_act))

            def projections(rhs, nk, groups, bank, full):
                for _g in range(groups):
                    ws = [next_slot().rearrange("p (k n) -> p k n", n=BANK) for _ in range(nk // 4)]
                    for mt in range(4):
                        b = bank()
                        for kk in range(nk):
                            mm = pe.matmul(b[:, 0:T], ws[kk // 4][:, kk % 4, mt * P:(mt + 1) * P],
                                           rhs[:, kk * T:(kk + 1) * T], start=(kk == 0), stop=(kk == nk - 1))
                            if mt == 3 and kk % 4 == 3 and kk < nk - 1:
                                mm.then_inc(weights_used, 1)
                        mm.then_inc(full, 1)
                    slot_read(full)

            def conditioning():
                from_act()
                for _g in range(12):
                    w0, w1 = (next_slot().rearrange("p (k n) -> p k n", n=BANK) for _ in range(2))
                    b = bank_for_dve()
                    for mt in range(4):
                        for kk in range(DK):
                            mm = pe.matmul(b[:, mt * MODS:(mt + 1) * MODS], (w0, w1)[kk // 4][:, kk % 4, mt * P:(mt + 1) * P],
                                           cs[:, kk * MODS:(kk + 1) * MODS], start=(kk == 0), stop=(kk == DK - 1))
                            if mt == 3 and kk == 3:
                                mm.then_inc(weights_used, 1)
                    mm.then_inc(dve_full, 1)
                    slot_read(dve_full)

            def norm_sum():
                from_act()
                b = bank_for_act()
                for kk in range(DK):
                    mm = pe.matmul(b[:, 0:T], ones, h[:, kk * T:(kk + 1) * T], start=(kk == 0), stop=(kk == DK - 1))
                mm.then_inc(act_full, 1)

            def token_scalars(tail, width):
                b = bank_for_dve()
                for c in range(CHUNKS):
                    for kk in range(DK):
                        mm = pe.matmul(b[0:C, c * width:(c + 1) * width], h[:, kk * T + c * C:kk * T + (c + 1) * C],
                                       tail[:, kk * width:(kk + 1) * width], start=(kk == 0), stop=(kk == DK - 1))
                mm.then_inc(dve_full, 1)

            def decay_sums(gt, nh):
                gp = gt.rearrange("p (h c) -> p h c", c=CHUNKS)
                b = bank_for_dve()
                np_, ns_ = nh * PC, nh
                pe.matmul(b[0:C, 0:np_], incl_p, gp[:, :, 0:PC], start=True, stop=True)
                pe.matmul(b[0:C, np_:np_ + ns_], incl_s, gp[:, :, PC], start=True, stop=True)
                o = np_ + ns_
                pe.matmul(b[0:C, o:o + np_], after_p, gp[:, :, 0:PC], start=True, stop=True)
                pe.matmul(b[0:C, o + np_:o + np_ + ns_], after_s, gp[:, :, PC], start=True, stop=True).then_inc(dve_full, 1)

            def blocks(bank, full, lhs, rhs, count, parts, width):
                per = BANK // width
                for i0 in range(0, count, per):
                    b = bank()
                    for i in range(i0, min(i0 + per, count)):
                        mm = pe.matmul(b[0:parts, (i - i0) * width:(i - i0 + 1) * width], lhs(i), rhs(i), start=True, stop=True)
                    mm.then_inc(full, 1)

            def turned(bank, full, src, count):
                for i0 in range(0, count, 4):
                    b = bank()
                    for i in range(i0, min(i0 + 4, count)):
                        mm = pe.transpose(b[0:C, (i - i0) * P:(i - i0 + 1) * P], src(i), ident)
                    mm.then_inc(full, 1)

            def c64(buf):
                return lambda i: buf[:, i * C:(i + 1) * C]

            def c128(buf):
                return lambda i: buf[:, i * P:(i + 1) * P]

            def head_norm_sum(sq, count):
                for i in range(count):
                    b = bank_for_act()
                    pe.matmul(b[:, 0:T], ones, sq[:, i * T:(i + 1) * T], start=True, stop=True).then_inc(act_full, 1)

            def state_chunk(Sx, QG, WTx, c):
                b = bank_for_dve()
                for hh in range(HEADS):
                    st = Sx[:, hh * P:(hh + 1) * P]
                    cols = slice(hh * T + c * C, hh * T + (c + 1) * C)
                    mm = pe.matmul(b[:, hh * C:(hh + 1) * C], st, QG[:, cols], start=True, stop=True)
                    if WTx is not None:
                        mm = pe.matmul(b[:, (HEADS + hh) * C:(HEADS + hh + 1) * C], st, WTx[:, cols], start=True, stop=True)
                mm.then_inc(dve_full, 1)

            def state_samples(SSx, QG, WTx):
                b = bank_for_dve()
                for s_ in range(SEQS):
                    for hh in range(HEADS):
                        st = SSx[:, (s_ * HEADS + hh) * P:(s_ * HEADS + hh + 1) * P]
                        cols = slice(hh * T + PROMPT + s_ * SEQ_LEN, hh * T + PROMPT + (s_ + 1) * SEQ_LEN)
                        o = hh * C + s_ * SEQ_LEN
                        mm = pe.matmul(b[:, o:o + SEQ_LEN], st, QG[:, cols], start=True, stop=True)
                        if WTx is not None:
                            mm = pe.matmul(b[:, HEADS * C + o:HEADS * C + o + SEQ_LEN], st, WTx[:, cols], start=True, stop=True)
                mm.then_inc(dve_full, 1)

            def update_chunk(kend, vtok, c):
                b = bank_for_dve()
                for hh in range(HEADS):
                    i = hh * CHUNKS + c
                    mm = pe.matmul(b[:, hh * P:(hh + 1) * P], kend[:, i * P:(i + 1) * P], vtok[:, i * P:(i + 1) * P], start=True, stop=True)
                mm.then_inc(dve_full, 1)

            def update_samples(kendm, vtok):
                for s_ in range(SEQS):
                    b = bank_for_dve()
                    for hh in range(HEADS):
                        i = hh * CHUNKS + PC
                        j = s_ * HEADS + hh
                        mm = pe.matmul(b[:, hh * P:(hh + 1) * P], kendm[:, j * P:(j + 1) * P], vtok[:, i * P:(i + 1) * P], start=True, stop=True)
                    mm.then_inc(dve_full, 1)

            def gdn():
                QT, KT, VT = CO0[:, 0:B], CO0[:, B:2 * B], CO0[:, 2 * B:3 * B]
                token_scalars(ab_tail, AB_TAIL)
                projections(h, DK, 8, bank_for_act, act_full)
                from_dve()
                decay_sums(sc[:, 0:BLOCKS], HEADS)
                from_dve()
                for i0 in range(0, B, BANK):
                    b = bank_for_dve()
                    w = min(BANK, B - i0)
                    pe.matmul(b[:, 0:w], ones64, EDEC[:, i0:i0 + w], start=True, stop=True).then_inc(dve_full, 1)
                for i0 in range(0, B, BANK):
                    b = bank_for_dve()
                    w = min(BANK, B - i0)
                    pe.matmul(b[0:C, 0:w], ones64[:, 0:C], U[:, i0:i0 + w], start=True, stop=True).then_inc(dve_full, 1)
                from_act()
                head_norm_sum(SQ, 2 * HEADS)
                from_dve()
                blocks(bank_for_dve, dve_full, c64(KT), c64(KT), BLOCKS, C, C)
                blocks(bank_for_dve, dve_full, c64(KT), c64(QT), BLOCKS, C, C)
                turned(bank_for_dve, dve_full, c64(KT), BLOCKS)
                turned(bank_for_dve, dve_full, c64(VT), BLOCKS)
                for lv in range(len(LEVELS)):
                    ct, mt = (CT, MT) if lv % 2 == 0 else (MT, CT)
                    from_dve()
                    blocks(bank_for_act, act_full, c64(ct), c64(M), BLOCKS, C, C)
                    from_act()
                    blocks(bank_for_dve, dve_full, c64(PROD), c64(mt), BLOCKS, C, C)
                    if lv < len(LEVELS) - 1:
                        blocks(bank_for_dve, dve_full, c64(mt), c64(PROD), BLOCKS, C, C)
                from_dve()
                blocks(bank_for_act, act_full, c128(BV), c64(MT), BLOCKS, P, C)
                blocks(bank_for_act, act_full, c128(BK), c64(MT), BLOCKS, P, C)
                from_act()
                from_dve()
                for c in range(PC):
                    if c:
                        from_dve()
                    state_chunk(S, GR, WT, c)
                    from_dve()
                    b = bank_for_act()
                    for hh in range(HEADS):
                        mm = pe.transpose(b[0:C, hh * P:(hh + 1) * P], VN[:, hh * C:(hh + 1) * C], ident)
                    mm.then_inc(act_full, 1)
                    from_act()
                    update_chunk(KEND, VTOK, c)
                pe.wait_ge(gdn_state_in, 16)
                state_samples(SS, GR, WT)
                from_dve()
                b = bank_for_act()
                for hh in range(HEADS):
                    mm = pe.transpose(b[0:C, hh * P:(hh + 1) * P], VN[:, hh * C:(hh + 1) * C], ident)
                mm.then_inc(act_full, 1)
                from_act()
                from_dve()
                update_samples(KENDM, VTOK)
                blocks(bank_for_dve, dve_full, c128(VTOK), c64(QKE), BLOCKS, P, C)
                from_act()
                head_norm_sum(SQ, HEADS)

            def hgrn():
                from_dve()
                blocks(bank_for_dve, dve_full, c64(hk), c64(hq), BLOCKS, C, C)
                for lv, half in enumerate(LEVELS):
                    from_dve()
                    zz = Z[lv % 2]
                    cs_ = [i for i in range(BLOCKS) if half < SEQ_LEN or i % CHUNKS < PC]
                    per = BANK // C
                    for i0 in range(0, BLOCKS, per):
                        b = bank_for_dve()
                        for i in range(i0, min(i0 + per, BLOCKS)):
                            if i in cs_:
                                mm = pe.matmul(b[0:C, (i - i0) * C:(i - i0 + 1) * C], zz[:, i * C:(i + 1) * C], zz[:, i * C:(i + 1) * C], start=True, stop=True)
                        mm.then_inc(dve_full, 1)
                from_dve()
                turned(bank_for_act, act_full, c64(KE), BLOCKS)
                turned(bank_for_act, act_full, c64(hv), BLOCKS)
                from_act()
                from_dve()
                for c in range(PC):
                    if c:
                        from_dve()
                    state_chunk(SHG, ED, None, c)
                    update_chunk(KENDH, VTOKH, c)
                pe.wait_ge(hgrn_state_in, 16)
                state_samples(SSH, ED, None)
                from_dve()
                update_samples(KENDMH, VTOKH)
                blocks(bank_for_dve, dve_full, c128(VTOKH), c64(ATT), BLOCKS, P, C)
                from_act()
                head_norm_sum(Z[0], HEADS)

            def ssd():
                token_scalars(dt_tail, SH)
                projections(h, DK, 10, bank_for_act, act_full)
                from_dve()
                decay_sums(sc1[:, 0:SH * CHUNKS], SH)
                from_dve()
                b = bank_for_dve()
                gp = sc1[:, 0:SH * CHUNKS].rearrange("p (h c) -> p c h", c=CHUNKS)
                pe.matmul(b[:, 0:PC * SH], ones64, gp[:, 0:PC, :], start=True, stop=True)
                pe.matmul(b[:, PC * SH:(PC + SEQS) * SH], ones64, GS, start=True, stop=True).then_inc(dve_full, 1)
                for gi in range(SG):
                    Bf = CO1[:, (SX + gi) * T:(SX + gi + 1) * T]
                    Cf = CO1[:, (SX + SG + gi) * T:(SX + SG + gi + 1) * T]
                    if gi == 0:
                        from_act()
                    blocks(bank_for_dve, dve_full, c64(Bf), c64(Cf), CHUNKS, C, C)
                    turned(bank_for_act, act_full, c64(Bf), CHUNKS)
                    from_dve()
                    for i0 in range(0, SHPG * T, BANK):
                        b = bank_for_dve()
                        pe.matmul(b[0:C, :], ones64[:, 0:C], GM1[:, i0:i0 + BANK], start=True, stop=True).then_inc(dve_full, 1)
                    for j in range(4):
                        b = bank_for_act()
                        for c in range(CHUNKS):
                            mm = pe.matmul(b[:, c * C:(c + 1) * C], GBC[:, (c * SHPG + 2 * j) * C:(c * SHPG + 2 * j + 2) * C],
                                           incl_p if c < PC else incl_s, start=True, stop=True)
                        mm.then_inc(act_full, 1)
                    for c in range(CHUNKS):
                        b = bank_for_dve()
                        for j in range(4):
                            mm = pe.transpose(b[0:C, j * P:(j + 1) * P], CO1[:, (4 * gi + j) * T + c * C:(4 * gi + j) * T + (c + 1) * C], ident)
                        mm.then_inc(dve_full, 1)
                    from_act()
                    for c in range(PC):
                        from_dve()
                        b = bank_for_dve()
                        for j in range(4):
                            mm = pe.matmul(b[:, j * C:(j + 1) * C], ST[:, (4 * gi + j) * P:(4 * gi + j + 1) * P], Cf[:, c * C:(c + 1) * C], start=True, stop=True)
                        mm.then_inc(dve_full, 1)
                        b = bank_for_dve()
                        pe.matmul(b[:, :], BTOK[:, c * P:(c + 1) * P], XEND[:, c * BANK:(c + 1) * BANK], start=True, stop=True).then_inc(dve_full, 1)
                    pe.wait_ge(ssd_state_in[gi % 2], 16 * (gi // 2 + 1))
                    b = bank_for_dve()
                    for s_ in range(SEQS):
                        for j in range(4):
                            o = j * C + s_ * SEQ_LEN
                            mm = pe.matmul(b[:, o:o + SEQ_LEN], SSS[gi % 2][:, s_ * BANK + j * P:s_ * BANK + (j + 1) * P],
                                           Cf[:, PROMPT + s_ * SEQ_LEN:PROMPT + (s_ + 1) * SEQ_LEN], start=True, stop=True)
                    mm.then_inc(dve_full, 1)
                    from_dve()
                    for s_ in range(SEQS):
                        b = bank_for_dve()
                        pe.matmul(b[:, :], BM[:, s_ * P:(s_ + 1) * P], XEND[:, PC * BANK:CHUNKS * BANK], start=True, stop=True).then_inc(dve_full, 1)
                    from_dve()
                    for j in range(4):
                        b = bank_for_dve()
                        for c in range(CHUNKS):
                            for o in range(2):
                                hh = 2 * j + o
                                mm = pe.matmul(b[o * C:(o + 1) * C, c * C:(c + 1) * C], XDT[:, c * BANK + hh * C:c * BANK + (hh + 1) * C],
                                               EG1[:, (hh * CHUNKS + c) * C:(hh * CHUNKS + c + 1) * C], start=True, stop=True)
                        mm.then_inc(dve_full, 1)
                    from_act()
                    b = bank_for_act()
                    for j in range(4):
                        mm = pe.matmul(b[:, 0:T], ones, SQ1[:, j * T:(j + 1) * T], start=(j == 0), stop=(j == 3))
                    mm.then_inc(act_full, 1)

            def experts():
                token_scalars(router, E)
                from_dve()
                for e in range(E):
                    b = bank_for_act()
                    for c in range(CHUNKS):
                        mm = pe.matmul(b[:, c * C:(c + 1) * C],
                                       R[:, e * CHUNKS + c:e * CHUNKS + c + 1].to_broadcast([C, P]),
                                       ident64, start=True, stop=True)
                    mm.then_inc(act_full, 1)
                turns = E // EXPERTS_A_TURN
                with pe.Fori(0, turns) as i:
                    per = {act_full: 4 * EXPERTS_A_TURN, dve_full: 12 * EXPERTS_A_TURN, weights_used: 6 * EXPERTS_A_TURN,
                           act_ready: 4 * EXPERTS_A_TURN}
                    per |= {w: 16 * 6 * EXPERTS_A_TURN // SLOTS for w in weights_in}
                    with n.repeat(i, turns, per):
                        for j in range(EXPERTS_A_TURN):
                            gw, uw = ([next_slot().rearrange("p (k n) -> p k n", n=BANK) for _ in range(2)] for _ in range(2))
                            for mt in range(FT):
                                for ws, bank, full in ((gw, bank_for_act, act_full), (uw, bank_for_dve, dve_full)):
                                    b = bank()
                                    for kk in range(DK):
                                        mm = pe.matmul(b[:, 0:T], ws[kk // 4][:, kk % 4, mt * P:(mt + 1) * P], h[:, kk * T:(kk + 1) * T],
                                                       start=(kk == 0), stop=(kk == DK - 1))
                                        if mt == FT - 1 and kk == 3:
                                            mm.then_inc(weights_used, 1)
                                    mm.then_inc(full, 1)
                                    if mt == FT - 1:
                                        slot_read(full)
                            dw = [next_slot().rearrange("p (k n) -> p k n", n=D) for _ in range(2)]
                            n.up(act_ready, 4)
                            pe.wait_ge(act_ready, n.at(act_ready))
                            for dt_ in range(DK):
                                b = bank_for_dve()
                                for f in range(FT):
                                    mm = pe.matmul(b[:, 0:T], dw[f // 2][:, f % 2, dt_ * P:(dt_ + 1) * P], ACTV[j % 2][:, f * T:(f + 1) * T],
                                                   start=(f == 0), stop=(f == FT - 1))
                                    if dt_ == DK - 1 and f == 1:
                                        mm.then_inc(weights_used, 1)
                                mm.then_inc(dve_full, 1)
                            slot_read(dve_full)

            pe.wait_ge(consts_in, 48)
            pe.wait_ge(tails_in, 48)
            for layer in range(2):
                conditioning()
                norm_sum()
                from_dve()
                if layer == 0:
                    gdn()
                    hgrn()
                    from_dve()
                    projections(h, DK, 2, bank_for_dve, dve_full)
                else:
                    ssd()
                    from_dve()
                    projections(CO1, SX, 2, bank_for_dve, dve_full)
                norm_sum()
                from_dve()
                experts()
            norm_sum()

        @block.scalar
        def _(act):
            n = Count()

            def bank():
                i = n.n.get(id(act_full), 0)
                n.up(act_full)
                act.wait_ge(act_full, n.at(act_full))
                return psum[i % BANKS]

            def from_dve():
                act.wait_ge(to_act, n.up(to_act))

            def step(ins):
                ins.then_inc(act_step, 1)
                act.wait_ge(act_step, n.up(act_step))

            def tell(what):
                act.sem_inc(what, 1)

            def banks_read():
                act.wait_ge(act_free, n.at(act_full))

            def squares(dst, src):
                from_dve()
                act.activation(dst, src, ACT.Square).then_inc(pe_from_act, 1)

            def root(scale):
                b = bank()
                act.activation(rs[:, :], b[:, 0:T], ACT.Sqrt, scale=scale, bias=eps).then_inc(act_free, 1)
                act.wait_ge(act_free, n.at(act_full))
                tell(to_dve)

            def softplus(e1, l1, a_exp, a_log, beta=None):
                from_dve()
                if beta is not None:
                    act.activation(beta, beta, ACT.Exp, scale=-1.0)
                act.activation(a_exp, a_log, ACT.Exp)
                step(act.activation(e1, e1, ACT.Exp))
                act.activation(l1, e1, ACT.Ln, bias=one_col[0:C, :]).then_inc(to_dve, 1)

            def conv_inputs(UP, CV, CO, tiles, bias, order):
                done = 0

                def silus(upto):
                    nonlocal done
                    while done < upto:
                        act.wait_ge(conv_ready, n.up(conv_ready))
                        cv = CV[:, (done % 4) * 348:(done % 4) * 348 + 347]
                        bb = {} if bias is None else {"bias": bias[:, done:done + 1]}
                        act.activation(CO[:, done * T:done * T + PROMPT], cv[:, 0:PROMPT], ACT.Silu, **bb)
                        act.activation(CO[:, done * T + PROMPT:(done + 1) * T].rearrange("p (b l) -> p b l", l=SEQ_LEN),
                                       cv[:, PAD + PROMPT:].rearrange("p (b l) -> p b l", l=PAD + SEQ_LEN)[:, :, 0:SEQ_LEN],
                                       ACT.Silu, **bb).then_inc(conv_silu, 1)
                        done += 1

                for f in range(tiles):
                    b = bank()
                    up = UP[:, f * UPW:(f + 1) * UPW]
                    act.activation(up[:, PAD:PAD + PROMPT], b[:, 0:PROMPT], ACT.Copy)
                    act.activation(up[:, PAD + PROMPT:].rearrange("p (b l) -> p b l", l=PAD + SEQ_LEN)[:, :, PAD:],
                                   b[:, PROMPT:T].rearrange("p (b l) -> p b l", l=SEQ_LEN), ACT.Copy).then_inc(act_free, 1)
                    banks_read()
                    tell(conv_in_ready)
                    silus(f - 1)
                silus(tiles)

            def copies(dst, parts, width, banks, last):
                total = dst.shape[-1]
                for i in range(banks):
                    w = min(width, total - i * width)
                    b = bank()
                    act.activation(dst[:, i * width:i * width + w], b[0:parts, 0:w], ACT.Copy).then_inc(act_free, 1)
                act.wait_ge(act_free, n.at(act_full))
                if last:
                    tell(pe_from_act)

            def gdn():
                conv_inputs(UP0, CV0, CO0, AB_CONV, None, None)
                for i in range(4):
                    b = bank()
                    act.activation(zs[:, i * T:(i + 1) * T], b[:, 0:T], ACT.Silu).then_inc(act_free, 1)
                for i in range(4):
                    b = bank()
                    act.activation(hq[:, i * T:(i + 1) * T], b[:, 0:T], ACT.Copy, scale=float(P) ** -0.5).then_inc(act_free, 1)
                for i in range(4):
                    b = bank()
                    act.activation(hf[:, i * T:(i + 1) * T], b[:, 0:T], ACT.Sigmoid)
                    act.activation(hk[:, i * T:(i + 1) * T], b[:, 0:T], ACT.Sigmoid, scale=-1.0).then_inc(act_free, 1)
                for i in range(4):
                    b = bank()
                    act.activation(hv[:, i * T:(i + 1) * T], b[:, 0:T], ACT.Copy).then_inc(act_free, 1)
                for i in range(4):
                    b = bank()
                    act.activation(hg[:, i * T:(i + 1) * T], b[:, 0:T], ACT.Silu).then_inc(act_free, 1)
                softplus(sc[:, 60:80], sc[:, 80:100], sc[:, 100:104], W("gdn_a_log")[0:C, :], sc[:, 200:220])
                from_dve()
                act.activation(sc[:, 160:200], sc[:, 120:160], ACT.Exp).then_inc(to_dve, 1)
                from_dve()
                act.activation(EDEC, EDEC, ACT.Exp)
                act.activation(EGR, GR, ACT.Exp).then_inc(to_dve, 1)
                act.wait_ge(conv_silu, AB_CONV)
                act.wait_ge(weights_used, N_AB)
                act.activation(SQ, CO0[:, 0:2 * B], ACT.Square).then_inc(pe_from_act, 1)
                for i in range(2 * HEADS):
                    b = bank()
                    act.activation(SQ[:, i * T:(i + 1) * T], b[:, 0:T], ACT.Sqrt, bias=eps).then_inc(act_free, 1)
                act.wait_ge(act_free, n.at(act_full))
                tell(to_dve)
                for lv in range(len(LEVELS)):
                    copies(PROD, C, BANK, 3, True)
                copies(UT, P, BANK, 3, False)
                copies(WT, P, BANK, 3, True)
                tell(to_dve)
                for c in range(CHUNKS):
                    b = bank()
                    v = VTOK.rearrange("p (h c n) -> p h c n", h=HEADS, c=CHUNKS)[:, :, c, :]
                    act.activation(v, b[0:C, :].rearrange("p (h n) -> p h n", h=HEADS), ACT.Copy).then_inc(act_free, 1)
                    act.wait_ge(act_free, n.at(act_full))
                    tell(pe_from_act)
                squares(SQ[:, 0:B], OI)
                for i in range(HEADS):
                    b = bank()
                    act.activation(SQ[:, B + i * T:B + (i + 1) * T], b[:, 0:T], ACT.Sqrt, scale=1.0 / P, bias=eps).then_inc(act_free, 1)
                act.wait_ge(act_free, n.at(act_full))
                tell(to_dve)

            def hgrn():
                from_dve()
                act.activation(LB[:, 0:12], LB[:, 0:12], ACT.Exp).then_inc(to_dve, 1)
                from_dve()
                act.activation(LFC, hf, ACT.Ln).then_inc(to_dve, 1)
                for lv, half in enumerate(LEVELS):
                    from_dve()
                    act.activation(ED, ED, ACT.Exp).then_inc(to_dve, 1)
                from_dve()
                act.activation(KE, KE, ACT.Exp)
                act.activation(EC, CUM, ACT.Exp).then_inc(to_dve, 1)
                copies(KENDH, C, BANK, 5, False)
                copies(VTOKH, C, BANK, 5, True)
                tell(to_dve)
                squares(Z[0], OIH)
                for i in range(HEADS):
                    b = bank()
                    act.activation(Z[1][:, i * T:(i + 1) * T], b[:, 0:T], ACT.Sqrt, scale=1.0 / P, bias=eps).then_inc(act_free, 1)
                act.wait_ge(act_free, n.at(act_full))
                tell(to_dve)

            def ssd():
                conv_inputs(UP1, CV1, CO1, SXBC, W("ssd_conv_b"), None)
                for i in range(SX):
                    b = bank()
                    act.activation(zs1[:, i * T:(i + 1) * T], b[:, 0:T], ACT.Silu).then_inc(act_free, 1)
                n5 = SH * CHUNKS
                softplus(sc1[:, 2 * n5:3 * n5], sc1[:, 3 * n5:4 * n5], sc1[:, 8 * n5:8 * n5 + SH], W("ssd_a_log")[0:C, :])
                from_dve()
                act.activation(sc1[:, 5 * n5:6 * n5], sc1[:, 5 * n5:6 * n5], ACT.Exp).then_inc(to_dve, 1)
                from_dve()
                act.activation(DEC, DEC, ACT.Exp).then_inc(to_dve, 1)
                act.wait_ge(conv_silu, SXBC)
                tell(pe_from_act)
                for gi in range(SG):
                    for i in range(2):
                        w = BANK if i == 0 else P
                        b = bank()
                        act.activation(BTOK[:, i * BANK:i * BANK + w], b[0:C, 0:w], ACT.Copy).then_inc(act_free, 1)
                    for j in range(4):
                        b = bank()
                        act.activation(ER[:, j * T:(j + 1) * T], b[:, 0:T], ACT.Exp).then_inc(act_free, 1)
                    act.wait_ge(act_free, n.at(act_full))
                    tell(pe_from_act)
                    tell(to_dve)
                    from_dve()
                    act.activation(EG1, EG1, ACT.Exp).then_inc(to_dve, 1)
                    squares(SQ1, CO1[:, 4 * gi * T:4 * (gi + 1) * T])
                    root(1.0 / BANK)

            def experts():
                from_dve()
                act.activation(R[:, 100:180], R[:, 100:180], ACT.Sigmoid).then_inc(to_dve, 1)
                for e in range(E):
                    b = bank()
                    act.activation(COMB[:, e * T:(e + 1) * T], b[:, 0:T], ACT.Copy).then_inc(act_free, 1)
                act.wait_ge(act_free, n.at(act_full))
                tell(to_dve)
                turns = E // EXPERTS_A_TURN
                with act.Fori(0, turns) as i:
                    with n.repeat(i, turns, {s_: 4 * EXPERTS_A_TURN for s_ in (act_full, gate_free, gate_silu)}):
                        for j in range(EXPERTS_A_TURN * FT):
                            b = bank()
                            act.wait_ge(gate_free, n.up(gate_free))
                            act.activation(SIL[:, (j % 2) * T:(j % 2 + 1) * T], b[:, 0:T], ACT.Silu).then_inc(gate_silu, 1)
                            act.wait_ge(gate_silu, n.up(gate_silu))
                            tell(act_free)

            act.wait_ge(cond_in, 16)
            act.activation(cs[:, :], cs[:, :], ACT.Silu).then_inc(pe_from_act, 1)
            act.wait_ge(consts_in, 48)
            for layer in range(2):
                if layer:
                    tell(pe_from_act)
                squares(h[:, :], x[:, :])
                root(1.0 / D)
                if layer == 0:
                    gdn()
                    hgrn()
                else:
                    ssd()
                squares(h[:, :], x[:, :])
                root(1.0 / D)
                experts()
            squares(h[:, :], x[:, :])
            root(1.0 / D)

        @block.vector
        def _(dve):
            n = Count()

            def bank():
                i = n.n.get(id(dve_full), 0)
                n.up(dve_full)
                dve.wait_ge(dve_full, n.at(dve_full))
                return psum[BANKS + i % BANKS]

            def freed(ins):
                ins.then_inc(dve_free, 1)
                dve.wait_ge(dve_free, n.at(dve_full))

            def step(ins):
                ins.then_inc(dve_step, 1)
                dve.wait_ge(dve_step, n.up(dve_step))

            def tell(what):
                dve.sem_inc(what, 1)

            def done(ins, what):
                step(ins)
                tell(what)

            def from_act():
                dve.wait_ge(to_dve, n.up(to_dve))

            tt, ts, stt, cp = dve.tensor_tensor, dve.tensor_scalar, dve.scalar_tensor_tensor, dve.tensor_copy

            def v3(ap, k_):
                return ap.rearrange("p (k n) -> p k n", k=k_)

            modv = mod[:, :].rearrange("p (f m) -> p f m", m=MODS)

            def conditioning(layer):
                bias = W("b_ada")[:, 48 * layer:48 * (layer + 1)]
                for gq in range(12):
                    b = bank()
                    freed(tt(modv[:, 4 * gq:4 * gq + 4, :], v3(b[:, 0:4 * MODS], 4), spread(bias[:, 4 * gq:4 * gq + 4], 2, MODS), ALU.add))
                for first, name in ((8, "norm_mix"), (32, "norm_ffn")):
                    gain = W(name)[:, DK * layer:DK * (layer + 1)]
                    step(stt(modv[:, first:first + DK, :], modv[:, first:first + DK, :], 1.0, spread(gain, 2, MODS), ALU.add, ALU.mult))

            def normalise(first):
                from_act()
                step(dve.reciprocal(rs[:, :], rs[:, :]))
                step(tt(v3(h[:, :], DK), v3(x[:, :], DK), spread(rs[:, :], 1, DK), ALU.mult))
                if first is None:
                    for kk in range(DK):
                        last = ts(h[:, kk * T:(kk + 1) * T], h[:, kk * T:(kk + 1) * T], W("norm_final")[:, kk:kk + 1], None, ALU.mult)
                    done(last, out_ready)
                    return
                hs = v3(h[:, :], DK)[:, :, PROMPT:T].rearrange("p k (b l) -> p k b l", l=SEQ_LEN)
                for kk in range(DK):
                    ts(h[:, kk * T:kk * T + PROMPT], h[:, kk * T:kk * T + PROMPT], modv[:, first + DK + kk, 0:1], modv[:, first + kk, 0:1], ALU.mult, ALU.add)
                step(tt(hs, hs, spread(modv[:, first + DK:first + 2 * DK, 1:MODS], 3, SEQ_LEN), ALU.mult))
                tt(hs, hs, spread(modv[:, first:first + DK, 1:MODS], 3, SEQ_LEN), ALU.add).then_inc(pe_from_dve, 1)

            def residual(src, kk, gate, is_bank):
                m0 = modv[:, gate + kk, 0:1]
                ms = spread(modv[:, gate + kk, 1:MODS], 2, SEQ_LEN)
                xk = x[:, kk * T:(kk + 1) * T]
                stt(xk[:, 0:PROMPT], src[:, 0:PROMPT], m0, xk[:, 0:PROMPT], ALU.mult, ALU.add)
                ins = tt(v3(rs[:, PROMPT:T], SEQS), v3(src[:, PROMPT:T], SEQS), ms, ALU.mult)
                freed(ins) if is_bank else step(ins)
                return tt(xk[:, PROMPT:T], xk[:, PROMPT:T], rs[:, PROMPT:T], ALU.add)

            def conv_states(UP, tiles, layer):
                dve.wait_ge(conv_state_in, 16 * (layer + 1))
                upv = v3(UP, tiles)
                dve.memset(upv[:, :, 0:PAD], 0.0)
                hist = upv[:, :, PAD + PROMPT:].rearrange("p k (b l) -> p k b l", l=PAD + SEQ_LEN)[:, :, :, 0:PAD]
                step(cp(hist, convst[:, 0:tiles * SEQS * PAD].rearrange("p (k b l) -> p k b l", k=tiles, b=SEQS)))

            def convolution(UP, CV, tiles, w):
                for f in range(tiles):
                    dve.wait_ge(conv_in_ready, n.up(conv_in_ready))
                    up = UP[:, f * UPW:(f + 1) * UPW]
                    cv = CV[:, (f % 4) * 348:(f % 4) * 348 + CVW]
                    if f >= 4:
                        dve.wait_ge(conv_silu, n.up(conv_silu))
                    step(ts(cv, up[:, 0:CVW], w[:, f * TAPS:f * TAPS + 1], None, ALU.mult))
                    for j in range(1, TAPS):
                        ins = stt(cv, up[:, j:j + CVW], w[:, f * TAPS + j:f * TAPS + j + 1], cv, ALU.mult, ALU.add)
                        if j < TAPS - 1:
                            step(ins)
                        else:
                            ins.then_inc(conv_ready, 1)
                n.up(conv_silu, 4)
                dve.wait_ge(conv_silu, n.at(conv_silu))
                upv = v3(UP, tiles)
                new = convnew[:, 0:tiles * MODS * PAD].rearrange("p (k m l) -> p k m l", k=tiles, m=MODS)
                cp(new[:, :, 0, :], upv[:, :, PROMPT:PROMPT + PAD])
                hist = upv[:, :, PAD + PROMPT:].rearrange("p k (b l) -> p k b l", l=PAD + SEQ_LEN)[:, :, :, SEQ_LEN:]
                done(cp(new[:, :, 1:, :], hist), out_ready)

            def log_decay(pre, t, e1, l1, nh, a_exp, bias, gl, dt_out):
                def hc(ap):
                    return ap.rearrange("p (h c) -> p h c", c=CHUNKS)
                step(tt(hc(t), pre, spread(bias, 2, CHUNKS), ALU.add))
                step(ts(e1, t, -1.0, None, ALU.mult))
                tt(e1, e1, t, ALU.min).then_inc(to_act, 1)
                from_act()
                step(stt(dt_out, t, 0.0, l1, ALU.max, ALU.add))
                step(ts(e1, dt_out, -1.0, None, ALU.mult))
                tt(hc(gl), hc(e1), spread(a_exp, 2, CHUNKS), ALU.mult).then_inc(pe_from_dve, 1)

            def decay_sums(gam, rem, nh):
                b = bank()
                np_ = nh * PC
                o = nh * CHUNKS
                for dst, at in ((gam, 0), (rem, o)):
                    d = dst.rearrange("p (h c) -> p h c", c=CHUNKS)
                    cp(d[:, :, 0:PC], b[0:C, at:at + np_].rearrange("p (h c) -> p h c", c=PC))
                    last = cp(d[:, :, PC], b[0:C, at + np_:at + o])
                freed(last)

            def each_bank(total, width):
                for i0 in range(0, total, width):
                    yield i0, min(width, total - i0), bank()

            def state_update(Sx, dec, b):
                for hh in range(HEADS):
                    last = stt(Sx[:, hh * P:(hh + 1) * P], Sx[:, hh * P:(hh + 1) * P], dec(hh), b[:, hh * P:(hh + 1) * P], ALU.mult, ALU.add)
                freed(last)

            def head_outputs(o, root_, gain, gate, dst):
                from_act()
                step(dve.reciprocal(root_, root_))
                step(tt(o, o, root_, ALU.mult))
                step(stt(dst, o, gain, gate, ALU.mult, ALU.mult))

            def gdn():
                gl, t, e1, l1 = sc[:, 0:20], sc[:, 20:40], sc[:, 60:80], sc[:, 80:100]
                a_exp, gam, rem = sc[:, 100:104], sc[:, 120:140], sc[:, 140:160]
                egam, erem, beta, ba = sc[:, 160:180], sc[:, 180:200], sc[:, 200:220], sc[:, 240:280]
                bg = sc[:, 220:240]
                QT, KT = CO0[:, 0:B], CO0[:, B:2 * B]
                conv_states(UP0, AB_CONV, 0)
                b = bank()
                freed(cp(rs[0:C, 0:CHUNKS * AB_TAIL], b[0:C, 0:CHUNKS * AB_TAIL]))
                convolution(UP0, CV0, AB_CONV, W("ab_conv_w"))
                dve.wait_ge(weights_used, N_AB)
                step(cp(ba, rs[0:C, 0:CHUNKS * AB_TAIL]))
                bav = ba.rearrange("p (c w) -> p w c", w=AB_TAIL)
                step(cp(beta.rearrange("p (h c) -> p h c", c=CHUNKS), bav[:, 0:HEADS, :]))
                log_decay(bav[:, HEADS:2 * HEADS, :], t, e1, l1, HEADS, a_exp, W("gdn_dt_bias")[0:C, :], gl, sc[:, 40:60])
                decay_sums(gam, rem, HEADS)
                tell(to_act)
                step(ts(beta, beta, 1.0, None, ALU.add))
                step(dve.reciprocal(beta, beta))
                from_act()
                step(tt(bg, beta, egam, ALU.mult))
                glv, bev = (q_.rearrange("p (h c) -> p h c", c=CHUNKS) for q_ in (gl, beta))
                inclv = incl.rearrange("p (c n) -> p c n", n=C)
                v4 = lambda ap: ap.rearrange("p (h c n) -> p h c n", h=HEADS, c=CHUNKS)
                tt(v4(EDEC), spread(inclv, 1, HEADS), spread(glv, 3, C), ALU.mult)
                tt(v4(U), spread(spread(ident64, 1, CHUNKS), 1, HEADS), spread(bev, 3, C), ALU.mult).then_inc(pe_from_dve, 1)
                for i0, w, b in each_bank(B, BANK):
                    freed(cp(GR[:, i0:i0 + w], b[:, 0:w]))
                for i0, w, b in each_bank(B, BANK):
                    freed(cp(BR[:, i0:i0 + w], b[0:C, 0:w]))
                step(tt(v3(EDEC, BLOCKS), v3(GR[0:C, :], BLOCKS), spread(gam, 2, C), ALU.subtract))
                ts(EDEC, EDEC, 0.0, None, ALU.min).then_inc(to_act, 1)
                from_act()
                step(tt(v4(EDEC), v4(EDEC), spread(inclv, 1, HEADS), ALU.mult))
                from_act()
                step(dve.reciprocal(SQ, SQ))
                stt(QT, QT, float(P) ** -0.5, SQ[:, 0:B], ALU.mult, ALU.mult)
                tt(KT, KT, SQ[:, B:2 * B], ALU.mult).then_inc(pe_from_dve, 1)
                for i0, w, b in each_bank(B, BANK):
                    freed(tt(U[:, i0:i0 + w], b[0:C, 0:w], EDEC[:, i0:i0 + w], ALU.mult))
                step(tt(U, U, BR, ALU.mult))
                for i0, w, b in each_bank(B, BANK):
                    freed(tt(QKE[:, i0:i0 + w], b[0:C, 0:w], EDEC[:, i0:i0 + w], ALU.mult))
                for i0, w, b in each_bank(BLOCKS * P, BANK):
                    q0 = i0 // P
                    tt(v3(BK[:, i0:i0 + w], 4), v3(b[0:C, :], 4), spread(bg[:, q0:q0 + 4], 2, P), ALU.mult)
                    freed(tt(v3(KEND[:, i0:i0 + w], 4), v3(b[0:C, :], 4), spread(erem[:, q0:q0 + 4], 2, P), ALU.mult))
                for i0, w, b in each_bank(BLOCKS * P, BANK):
                    q0 = i0 // P
                    freed(tt(v3(BV[:, i0:i0 + w], 4), v3(b[0:C, :], 4), spread(beta[:, q0:q0 + 4], 2, P), ALU.mult))
                cp(v3(M, BLOCKS), spread(ident64, 1, BLOCKS))
                step(cp(v3(MT, BLOCKS), spread(ident64, 1, BLOCKS)))
                dve.wait_ge(levels_in, 16)
                for lv in range(len(LEVELS)):
                    mk = levels.rearrange("p (l n) -> p l n", l=len(LEVELS))[:, len(LEVELS) - 1 - lv, :].rearrange("p (c n) -> p c n", n=C)
                    ct, mt = (CT, MT) if lv % 2 == 0 else (MT, CT)
                    tt(v4(ct), v4(U), spread(mk, 1, HEADS), ALU.mult).then_inc(pe_from_dve, 1)
                    for i0, w, b in each_bank(B, BANK):
                        freed(stt(ct[:, i0:i0 + w], b[0:C, 0:w], -1.0, mt[:, i0:i0 + w], ALU.mult, ALU.add))
                    if lv < len(LEVELS) - 1:
                        for i0, w, b in each_bank(B, BANK):
                            freed(stt(M[:, i0:i0 + w], b[0:C, 0:w], -1.0, M[:, i0:i0 + w], ALU.mult, ALU.add))
                tell(pe_from_dve)
                dve.memset(S, 0.0)
                done(tt(GR, QT, EGR, ALU.mult), pe_from_dve)
                from_act()
                hv4 = lambda ap: ap.rearrange("p (h c n) -> p h c n", h=HEADS, c=CHUNKS)
                egr = EGR.rearrange("p (h t) -> p h t", h=HEADS)
                for c in range(CHUNKS):
                    b = bank()
                    cp(hv4(OI)[:, :, c, :], v3(b[:, 0:HEADS * C], HEADS))
                    freed(tt(v3(VN, HEADS), hv4(UT)[:, :, c, :], v3(b[:, HEADS * C:2 * HEADS * C], HEADS), ALU.subtract))
                    tell(pe_from_dve)
                    if c < PC:
                        b = bank()
                        state_update(S, lambda hh: egr[:, hh, c * C + C - 1:c * C + C], b)
                        if c < PC - 1:
                            tell(pe_from_dve)
                        else:
                            tell(out_ready)
                kv = KEND.rearrange("p (h c n) -> p h c n", h=HEADS, c=CHUNKS)[:, :, PC, :]
                for hh in range(HEADS):
                    last = tt(KENDM.rearrange("p (b h n) -> p b h n", b=SEQS, h=HEADS)[:, :, hh, :], spread(kv[:, hh, :], 1, SEQS), spread(seq, 2, P), ALU.mult)
                done(last, pe_from_dve)
                for s_ in range(SEQS):
                    b = bank()
                    at = PROMPT + s_ * SEQ_LEN + SEQ_LEN - 1
                    state_update(SS[:, s_ * HEADS * P:(s_ + 1) * HEADS * P], lambda hh: egr[:, hh, at:at + 1], b)
                tell(out_ready)
                for i0, w, b in each_bank(B, BANK):
                    freed(tt(OI[:, i0:i0 + w], b[:, 0:w], OI[:, i0:i0 + w], ALU.add))
                tell(to_act)
                head_outputs(OI, SQ[:, B:2 * B], W("gdn_norm"), zs, h[:, 0:B])
                tell(out_ready)

            def hgrn():
                lb = LB.rearrange("p (k n) -> p k n", n=4)
                lg = W("lb_logits")
                dve.wait_ge(stored, 48)
                step(tt(LB[:, 12:16], lg[:, 0:4], lg[:, 4:8], ALU.max))
                step(tt(LB[:, 12:16], LB[:, 12:16], lg[:, 8:12], ALU.max))
                tt(v3(LB[:, 0:12], 3), v3(lg, 3), spread(LB[:, 12:16], 1, 3), ALU.subtract).then_inc(to_act, 1)
                from_act()
                step(tt(LB[:, 16:20], LB[:, 4:8], LB[:, 8:12], ALU.add))
                step(tt(LB[:, 20:24], LB[:, 16:20], LB[:, 0:4], ALU.add))
                step(dve.reciprocal(LB[:, 24:28], LB[:, 20:24]))
                tt(LB[:, 28:32], LB[:, 0:4], LB[:, 24:28], ALU.mult)
                step(tt(LB[:, 32:36], LB[:, 16:20], LB[:, 24:28], ALU.mult))
                for hh in range(HEADS):
                    cols = slice(hh * T, (hh + 1) * T)
                    ts(hf[:, cols], hf[:, cols], LB[:, 32 + hh:33 + hh], LB[:, 28 + hh:29 + hh], ALU.mult, ALU.add)
                    last = ts(hk[:, cols], hk[:, cols], LB[:, 32 + hh:33 + hh], None, ALU.mult)
                done(last, pe_from_dve)
                step(ts(hf, hf, 1e-19, None, ALU.max))
                tell(to_act)
                from_act()
                for hh in range(HEADS):
                    cols = slice(hh * T, (hh + 1) * T)
                    last = dve.tensor_tensor_scan(CUM[:, cols], restart, LFC[:, cols], 0.0, ALU.mult, ALU.add)
                step(last)
                for i0, w, b in each_bank(B, BANK):
                    freed(tt(v3(ATT[0:C, i0:i0 + w], w // C), v3(b[0:C, 0:w], w // C), spread(ident64, 1, w // C), ALU.mult))
                for lv, half in enumerate(LEVELS):
                    nb = T // (2 * half) if half < SEQ_LEN else PROMPT // (2 * half)
                    used = nb * 2 * half
                    zz = Z[lv % 2]

                    def halves(buf, hh):
                        return buf[:, hh * T:hh * T + used].rearrange("p (n two w) -> p n two w", two=2, w=half)
                    for hh in range(HEADS):
                        cu, ed = halves(CUM, hh), halves(ED, hh)
                        mid = spread(cu[:, :, 0, half - 1], 2, half)
                        tt(ed[:, :, 0, :], mid, cu[:, :, 0, :], ALU.subtract)
                        last = tt(ed[:, :, 1, :], cu[:, :, 1, :], mid, ALU.subtract)
                        if used < T:
                            last = dve.memset(ED[:, hh * T + used:(hh + 1) * T], 0.0)
                    done(last, to_act)
                    from_act()
                    for hh in range(HEADS):
                        ed, zv = halves(ED, hh), halves(zz, hh)
                        tt(zv[:, :, 0, :], ed[:, :, 0, :], halves(hk, hh)[:, :, 0, :], ALU.mult)
                        last = tt(zv[:, :, 1, :], ed[:, :, 1, :], halves(hq, hh)[:, :, 1, :], ALU.mult)
                    done(last, pe_from_dve)
                    mk = levels.rearrange("p (l n) -> p l n", l=len(LEVELS))[:, lv, :]
                    for i0, w, b in each_bank(B, BANK):
                        i, end = i0 // C, (i0 + w) // C
                        runs = []
                        while i < end:
                            hh, c = divmod(i, CHUNKS)
                            stop = min(end - i, (CHUNKS if half < SEQ_LEN else PC) - c)
                            if stop > 0:
                                runs.append((i, c, stop))
                            i += max(1, min(end - i, CHUNKS - c))
                        for i, c, m_ in runs:
                            last = dve.copy_predicated(ATT[0:C, i * C:(i + m_) * C], mk[:, c * C:(c + m_) * C].bitcast(U32),
                                                       b[0:C, i * C - i0:(i + m_) * C - i0])
                        freed(last)
                cum4 = CUM.rearrange("p (h t) -> p h t", h=HEADS)
                ke4 = KE.rearrange("p (h t) -> p h t", h=HEADS)
                for hh in range(HEADS):
                    for lo_, hi_, w in ((0, PROMPT, C), (PROMPT, T, SEQ_LEN)):
                        cu = cum4[:, hh, lo_:hi_].rearrange("p (n w) -> p n w", w=w)
                        ke = ke4[:, hh, lo_:hi_].rearrange("p (n w) -> p n w", w=w)
                        last = tt(ke, spread(cu[:, :, w - 1], 2, w), cu, ALU.subtract)
                done(last, to_act)
                from_act()
                step(tt(KE, KE, hk, ALU.mult))
                tell(pe_from_dve)
                dve.memset(SHG, 0.0)
                step(tt(ED, hq, EC, ALU.mult))
                tell(pe_from_dve)
                from_act()
                ov = OIH.rearrange("p (h c n) -> p h c n", h=HEADS, c=CHUNKS)
                ec = EC.rearrange("p (h t) -> p h t", h=HEADS)
                for c in range(PC):
                    b = bank()
                    freed(cp(ov[:, :, c, :], v3(b[:, 0:HEADS * C], HEADS)))
                    b = bank()
                    state_update(SHG, lambda hh: ec[:, hh, c * C + C - 1:c * C + C], b)
                    tell(pe_from_dve if c < PC - 1 else out_ready)
                b = bank()
                freed(cp(ov[:, :, PC, :], v3(b[:, 0:HEADS * C], HEADS)))
                kv = KENDH.rearrange("p (h c n) -> p h c n", h=HEADS, c=CHUNKS)[:, :, PC, :]
                for hh in range(HEADS):
                    last = tt(KENDMH.rearrange("p (b h n) -> p b h n", b=SEQS, h=HEADS)[:, :, hh, :], spread(kv[:, hh, :], 1, SEQS), spread(seq, 2, P), ALU.mult)
                done(last, pe_from_dve)
                for s_ in range(SEQS):
                    b = bank()
                    at = PROMPT + s_ * SEQ_LEN + SEQ_LEN - 1
                    state_update(SSH[:, s_ * HEADS * P:(s_ + 1) * HEADS * P], lambda hh: ec[:, hh, at:at + 1], b)
                tell(out_ready)
                for i0, w, b in each_bank(B, BANK):
                    freed(tt(OIH[:, i0:i0 + w], b[:, 0:w], OIH[:, i0:i0 + w], ALU.add))
                tell(to_act)
                head_outputs(OIH, Z[1], W("hgrn_norm"), hg, h[:, B:2 * B])
                tell(pe_from_dve)
                dve.wait_ge(stored, 80)
                tell(mixer_done)

            def ssd():
                n5 = SH * CHUNKS
                gl, t, e1, l1, gam, rem = (sc1[:, i * n5:(i + 1) * n5] for i in range(6))
                dt, xr = sc1[:, 6 * n5:7 * n5], sc1[:, 7 * n5:8 * n5]
                a_exp = sc1[:, 8 * n5:8 * n5 + SH]
                conv_states(UP1, SXBC, 1)
                b = bank()
                freed(cp(rs[0:C, 0:n5], b[0:C, 0:n5]))
                convolution(UP1, CV1, SXBC, W("ssd_conv_w"))
                dve.wait_ge(weights_used, N_SSD)
                log_decay(rs[0:C, 0:n5].rearrange("p (c h) -> p h c", c=CHUNKS), t, e1, l1, SH, a_exp, W("ssd_dt_bias")[0:C, :], gl, dt)
                decay_sums(gam, rem, SH)
                tell(to_act)
                glv = gl.rearrange("p (h c) -> p c h", c=CHUNKS)
                tt(GS.rearrange("p (b h) -> p b h", b=SEQS), spread(glv[:, PC, :], 1, SEQS), spread(seq, 2, SH), ALU.mult).then_inc(pe_from_dve, 1)
                from_act()
                b = bank()
                freed(cp(DEC, b[:, 0:(PC + SEQS) * SH]))
                tell(to_act)
                from_act()
                dve.memset(ST, 0.0)
                decv = DEC.rearrange("p (c h) -> p c h", h=SH)
                inclv = incl.rearrange("p (c n) -> p c n", n=C)
                for gi in range(SG):
                    hs = slice(gi * SHPG * CHUNKS, (gi + 1) * SHPG * CHUNKS)

                    def g8(ap):
                        return ap[:, hs].rearrange("p (h c) -> p h c", c=CHUNKS)
                    b = bank()
                    freed(tt(CBM, b[0:C, 0:T], incl, ALU.mult))
                    v4 = lambda ap: ap.rearrange("p (h c n) -> p h c n", h=SHPG, c=CHUNKS)
                    tt(v4(GM1), spread(inclv, 1, SHPG), spread(g8(gl), 3, C), ALU.mult)
                    cp(GBC.rearrange("p (c h n) -> p c h n", c=CHUNKS, h=SHPG), spread(g8(gl).rearrange("p h c -> p c h"), 3, C)).then_inc(pe_from_dve, 1)
                    for i0, w, b in each_bank(SHPG * T, BANK):
                        q0 = gi * SHPG * CHUNKS + i0 // C
                        freed(tt(v3(EG1[:, i0:i0 + w], 8), v3(b[0:C, :], 8), spread(gam[:, q0:q0 + 8], 2, C), ALU.subtract))
                    step(ts(EG1, EG1, 0.0, None, ALU.min))
                    xdt = XDT.rearrange("p (c h n) -> p c h n", c=CHUNKS, h=SHPG)
                    xend = XEND.rearrange("p (c h n) -> p c h n", c=CHUNKS, h=SHPG)
                    for c in range(CHUNKS):
                        b = bank()
                        freed(tt(xdt[:, c], v3(b[0:C, :], SHPG), spread(g8(dt)[:, :, c], 2, C), ALU.mult))
                    for c in range(CHUNKS):
                        last = tt(xend[:, c], xdt[:, c], spread(g8(rem)[:, :, c], 2, C), ALU.mult)
                    step(last)
                    tell(pe_from_dve)
                    from_act()
                    tell(to_act)
                    yi = YI.rearrange("p (j c n) -> p j c n", j=4, c=CHUNKS)
                    er = ER.rearrange("p (j c n) -> p j c n", j=4, c=CHUNKS)
                    stg = ST[:, gi * BANK:(gi + 1) * BANK]
                    for c in range(PC):
                        b = bank()
                        freed(tt(yi[:, :, c, :], v3(b[:, 0:4 * C], 4), er[:, :, c, :], ALU.mult))
                        b = bank()
                        step(tt(v3(stg, SHPG), v3(stg, SHPG), spread(decv[:, c, gi * SHPG:(gi + 1) * SHPG], 2, C), ALU.mult))
                        freed(tt(stg, b[:, :], stg, ALU.add))
                        if c < PC - 1:
                            tell(pe_from_dve)
                    b = bank()
                    freed(tt(yi[:, :, PC, :], v3(b[:, 0:4 * C], 4), er[:, :, PC, :], ALU.mult))
                    tt(v3(BM, SEQS), spread(BTOK[:, PC * P:CHUNKS * P], 1, SEQS), spread(seq, 2, P), ALU.mult).then_inc(pe_from_dve, 1)
                    for s_ in range(SEQS):
                        b = bank()
                        st = SSS[gi % 2][:, s_ * BANK:(s_ + 1) * BANK]
                        step(tt(v3(st, SHPG), v3(st, SHPG), spread(decv[:, PC + s_, gi * SHPG:(gi + 1) * SHPG], 2, C), ALU.mult))
                        freed(tt(st, b[:, :], st, ALU.add))
                    tell(out_ready)
                    from_act()
                    step(tt(v4(EG1), v4(EG1), spread(CBM.rearrange("p (c n) -> p c n", n=C), 1, SHPG), ALU.mult))
                    tell(pe_from_dve)
                    for j in range(4):
                        q = 4 * gi + j
                        xt, yt = CO1[:, q * T:(q + 1) * T], YI[:, j * T:(j + 1) * T]
                        step(stt(yt, xt, W("ssd_d")[:, q:q + 1], yt, ALU.mult, ALU.add))
                        b = bank()
                        freed(tt(yt, b[:, 0:T], yt, ALU.add))
                        step(tt(xt, yt, zs1[:, q * T:(q + 1) * T], ALU.mult))
                    tell(to_act)
                    from_act()
                    step(dve.reciprocal(rs[:, :], rs[:, :]))
                    for j in range(4):
                        q = 4 * gi + j
                        xt = CO1[:, q * T:(q + 1) * T]
                        step(stt(xt, xt, W("ssd_norm")[:, q:q + 1], rs[:, :], ALU.mult, ALU.mult))
                tell(pe_from_dve)
                tell(out_ready)
                dve.wait_ge(stored, 112)
                for i in range(2):
                    dve.wait_ge(stored_state[i], 16 * SG // 2)
                tell(mixer_done)

            def route():
                sg, bi = R[:, 100:180], R[:, 180:260]
                b = bank()
                freed(cp(sg, b[0:C, 0:CHUNKS * E]))
                tell(to_act)
                from_act()
                step(tt(v3(bi, CHUNKS), v3(sg, CHUNKS), spread(W("router_b")[0:C, :], 1, CHUNKS), ALU.add))
                v = bi.rearrange("p (g e) -> p g e", e=EPG)
                NG = CHUNKS * EG
                t = [R[:, 300 + 20 * i:320 + 20 * i] for i in range(20)]
                hi1, lo1, hi2, lo2, mid, m1, m2, gs, gsel = t[:9]
                tt(hi1, v[:, :, 0], v[:, :, 1], ALU.max)
                tt(lo1, v[:, :, 0], v[:, :, 1], ALU.min)
                tt(hi2, v[:, :, 2], v[:, :, 3], ALU.max)
                step(tt(lo2, v[:, :, 2], v[:, :, 3], ALU.min))
                tt(m1, hi1, hi2, ALU.max)
                tt(mid, hi1, hi2, ALU.min)
                step(tt(m2, lo1, lo2, ALU.max))
                step(tt(m2, m2, mid, ALU.max))
                step(tt(gs, m1, m2, ALU.add))
                gmax, nf = R[:, 800:805], R[:, 810:815]
                gv, sv = (q.rearrange("p (c g) -> p c g", g=EG) for q in (gs, gsel))
                dve.memset(nf, 1.0)
                step(dve.tensor_reduce(gmax, gv, AX.X, ALU.max))
                for g_ in range(EG):
                    step(tt(sv[:, :, g_], gv[:, :, g_], gmax, ALU.is_equal))
                    step(tt(sv[:, :, g_], sv[:, :, g_], nf, ALU.mult))
                    step(tt(nf, nf, sv[:, :, g_], ALU.subtract))
                cmpv = R[:, 900:900 + NG * EPG * 3].rearrange("p (g e j) -> p g e j", g=NG, e=EPG)
                for e in range(EPG):
                    for q, j in enumerate([j for j in range(EPG) if j != e]):
                        last = tt(cmpv[:, :, e, q], v[:, :, j], v[:, :, e], ALU.is_ge if j < e else ALU.is_gt)
                step(last)
                cnt = R[:, 1200:1200 + NG * EPG]
                step(dve.tensor_reduce(cnt, R[:, 900:900 + NG * EPG * 3].rearrange("p (g j) -> p g j", j=3), AX.X, ALU.add))
                step(ts(cnt, cnt, 1.5, None, ALU.is_lt))
                cg = cnt.rearrange("p (g e) -> p g e", e=EPG)
                step(tt(cg, cg, spread(gsel, 2, EPG), ALU.mult))
                step(tt(cnt, cnt, sg, ALU.mult))
                tot = R[:, 820:825]
                step(dve.tensor_reduce(tot, v3(cnt, CHUNKS), AX.X, ALU.add))
                step(dve.reciprocal(tot, tot))
                tt(R[:, 0:80].rearrange("p (e c) -> p e c", c=CHUNKS), cnt.rearrange("p (c e) -> p e c", e=E), spread(tot, 1, E), ALU.mult).then_inc(pe_from_dve, 1)

            def experts(layer):
                route()
                from_act()
                step(dve.memset(YACC, 0.0))
                turns = E // EXPERTS_A_TURN
                with dve.Fori(0, turns) as i:
                    per = {dve_full: 12 * EXPERTS_A_TURN, gate_silu: 4 * EXPERTS_A_TURN}
                    with n.repeat(i, turns, per):
                        for j in range(EXPERTS_A_TURN):
                            for f in range(FT):
                                dst = ACTV[j % 2][:, f * T:(f + 1) * T]
                                b = bank()
                                dve.wait_ge(gate_silu, n.up(gate_silu))
                                ins = tt(dst, b[:, 0:T], SIL[:, (f % 2) * T:(f % 2 + 1) * T], ALU.mult)
                                freed(ins)
                                tell(gate_free)
                                comb = COMB[:, bass.ds(i * (EXPERTS_A_TURN * T) + j * T, T)]
                                tt(dst, dst, comb, ALU.mult).then_inc(act_ready, 1)
                            for dt_ in range(DK):
                                b = bank()
                                ya = YACC[:, dt_ * T:(dt_ + 1) * T]
                                tt(ya, b[:, 0:T], ya, ALU.add).then_inc(dve_free, 1)
                dve.wait_ge(dve_free, n.at(dve_full))
                for kk in range(DK):
                    step(residual(YACC[:, kk * T:(kk + 1) * T], kk, 40, False))

            dve.wait_ge(consts_in, 48)
            dve.sem_inc(gate_free, 2)
            for layer in range(2):
                tell(to_act)
                conditioning(layer)
                normalise(0)
                if layer == 0:
                    gdn()
                    hgrn()
                else:
                    ssd()
                for kk in range(DK):
                    b = bank()
                    step(residual(b, kk, 16, True))
                tell(to_act)
                normalise(24)
                experts(layer)
            tell(to_act)
            normalise(None)


_WEIGHTS = ("w_ada", "ab_w_in", "ab_w_out", "ssd_w_in", "ssd_w_out", "moe_w_gate", "moe_w_up", "moe_w_down")


def _constants():
    def put(a, name, v):
        at, cols = CONST[name]
        a[:v.shape[0], at:at + cols] = v.reshape(v.shape[0], cols)

    a = np.zeros((P, CONST_COLS), np.float32)
    s, t = np.arange(C)[:, None], np.arange(C)[None, :]
    same = s // SEQ_LEN == t // SEQ_LEN
    put(a, "ones", np.ones((P, P), np.float32))
    put(a, "ident", np.eye(P, dtype=np.float32))
    put(a, "incl", np.stack([s <= t] * PC + [(s <= t) & same], 1).astype(np.float32))
    put(a, "after", np.stack([s > t, (s > t) & same], 1).astype(np.float32))
    put(a, "seq", (s // SEQ_LEN == np.arange(SEQS)[None, :]).astype(np.float32))
    tok = np.arange(T)
    first = np.where(tok < PROMPT, tok % C == 0, (tok - PROMPT) % SEQ_LEN == 0)
    put(a, "restart", np.broadcast_to(1.0 - first.astype(np.float32), (P, T)))
    put(a, "eps", np.full((P, 1), EPS, np.float32))
    levels = []
    for half in LEVELS:
        m = (s // (2 * half) == t // (2 * half)) & (s // half % 2 == 0) & (t // half % 2 == 1)
        levels.append(np.stack([m] * PC + [m & (half < SEQ_LEN)], 1))
    return a, np.stack(levels, 1).astype(np.float32).reshape(C, -1)


def _small(v):
    a = np.zeros((P, SMALL_COLS), np.float32)

    def put(name, x):
        at, cols = SMALL[name]
        a[:, at:at + cols] = x

    def features(x):
        x = np.asarray(x)
        return x.reshape(-1, P).T

    def taps(w):
        return np.asarray(w).reshape(TAPS, -1, P).transpose(2, 1, 0).reshape(P, -1)

    for name in ("norm_mix", "norm_ffn", "norm_final", "b_ada", "gdn_norm", "hgrn_norm", "ssd_conv_b", "ssd_norm"):
        put(name, features(v[name]))
    put("lb_logits", features(v["hgrn_lb_logits"]))
    put("ab_conv_w", taps(v["ab_conv_w"]))
    put("ssd_conv_w", taps(v["ssd_conv_w"]))
    put("ssd_d", features(np.repeat(np.asarray(v["ssd_d"]).reshape(-1), C)))
    for name in ("gdn_a_log", "gdn_dt_bias", "ssd_a_log", "ssd_dt_bias", "router_b"):
        put(name, np.broadcast_to(np.asarray(v[name]).reshape(1, -1), (P, SMALL[name][1])))
    return a


def kernel(**v):
    import concourse.bacc as bacc
    from concourse.bass_utils import run_bass_kernel_spmd

    v = {name: np.asarray(x) for name, x in v.items()}

    def conv_t(st):
        return st[0].reshape(SEQS, PAD, -1, P).transpose(3, 2, 0, 1).reshape(P, -1)

    consts, levels = _constants()
    arrays = {
        "consts": consts, "levels": levels, "small": _small(v),
        "x_t": np.concatenate([v["x_prompt"].reshape(-1, D), v["x_sample"].reshape(-1, D)]).T,
        "c_t": np.concatenate([v["c_prompt"], v["c_sample"]]).T,
        "router_w": v["router_w"],
        "gdn_conv_t": conv_t(v["state_gdn_conv"]), "ssd_conv_t": conv_t(v["state_ssd_conv"]),
        "gdn_state": v["state_gdn"][0].transpose(2, 0, 1, 3).reshape(P, -1),
        "hgrn_state": v["state_hgrn"][0].transpose(2, 0, 1, 3).reshape(P, -1),
        "ssd_state": v["state_ssd"][0].transpose(3, 0, 1, 2).reshape(P, SEQS, -1),
    }
    arrays |= {name: v[name] for name in _WEIGHTS}
    arrays = {name: np.ascontiguousarray(x) for name, x in arrays.items()}
    shapes = {"y": (D, T), "gdn_p": (P, HEADS * P), "gdn_s": (P, SEQS * HEADS * P), "gdn_conv": (P, AB_CONV * MODS * PAD),
              "hgrn_p": (P, HEADS * P), "hgrn_s": (P, SEQS * HEADS * P), "ssd_p": (P, SH * C), "ssd_s": (P, SEQS, SH * C),
              "ssd_conv": (P, SXBC * MODS * PAD)}
    nc = bacc.Bacc("TRN2", target_bir_lowering=False, num_devices=1)
    a = {name: nc.dram_tensor(name + "_in", x.shape, F32, kind="ExternalInput").ap() for name, x in arrays.items()}
    out = {name: nc.dram_tensor(name + "_out", shape, F32, kind="ExternalOutput").ap() for name, shape in shapes.items()}
    trunk_program(nc, a, out)
    r = run_bass_kernel_spmd(nc, [{name + "_in": x for name, x in arrays.items()}], core_ids=[0]).results[0]
    r = {name: r[name + "_out"] for name in shapes}

    def conv_out(m):
        m = m.reshape(P, -1, MODS, PAD).transpose(2, 3, 1, 0).reshape(1, MODS, PAD, -1)
        return m[:, 0:1], m[:, 1:]

    y = r["y"].T
    gc, sc_ = conv_out(r["gdn_conv"]), conv_out(r["ssd_conv"])
    heads = lambda m: m.reshape(P, -1, HEADS, P).transpose(1, 2, 0, 3)[None]
    got = (y[:PROMPT].reshape(1, PROMPT, D), y[PROMPT:].reshape(SEQS, SEQ_LEN, D),
           heads(r["gdn_p"]), gc[0], heads(r["hgrn_p"]), r["ssd_p"].reshape(P, 1, SH, C).transpose(1, 2, 3, 0)[None], sc_[0],
           heads(r["gdn_s"]), gc[1], heads(r["hgrn_s"]), r["ssd_s"].reshape(P, SEQS, SH, C).transpose(1, 2, 3, 0)[None], sc_[1])
    return tuple(np.ascontiguousarray(g) for g in got)
```

```python
from contextlib import ExitStack, contextmanager

import numpy as np

import concourse.bass as bass
from concourse import mybir

ALU = mybir.AluOpType
ACT = mybir.ActivationFunctionType
AX = mybir.AxisListType
F32 = mybir.dt.float32
U32 = mybir.dt.uint32

P = 128
D = 1024
DK = D // P
PROMPT = 256
SEQS, SEQ_LEN = 8, 8
T = PROMPT + SEQS * SEQ_LEN
C = 64
PC = PROMPT // C
CHUNKS = PC + 1
MODS = 1 + SEQS
TAPS = 4
PAD = TAPS - 1
UPW = PAD + PROMPT + SEQS * (PAD + SEQ_LEN)
CVW = UPW - PAD
EPS = 1e-6

HEADS = 4
BLOCKS = HEADS * CHUNKS
AB_CONV = 12
AB_TAIL = 2 * HEADS
AB_TAIL_AT = 2048
AB_IN = 4104

SX = 16
SG = 4
SHPG = 8
SH = SG * SHPG
SXBC = 24
SSD_IN = 5152

E = 16
EG, EPG = 4, 4
FT = 4
FE = FT * P

SLOT = 2048
SLOTS = 8
BANKS = 4
BANK = 512
N_AB = 2 * 12 + 2 * 8
N_SSD = N_AB + 2 * 2 + 6 * E + 2 * 12 + 2 * 10
EXPERTS_A_TURN = 4
TURNS = 3
CAP = 128
SPARE = E * CAP
ROWS = SPARE + 2 * T

SMALL = {}
_at = 0
for _name, _n in (("norm_mix", 16), ("norm_ffn", 16), ("norm_final", 8), ("b_ada", 96),
                  ("ab_conv_w", 48), ("gdn_norm", 1), ("hgrn_norm", 1), ("lb_logits", 12),
                  ("ssd_conv_w", 96), ("ssd_conv_b", 24), ("ssd_norm", 16), ("ssd_d", 16),
                  ("gdn_a_log", 4), ("gdn_dt_bias", 4), ("ssd_a_log", 32), ("ssd_dt_bias", 32),
                  ("router_b", 16)):
    SMALL[_name] = (_at, _n)
    _at += _n
SMALL_COLS = _at

LEVELS = (32, 16, 8, 4, 2, 1)
CONST = {}
_at = 0
for _name, _n in (("ones", P), ("ident", P), ("incl", CHUNKS * C), ("after", 2 * C), ("seq", SEQS),
                  ("restart", T), ("eps", 1), ("row0", E), ("spare", 2 * CHUNKS)):
    CONST[_name] = (_at, _n)
    _at += _n
CONST_COLS = _at


class Count:

    def __init__(self):
        self.n, self.turn = {}, {}

    def at(self, sem, more=0):
        v = self.n.get(id(sem), 0) + more
        if id(sem) in self.turn:
            i, per = self.turn[id(sem)]
            v = i * per + v
        return v

    def up(self, sem, k=1):
        self.n[id(sem)] = self.n.get(id(sem), 0) + k
        return self.at(sem)

    @contextmanager
    def repeat(self, i, turns, per):
        start = {id(s): self.n.get(id(s), 0) for s in per}
        self.turn = {id(s): (i, k) for s, k in per.items()}
        yield
        for s, k in per.items():
            assert self.n[id(s)] - start[id(s)] == k, (self.n[id(s)] - start[id(s)], k)
            self.n[id(s)] = start[id(s)] + turns * k
        self.turn = {}


def spread(ap, axis, n):
    ap = ap.unsqueeze(axis)
    shape = list(ap.shape)
    shape[axis] = n
    return ap.to_broadcast(shape)


def trunk_program(nc, a, out):
    with ExitStack() as ctx:
        def sb(name, cols, parts=P):
            return ctx.enter_context(nc.sbuf_tensor(name, [parts, cols], F32))

        def sem(name):
            return ctx.enter_context(nc.semaphore(name))

        const = sb("const", CONST_COLS)
        small = sb("small", SMALL_COLS)
        x = sb("x", DK * T)
        h = sb("h", DK * T)
        cs = sb("cs", DK * MODS)
        mod = sb("mod", 48 * MODS)
        router = sb("router", DK * E)
        ab_tail = sb("ab_tail", DK * AB_TAIL)
        dt_tail = sb("dt_tail", DK * SH)
        cond = sb("cond", 2 * BANK)
        convst = sb("convst", SXBC * SEQS * PAD)
        convnew = sb("convnew", SXBC * MODS * PAD)
        rs = sb("rs", T)
        overflow = ctx.enter_context(nc.sbuf_tensor("overflow", [1, 2], mybir.dt.int32))
        pool_cols = (nc.sbuf_usable_end - nc.sbuf_base) // 4 - 64
        pool = sb("pool", pool_cols)
        RING = pool_cols - SLOTS * SLOT

        def K(name, parts=P):
            at, n = CONST[name]
            return const[0:parts, at:at + n]

        def W(name):
            at, n = SMALL[name]
            return small[:, at:at + n]

        ones, ident = K("ones"), K("ident")
        ident64 = const[0:C, CONST["ident"][0]:CONST["ident"][0] + C]
        ones64 = const[0:C, CONST["ones"][0]:CONST["ones"][0] + P]
        incl = K("incl", C)
        incl_p, incl_s = incl[:, 0:C], incl[:, PC * C:CHUNKS * C]
        after = K("after", C)
        after_p, after_s = after[:, 0:C], after[:, C:2 * C]
        seq = K("seq", C)
        restart = K("restart")
        eps = K("eps")
        one_col = ones[:, 0:1]

        psum = [ctx.enter_context(nc.psum_tensor(f"bank{i}", [P, BANK], F32)) for i in range(2 * BANKS)]

        def area(at, cols, parts=P):
            return pool[0:parts, at:at + cols]

        def slot(n):
            at = RING + (n % SLOTS) * SLOT
            return pool[:, at:at + SLOT]

        class Plan:
            def __init__(self, *free):
                self.free = [list(f) for f in free]

            def __call__(self, cols, parts=P):
                for f in self.free:
                    if f[1] - f[0] >= cols:
                        f[0] += cols
                        return area(f[0] - cols, cols, parts)
                raise MemoryError((cols, self.free, pool_cols, RING))

        lo = Plan((0, RING))
        UP0 = lo(AB_CONV * UPW)
        CV0 = lo(4 * 348)
        ab_free = AB_CONV * UPW + 4 * 348
        CO0 = lo(AB_CONV * T)
        zs, hq, hk, hf, hv, hg = (lo(HEADS * T) for _ in range(6))
        ab_lo_end = lo.free[0][0]
        B = BLOCKS * C
        g = Plan((0, ab_free), (ab_lo_end, pool_cols))
        levels = g(len(LEVELS) * CHUNKS * C, C)
        SQ = g(2 * HEADS * T)
        UT, WT = SQ[:, 0:B], SQ[:, B:2 * B]
        BK, KEND, BV, VTOK = (g(BLOCKS * P, C) for _ in range(4))
        EDEC, U, QKE = (g(B, C) for _ in range(3))
        MM = g(4 * B)
        M, MT, PROD, CT = (MM[0:C, i * B:(i + 1) * B] for i in range(4))
        BR = CT
        KENDM = MM[0:C, 0:SEQS * HEADS * P]
        GR, EGR = g(B), g(B)
        SS = g(SEQS * HEADS * P)
        OI = CO0[:, 2 * B:3 * B]
        VN = g(HEADS * C)
        S = g(HEADS * P)
        sc = g(288, C)
        k = Plan((0, ab_free), (ab_lo_end, pool_cols))
        assert k(len(LEVELS) * CHUNKS * C, C).offset == levels.offset
        LFC, CUM, ED, EC, KE, OIH = (k(B) for _ in range(6))
        ATT = k(B, C)
        Z = [k(B), k(B)]
        KENDH, VTOKH = k(BLOCKS * P, C), k(BLOCKS * P, C)
        SSH = k(SEQS * HEADS * P)
        KENDMH = k(SEQS * HEADS * P, C)
        SHG = k(HEADS * P)
        LB = k(40)
        lo = Plan((0, RING))
        UP1 = lo(SXBC * UPW)
        CV1 = lo(4 * 348)
        ssd_free = lo.free[0][0]
        CO1 = lo(SXBC * T)
        zs1 = lo(SX * T)
        s = Plan((0, ssd_free), (lo.free[0][0], pool_cols))
        ST = s(SH * C)
        SSS = [s(SEQS * SHPG * C), s(SEQS * SHPG * C)]
        XDT, XEND = s(CHUNKS * SHPG * C, C), s(CHUNKS * SHPG * C, C)
        BTOK, BM, CBM = s(CHUNKS * P, C), s(SEQS * P, C), s(CHUNKS * C, C)
        EG1, GM1, GBC = (s(SHPG * T, C) for _ in range(3))
        ER, YI, SQ1 = s(4 * T), s(4 * T), s(4 * T)
        DEC = s((PC + SEQS) * SH)
        sc1 = s(832, C)
        GS = GBC[:, 0:SEQS * SH]
        m = Plan((0, RING))
        HY = m(2 * CHUNKS * D, C)
        HTOK = HY[:, 0:CHUNKS * D]
        YG = HY
        XE = [m(D), m(D)]
        XT = [m(DK * CAP), m(DK * CAP)]
        SILE = [m(FE), m(FE)]
        ACTS = [m(FE), m(FE)]
        AT = [m(FE), m(FE)]
        YE = [m(D), m(D)]
        TMP = m(BANK)
        R = m(2100, C)
        o = Plan((0, RING - 2100))
        COMB = o(E * T)
        SIL, ACTV = o(FT * T), o(FT * T)
        YACC = o(DK * T)
        x_rows = nc.dram_tensor("x_rows", [ROWS, D], F32, kind="Internal").ap()
        y_rows = nc.dram_tensor("y_rows", [ROWS, D], F32, kind="Internal").ap()
        ZERO = area(10000, D)

        consts_in = sem("consts_in")
        cond_in = sem("cond_in")
        tails_in = sem("tails_in")
        conv_state_in = sem("conv_state_in")
        levels_in = sem("levels_in")
        gdn_state_in = sem("gdn_state_in")
        hgrn_state_in = sem("hgrn_state_in")
        ssd_state_in = [sem("ssd_state_in0"), sem("ssd_state_in1")]
        weights_in = [sem(f"weights_in{i}") for i in range(SLOTS)]
        weights_used = sem("weights_used")
        act_full, act_free = sem("act_full"), sem("act_free")
        dve_full, dve_free = sem("dve_full"), sem("dve_free")
        act_step, dve_step = sem("act_step"), sem("dve_step")
        mixer_done = sem("mixer_done")
        to_act = sem("to_act")
        to_dve = sem("to_dve")
        pe_from_dve = sem("pe_from_dve")
        pe_from_act = sem("pe_from_act")
        conv_in_ready = sem("conv_in_ready")
        conv_ready = sem("conv_ready")
        conv_silu = sem("conv_silu")
        gate_silu = sem("gate_silu")
        cond_turned = sem("cond_turned")
        gate_free = sem("gate_free")
        act_ready = sem("act_ready")
        act_turned = sem("act_turned")
        xt_ready = sem("xt_ready")
        xe_turned = sem("xe_turned")
        xe_in = [sem("xe_in0"), sem("xe_in1")]
        zeroed = sem("zeroed")
        zero_made = sem("zero_made")
        h_by_token = sem("h_by_token")
        rows_ready = sem("rows_ready")
        scattered = sem("scattered")
        y_stored = [sem("y_stored0"), sem("y_stored1")]
        gathered = sem("gathered")
        out_ready = sem("out_ready")
        stored = sem("stored")
        stored_state = [sem("stored_state0"), sem("stored_state1")]
        overflow_known = sem("overflow_known")
        by_layer = lambda name: [sem(f"{name}{layer}") for layer in range(2)]
        left_ready = by_layer("left_ready")
        left_full = by_layer("left_full")
        left_banks_free = by_layer("left_banks_free")
        left_weights_in = by_layer("left_weights_in")
        left_weights_free = by_layer("left_weights_free")
        left_products = by_layer("left_products")
        left_silu = by_layer("left_silu")
        left_hidden = by_layer("left_hidden")
        left_outputs = by_layer("left_outputs")
        left_step = by_layer("left_step")

        block = ctx.enter_context(nc.Block())

        @block.sync
        def _(sp):
            n = Count()

            def load(src):
                i = n.n.get(id(weights_used), 0)
                if i >= SLOTS:
                    sp.wait_ge(weights_used, n.at(weights_used, 1 - SLOTS))
                n.up(weights_used)
                sp.dma_start(slot(i).rearrange("p (k n) -> p k n", n=src.shape[-1]), src) \
                    .then_inc(weights_in[i % SLOTS], 16)

            def load_square(w, cols, nk, n_groups):
                wk = w.rearrange("(k p) n -> p k n", p=P)
                for c0 in cols[:n_groups]:
                    for k0 in range(0, nk, 4):
                        load(wk[:, k0:k0 + 4, c0:c0 + BANK])

            def experts(layer):
                wg, wu, wd = a["moe_w_gate"][layer], a["moe_w_up"][layer], a["moe_w_down"][layer]

                def gate_up(e):
                    for w in (wg, wu):
                        wk = w[bass.ds(e, 1)].rearrange("o (k p) n -> p (o k) n", p=P)
                        for k0 in (0, 4):
                            load(wk[:, k0:k0 + 4, :])

                def down(e):
                    wk = wd[bass.ds(e, 1)].rearrange("o (k p) n -> p (o k) n", p=P)
                    for k0 in (0, 2):
                        load(wk[:, k0:k0 + 2, :])

                def tokens(e, b, reuse=True):
                    if reuse:
                        n.up(xe_turned)
                        sp.wait_ge(xe_turned, n.at(xe_turned))
                    sp.dma_start(XE[b], x_rows[bass.ds(e * CAP, CAP), :]).then_inc(xe_in[b], 16)

                gate_up(0)
                gate_up(1)
                sp.wait_ge(scattered, 16 * 2 * CHUNKS * (layer + 1))
                tokens(0, 0, False)
                tokens(1, 1, False)
                down(0)
                with sp.Fori(0, TURNS) as i:
                    with n.repeat(i, TURNS, {weights_used: 6 * EXPERTS_A_TURN, xe_turned: EXPERTS_A_TURN}):
                        for j in range(EXPERTS_A_TURN):
                            e = i * EXPERTS_A_TURN + (2 + j)
                            gate_up(e)
                            tokens(e, j % 2)
                            down(i * EXPERTS_A_TURN + (1 + j))
                for e in range(2 + TURNS * EXPERTS_A_TURN, E):
                    gate_up(e)
                    tokens(e, e % 2)
                    down(e - 1)
                down(E - 1)
                n.up(xe_turned, 2)
                sp.wait_ge(overflow_known, layer + 1)
                with sp.If(sp.value_load(overflow[0:1, layer:layer + 1], min_val=0, max_val=1) > 0):
                    with sp.Fori(0, E) as e:
                        sp.wait_ge(left_weights_free[layer], e + 1)
                        for i, w in enumerate((wg, wg, wu, wu, wd, wd)):
                            wk = w[bass.ds(e, 1)].rearrange("o (k p) n -> p (o k) n", p=P)
                            nk = wk.shape[1] // 2
                            sp.dma_start(slot(i).rearrange("p (k n) -> p k n", k=nk), wk[:, i % 2 * nk:(i % 2 + 1) * nk, :]) \
                                .then_inc(left_weights_in[layer], 16)
                    sp.wait_ge(left_weights_free[layer], E + 1)

            sp.dma_start(cs[:, :].rearrange("p (k n) -> p k n", k=DK), a["c_t"].rearrange("(k p) n -> p k n", p=P)).then_inc(cond_in, 16)
            for dst, src in ((const, a["consts"]), (small, a["small"])):
                sp.dma_start(dst[:, :], src).then_inc(consts_in, 16)
            sp.dma_start(x[:, :].rearrange("p (k n) -> p k n", k=DK), a["x_t"].rearrange("(k p) n -> p k n", p=P)).then_inc(consts_in, 16)
            for dst, src, k_ in ((router, a["router_w"], DK), (ab_tail, a["ab_w_in"][0][:, AB_TAIL_AT:AB_TAIL_AT + AB_TAIL], DK),
                                 (dt_tail, a["ssd_w_in"][0][:, SSD_IN - SH:SSD_IN], DK)):
                sp.dma_start(dst[:, :].rearrange("p (k n) -> p k n", k=k_), src.rearrange("(k p) n -> p k n", p=P)).then_inc(tails_in, 16)
            every = [BANK * i for i in range(12)]
            load_square(a["w_ada"][0], every, DK, 12)
            load_square(a["ab_w_in"][0], [0, 512, 1024, 1536] + [AB_TAIL_AT + AB_TAIL + BANK * i for i in range(4)], DK, 8)
            sp.wait_ge(mixer_done, 1)
            load_square(a["ab_w_out"][0], every, DK, 2)
            experts(0)
            load_square(a["w_ada"][1], every, DK, 12)
            load_square(a["ssd_w_in"][0], [BANK * i for i in range(4, 10)] + [BANK * i for i in range(4)], DK, 10)
            sp.wait_ge(mixer_done, 2)
            load_square(a["ssd_w_out"][0], every, SX, 2)
            experts(1)

        @block.gpsimd
        def _(pool_eng):
            n = Count()

            def store(dst, src):
                pool_eng.wait_ge(out_ready, n.up(out_ready))
                n.up(stored, 16)
                pool_eng.dma_start(dst, src).then_inc(stored, 16)

            pool_eng.memset(ZERO, 0.0).then_inc(zero_made, 1)
            pool_eng.wait_ge(zero_made, 1)
            pool_eng.dma_start(x_rows[0:SPARE, :].rearrange("(i p) d -> p i d", p=P), spread(ZERO, 1, E)).then_inc(zeroed, 16)
            pool_eng.dma_start(y_rows[SPARE:ROWS, :].rearrange("(i p) d -> p i d", p=P), spread(ZERO, 1, 2 * T // P)).then_inc(zeroed, 16)

            def exchange(layer):
                rows = R[:, 1960:1960 + 2 * CHUNKS].bitcast(mybir.dt.uint32)
                pool_eng.wait_ge(rows_ready, layer + 1)
                pool_eng.wait_ge(h_by_token, layer + 1)
                if layer == 0:
                    pool_eng.wait_ge(zeroed, 32)
                for k_ in range(2):
                    for c in range(CHUNKS):
                        i = k_ * CHUNKS + c
                        pool_eng.indirect_dma_start(x_rows[:, :], bass.IndirectOffsetOnAxis(rows[:, i:i + 1], 0),
                                                    HTOK[:, c * D:(c + 1) * D], None).then_inc(scattered, 16)
                for q in range(2):
                    pool_eng.wait_ge(y_stored[q], 16 * E // 2 * (layer + 1))
                for k_ in range(2):
                    for c in range(CHUNKS):
                        i = k_ * CHUNKS + c
                        pool_eng.indirect_dma_start(YG[:, i * D:(i + 1) * D], None, y_rows[:, :],
                                                    bass.IndirectOffsetOnAxis(rows[:, i:i + 1], 0)).then_inc(gathered, 16)

            pool_eng.dma_start(convst[:, 0:AB_CONV * SEQS * PAD], a["gdn_conv_t"]).then_inc(conv_state_in, 16)
            store(out["gdn_conv"], convnew[:, 0:AB_CONV * MODS * PAD])
            pool_eng.dma_start(convst[:, :], a["ssd_conv_t"]).then_inc(conv_state_in, 16)
            pool_eng.wait_ge(weights_used, N_AB)
            pool_eng.wait_ge(conv_silu, AB_CONV)
            pool_eng.dma_start(levels, a["levels"]).then_inc(levels_in, 16)
            pool_eng.dma_start(SS.rearrange("p (b n) -> p b n", b=SEQS), a["gdn_state"].rearrange("p (b n) -> p b n", b=SEQS)).then_inc(gdn_state_in, 16)
            store(out["gdn_p"], S)
            store(out["gdn_s"], SS)
            pool_eng.wait_ge(out_ready, n.up(out_ready))
            pool_eng.wait_ge(stored, n.at(stored))
            pool_eng.dma_start(SSH.rearrange("p (b n) -> p b n", b=SEQS), a["hgrn_state"].rearrange("p (b n) -> p b n", b=SEQS)).then_inc(hgrn_state_in, 16)
            store(out["hgrn_p"], SHG)
            store(out["hgrn_s"], SSH)
            pool_eng.wait_ge(stored, n.at(stored))
            exchange(0)
            store(out["ssd_conv"], convnew[:, :])
            pool_eng.wait_ge(weights_used, N_SSD)
            pool_eng.wait_ge(conv_silu, AB_CONV + SXBC)
            for gi in range(SG):
                if gi >= 2:
                    pool_eng.wait_ge(stored_state[gi % 2], 16 * (gi // 2))
                pool_eng.dma_start(SSS[gi % 2].rearrange("p (b n) -> p b n", b=SEQS),
                                   a["ssd_state"][:, :, gi * SHPG * C:(gi + 1) * SHPG * C]).then_inc(ssd_state_in[gi % 2], 16)
                if gi >= 1:
                    q = gi - 1
                    pool_eng.wait_ge(out_ready, n.up(out_ready))
                    pool_eng.dma_start(out["ssd_s"][:, :, q * SHPG * C:(q + 1) * SHPG * C],
                                       SSS[q % 2].rearrange("p (b n) -> p b n", b=SEQS)).then_inc(stored_state[q % 2], 16)
            q = SG - 1
            pool_eng.wait_ge(out_ready, n.up(out_ready))
            pool_eng.dma_start(out["ssd_s"][:, :, q * SHPG * C:(q + 1) * SHPG * C],
                               SSS[q % 2].rearrange("p (b n) -> p b n", b=SEQS)).then_inc(stored_state[q % 2], 16)
            store(out["ssd_p"], ST)
            exchange(1)
            store(out["y"].rearrange("(k p) n -> p k n", p=P), h[:, :].rearrange("p (k n) -> p k n", k=DK))
            pool_eng.wait_ge(stored, n.at(stored))
            for i in range(2):
                pool_eng.wait_ge(stored_state[i], 16 * SG // 2)

        @block.tensor
        def _(pe):
            n = Count()

            def bank_for_act():
                i = n.n.get(id(act_full), 0)
                if i >= BANKS:
                    pe.wait_ge(act_free, n.at(act_full, 1 - BANKS))
                n.up(act_full)
                return psum[i % BANKS]

            def bank_for_dve():
                i = n.n.get(id(dve_full), 0)
                if i >= BANKS:
                    pe.wait_ge(dve_free, n.at(dve_full, 1 - BANKS))
                n.up(dve_full)
                return psum[BANKS + i % BANKS]

            def slot_read(full):
                pe.wait_ge(full, n.at(full))
                pe.sem_inc(weights_used, 1)

            def next_slot():
                i = n.n.get(id(weights_used), 0)
                n.up(weights_used)
                n.up(weights_in[i % SLOTS], 16)
                pe.wait_ge(weights_in[i % SLOTS], n.at(weights_in[i % SLOTS]))
                return slot(i)

            def from_dve():
                pe.wait_ge(pe_from_dve, n.up(pe_from_dve))

            def from_act():
                pe.wait_ge(pe_from_act, n.up(pe_from_act))

            def projections(rhs, nk, groups, bank, full):
                for _g in range(groups):
                    ws = [next_slot().rearrange("p (k n) -> p k n", n=BANK) for _ in range(nk // 4)]
                    for mt in range(4):
                        b = bank()
                        for kk in range(nk):
                            mm = pe.matmul(b[:, 0:T], ws[kk // 4][:, kk % 4, mt * P:(mt + 1) * P],
                                           rhs[:, kk * T:(kk + 1) * T], start=(kk == 0), stop=(kk == nk - 1))
                            if mt == 3 and kk % 4 == 3 and kk < nk - 1:
                                mm.then_inc(weights_used, 1)
                        mm.then_inc(full, 1)
                    slot_read(full)

            def conditioning():
                from_act()

                def turn(gq):
                    from_act()
                    b = bank_for_dve()
                    for mt in range(4):
                        mm = pe.transpose(b[:, mt * MODS:(mt + 1) * MODS], cond[0:MODS, (gq % 2) * BANK + mt * P:(gq % 2) * BANK + (mt + 1) * P],
                                          ident[0:MODS, 0:MODS])
                    mm.then_inc(dve_full, 1)

                for gq in range(12):
                    b = bank_for_act()
                    for k0 in (0, 4):
                        w = next_slot().rearrange("p (k n) -> p k n", n=BANK)
                        for kk in range(4):
                            mm = pe.matmul(b[0:MODS, :], cs[:, (k0 + kk) * MODS:(k0 + kk + 1) * MODS], w[:, kk, :],
                                           start=(k0 + kk == 0), stop=(k0 + kk == DK - 1))
                        if k0 == 0:
                            mm.then_inc(weights_used, 1)
                    mm.then_inc(act_full, 1)
                    slot_read(act_full)
                    if gq:
                        turn(gq - 1)
                turn(11)

            def norm_sum():
                from_act()
                b = bank_for_act()
                for kk in range(DK):
                    mm = pe.matmul(b[:, 0:T], ones, h[:, kk * T:(kk + 1) * T], start=(kk == 0), stop=(kk == DK - 1))
                mm.then_inc(act_full, 1)

            def token_scalars(tail, width):
                b = bank_for_dve()
                for c in range(CHUNKS):
                    for kk in range(DK):
                        mm = pe.matmul(b[0:C, c * width:(c + 1) * width], h[:, kk * T + c * C:kk * T + (c + 1) * C],
                                       tail[:, kk * width:(kk + 1) * width], start=(kk == 0), stop=(kk == DK - 1))
                mm.then_inc(dve_full, 1)

            def decay_sums(gt, nh):
                gp = gt.rearrange("p (h c) -> p h c", c=CHUNKS)
                b = bank_for_dve()
                np_, ns_ = nh * PC, nh
                pe.matmul(b[0:C, 0:np_], incl_p, gp[:, :, 0:PC], start=True, stop=True)
                pe.matmul(b[0:C, np_:np_ + ns_], incl_s, gp[:, :, PC], start=True, stop=True)
                o = np_ + ns_
                pe.matmul(b[0:C, o:o + np_], after_p, gp[:, :, 0:PC], start=True, stop=True)
                pe.matmul(b[0:C, o + np_:o + np_ + ns_], after_s, gp[:, :, PC], start=True, stop=True).then_inc(dve_full, 1)

            def blocks(bank, full, lhs, rhs, count, parts, width):
                per = BANK // width
                for i0 in range(0, count, per):
                    b = bank()
                    for i in range(i0, min(i0 + per, count)):
                        mm = pe.matmul(b[0:parts, (i - i0) * width:(i - i0 + 1) * width], lhs(i), rhs(i), start=True, stop=True)
                    mm.then_inc(full, 1)

            def turned(bank, full, src, count):
                for i0 in range(0, count, 4):
                    b = bank()
                    for i in range(i0, min(i0 + 4, count)):
                        mm = pe.transpose(b[0:C, (i - i0) * P:(i - i0 + 1) * P], src(i), ident)
                    mm.then_inc(full, 1)

            def c64(buf):
                return lambda i: buf[:, i * C:(i + 1) * C]

            def c128(buf):
                return lambda i: buf[:, i * P:(i + 1) * P]

            def head_norm_sum(sq, count):
                for i in range(count):
                    b = bank_for_act()
                    pe.matmul(b[:, 0:T], ones, sq[:, i * T:(i + 1) * T], start=True, stop=True).then_inc(act_full, 1)

            def state_chunk(Sx, QG, WTx, c):
                b = bank_for_dve()
                for hh in range(HEADS):
                    st = Sx[:, hh * P:(hh + 1) * P]
                    cols = slice(hh * T + c * C, hh * T + (c + 1) * C)
                    mm = pe.matmul(b[:, hh * C:(hh + 1) * C], st, QG[:, cols], start=True, stop=True)
                    if WTx is not None:
                        mm = pe.matmul(b[:, (HEADS + hh) * C:(HEADS + hh + 1) * C], st, WTx[:, cols], start=True, stop=True)
                mm.then_inc(dve_full, 1)

            def state_samples(SSx, QG, WTx):
                b = bank_for_dve()
                for s_ in range(SEQS):
                    for hh in range(HEADS):
                        st = SSx[:, (s_ * HEADS + hh) * P:(s_ * HEADS + hh + 1) * P]
                        cols = slice(hh * T + PROMPT + s_ * SEQ_LEN, hh * T + PROMPT + (s_ + 1) * SEQ_LEN)
                        o = hh * C + s_ * SEQ_LEN
                        mm = pe.matmul(b[:, o:o + SEQ_LEN], st, QG[:, cols], start=True, stop=True)
                        if WTx is not None:
                            mm = pe.matmul(b[:, HEADS * C + o:HEADS * C + o + SEQ_LEN], st, WTx[:, cols], start=True, stop=True)
                mm.then_inc(dve_full, 1)

            def update_chunk(kend, vtok, c):
                b = bank_for_dve()
                for hh in range(HEADS):
                    i = hh * CHUNKS + c
                    mm = pe.matmul(b[:, hh * P:(hh + 1) * P], kend[:, i * P:(i + 1) * P], vtok[:, i * P:(i + 1) * P], start=True, stop=True)
                mm.then_inc(dve_full, 1)

            def update_samples(kendm, vtok):
                for s_ in range(SEQS):
                    b = bank_for_dve()
                    for hh in range(HEADS):
                        i = hh * CHUNKS + PC
                        j = s_ * HEADS + hh
                        mm = pe.matmul(b[:, hh * P:(hh + 1) * P], kendm[:, j * P:(j + 1) * P], vtok[:, i * P:(i + 1) * P], start=True, stop=True)
                    mm.then_inc(dve_full, 1)

            def gdn():
                QT, KT, VT = CO0[:, 0:B], CO0[:, B:2 * B], CO0[:, 2 * B:3 * B]
                token_scalars(ab_tail, AB_TAIL)
                projections(h, DK, 8, bank_for_act, act_full)
                from_dve()
                decay_sums(sc[:, 0:BLOCKS], HEADS)
                from_dve()
                for i0 in range(0, B, BANK):
                    b = bank_for_dve()
                    w = min(BANK, B - i0)
                    pe.matmul(b[:, 0:w], ones64, EDEC[:, i0:i0 + w], start=True, stop=True).then_inc(dve_full, 1)
                for i0 in range(0, B, BANK):
                    b = bank_for_dve()
                    w = min(BANK, B - i0)
                    pe.matmul(b[0:C, 0:w], ones64[:, 0:C], U[:, i0:i0 + w], start=True, stop=True).then_inc(dve_full, 1)
                from_act()
                head_norm_sum(SQ, 2 * HEADS)
                from_dve()
                blocks(bank_for_dve, dve_full, c64(KT), c64(KT), BLOCKS, C, C)
                blocks(bank_for_dve, dve_full, c64(KT), c64(QT), BLOCKS, C, C)
                turned(bank_for_dve, dve_full, c64(KT), BLOCKS)
                turned(bank_for_dve, dve_full, c64(VT), BLOCKS)
                for lv in range(len(LEVELS)):
                    ct, mt = (CT, MT) if lv % 2 == 0 else (MT, CT)
                    from_dve()
                    blocks(bank_for_act, act_full, c64(ct), c64(M), BLOCKS, C, C)
                    from_act()
                    blocks(bank_for_dve, dve_full, c64(PROD), c64(mt), BLOCKS, C, C)
                    if lv < len(LEVELS) - 1:
                        blocks(bank_for_dve, dve_full, c64(mt), c64(PROD), BLOCKS, C, C)
                from_dve()
                blocks(bank_for_act, act_full, c128(BV), c64(MT), BLOCKS, P, C)
                blocks(bank_for_act, act_full, c128(BK), c64(MT), BLOCKS, P, C)
                from_act()
                from_dve()
                for c in range(PC):
                    if c:
                        from_dve()
                    state_chunk(S, GR, WT, c)
                    from_dve()
                    b = bank_for_act()
                    for hh in range(HEADS):
                        mm = pe.transpose(b[0:C, hh * P:(hh + 1) * P], VN[:, hh * C:(hh + 1) * C], ident)
                    mm.then_inc(act_full, 1)
                    from_act()
                    update_chunk(KEND, VTOK, c)
                pe.wait_ge(gdn_state_in, 16)
                state_samples(SS, GR, WT)
                from_dve()
                b = bank_for_act()
                for hh in range(HEADS):
                    mm = pe.transpose(b[0:C, hh * P:(hh + 1) * P], VN[:, hh * C:(hh + 1) * C], ident)
                mm.then_inc(act_full, 1)
                from_act()
                from_dve()
                update_samples(KENDM, VTOK)
                blocks(bank_for_dve, dve_full, c128(VTOK), c64(QKE), BLOCKS, P, C)
                from_act()
                head_norm_sum(SQ, HEADS)

            def hgrn():
                from_dve()
                blocks(bank_for_dve, dve_full, c64(hk), c64(hq), BLOCKS, C, C)
                for lv, half in enumerate(LEVELS):
                    from_dve()
                    zz = Z[lv % 2]
                    cs_ = [i for i in range(BLOCKS) if half < SEQ_LEN or i % CHUNKS < PC]
                    per = BANK // C
                    for i0 in range(0, BLOCKS, per):
                        b = bank_for_dve()
                        for i in range(i0, min(i0 + per, BLOCKS)):
                            if i in cs_:
                                mm = pe.matmul(b[0:C, (i - i0) * C:(i - i0 + 1) * C], zz[:, i * C:(i + 1) * C], zz[:, i * C:(i + 1) * C], start=True, stop=True)
                        mm.then_inc(dve_full, 1)
                from_dve()
                turned(bank_for_act, act_full, c64(KE), BLOCKS)
                turned(bank_for_act, act_full, c64(hv), BLOCKS)
                from_act()
                from_dve()
                for c in range(PC):
                    if c:
                        from_dve()
                    state_chunk(SHG, ED, None, c)
                    update_chunk(KENDH, VTOKH, c)
                pe.wait_ge(hgrn_state_in, 16)
                state_samples(SSH, ED, None)
                from_dve()
                update_samples(KENDMH, VTOKH)
                blocks(bank_for_dve, dve_full, c128(VTOKH), c64(ATT), BLOCKS, P, C)
                from_act()
                head_norm_sum(Z[0], HEADS)

            def ssd():
                token_scalars(dt_tail, SH)
                projections(h, DK, 10, bank_for_act, act_full)
                from_dve()
                decay_sums(sc1[:, 0:SH * CHUNKS], SH)
                from_dve()
                b = bank_for_dve()
                gp = sc1[:, 0:SH * CHUNKS].rearrange("p (h c) -> p c h", c=CHUNKS)
                pe.matmul(b[:, 0:PC * SH], ones64, gp[:, 0:PC, :], start=True, stop=True)
                pe.matmul(b[:, PC * SH:(PC + SEQS) * SH], ones64, GS, start=True, stop=True).then_inc(dve_full, 1)
                for gi in range(SG):
                    Bf = CO1[:, (SX + gi) * T:(SX + gi + 1) * T]
                    Cf = CO1[:, (SX + SG + gi) * T:(SX + SG + gi + 1) * T]
                    if gi == 0:
                        from_act()
                    blocks(bank_for_dve, dve_full, c64(Bf), c64(Cf), CHUNKS, C, C)
                    turned(bank_for_act, act_full, c64(Bf), CHUNKS)
                    from_dve()
                    for i0 in range(0, SHPG * T, BANK):
                        b = bank_for_dve()
                        pe.matmul(b[0:C, :], ones64[:, 0:C], GM1[:, i0:i0 + BANK], start=True, stop=True).then_inc(dve_full, 1)
                    for j in range(4):
                        b = bank_for_act()
                        for c in range(CHUNKS):
                            mm = pe.matmul(b[:, c * C:(c + 1) * C], GBC[:, (c * SHPG + 2 * j) * C:(c * SHPG + 2 * j + 2) * C],
                                           incl_p if c < PC else incl_s, start=True, stop=True)
                        mm.then_inc(act_full, 1)
                    for c in range(CHUNKS):
                        b = bank_for_dve()
                        for j in range(4):
                            mm = pe.transpose(b[0:C, j * P:(j + 1) * P], CO1[:, (4 * gi + j) * T + c * C:(4 * gi + j) * T + (c + 1) * C], ident)
                        mm.then_inc(dve_full, 1)
                    from_act()
                    for c in range(PC):
                        from_dve()
                        b = bank_for_dve()
                        for j in range(4):
                            mm = pe.matmul(b[:, j * C:(j + 1) * C], ST[:, (4 * gi + j) * P:(4 * gi + j + 1) * P], Cf[:, c * C:(c + 1) * C], start=True, stop=True)
                        mm.then_inc(dve_full, 1)
                        b = bank_for_dve()
                        pe.matmul(b[:, :], BTOK[:, c * P:(c + 1) * P], XEND[:, c * BANK:(c + 1) * BANK], start=True, stop=True).then_inc(dve_full, 1)
                    pe.wait_ge(ssd_state_in[gi % 2], 16 * (gi // 2 + 1))
                    b = bank_for_dve()
                    for s_ in range(SEQS):
                        for j in range(4):
                            o = j * C + s_ * SEQ_LEN
                            mm = pe.matmul(b[:, o:o + SEQ_LEN], SSS[gi % 2][:, s_ * BANK + j * P:s_ * BANK + (j + 1) * P],
                                           Cf[:, PROMPT + s_ * SEQ_LEN:PROMPT + (s_ + 1) * SEQ_LEN], start=True, stop=True)
                    mm.then_inc(dve_full, 1)
                    from_dve()
                    for s_ in range(SEQS):
                        b = bank_for_dve()
                        pe.matmul(b[:, :], BM[:, s_ * P:(s_ + 1) * P], XEND[:, PC * BANK:CHUNKS * BANK], start=True, stop=True).then_inc(dve_full, 1)
                    from_dve()
                    for j in range(4):
                        b = bank_for_dve()
                        for c in range(CHUNKS):
                            for o in range(2):
                                hh = 2 * j + o
                                mm = pe.matmul(b[o * C:(o + 1) * C, c * C:(c + 1) * C], XDT[:, c * BANK + hh * C:c * BANK + (hh + 1) * C],
                                               EG1[:, (hh * CHUNKS + c) * C:(hh * CHUNKS + c + 1) * C], start=True, stop=True)
                        mm.then_inc(dve_full, 1)
                    from_act()
                    b = bank_for_act()
                    for j in range(4):
                        mm = pe.matmul(b[:, 0:T], ones, SQ1[:, j * T:(j + 1) * T], start=(j == 0), stop=(j == 3))
                    mm.then_inc(act_full, 1)

            def experts(layer):
                token_scalars(router, E)
                for c in range(CHUNKS):
                    for k0 in (0, 4):
                        b = bank_for_act()
                        for kk in range(k0, k0 + 4):
                            mm = pe.transpose(b[0:C, (kk - k0) * P:(kk - k0 + 1) * P], h[:, kk * T + c * C:kk * T + (c + 1) * C], ident)
                        mm.then_inc(act_full, 1)
                from_dve()
                chosen = R[:, 1200:1280]
                b = bank_for_dve()
                for c in range(CHUNKS):
                    pe.matmul(b[0:C, 0:E], ones64[:, 0:C], chosen[:, c * E:(c + 1) * E], start=(c == 0), stop=(c == CHUNKS - 1))
                pe.matmul(b[0:C, E:E + CHUNKS * E], incl_p, chosen, start=True, stop=False)
                for c in range(CHUNKS - 1):
                    later = CHUNKS - 1 - c
                    mm = pe.matmul(b[0:C, E + (c + 1) * E:E + CHUNKS * E], ones64[:, 0:C], spread(chosen[:, c * E:(c + 1) * E], 1, later),
                                   start=False, stop=(c == CHUNKS - 2))
                mm.then_inc(dve_full, 1)

                def turn_tokens(q):
                    n.up(xe_in[q], 16)
                    pe.wait_ge(xe_in[q], n.at(xe_in[q]))
                    for k0 in (0, 4):
                        b = bank_for_act()
                        for kk in range(k0, k0 + 4):
                            mm = pe.transpose(b[:, (kk - k0) * P:(kk - k0 + 1) * P], XE[q][:, kk * P:(kk + 1) * P], ident)
                        mm.then_inc(act_full, 1)
                    pe.wait_ge(act_full, n.at(act_full))
                    pe.sem_inc(xe_turned, 1)

                def product(b, lhs, nk, ws, per, col, full):
                    for kk in range(nk):
                        mm = pe.matmul(b[:, :], lhs[:, kk * CAP:(kk + 1) * CAP], ws[kk // per][:, kk % per, col:col + BANK],
                                       start=(kk == 0), stop=(kk == nk - 1))
                        if kk == per - 1 and kk < nk - 1 and col + BANK == ws[0].shape[-1]:
                            mm.then_inc(weights_used, 1)
                    mm.then_inc(full, 1)

                def wide(ws_cols):
                    return [next_slot().rearrange("p (k n) -> p k n", n=ws_cols) for _ in range(2)]

                def gate(q):
                    pe.wait_ge(xt_ready, n.up(xt_ready))
                    product(bank_for_act(), XT[q], DK, wide(BANK), 4, 0, act_full)
                    slot_read(act_full)

                def up(q):
                    product(bank_for_dve(), XT[q], DK, wide(BANK), 4, 0, dve_full)
                    slot_read(dve_full)

                def turn_hidden(q):
                    pe.wait_ge(act_ready, n.up(act_ready))
                    b = bank_for_dve()
                    for f in range(FT):
                        mm = pe.transpose(b[:, f * CAP:(f + 1) * CAP], ACTS[q][:, f * P:(f + 1) * P], ident)
                    mm.then_inc(dve_full, 1)

                def down(q):
                    ws = wide(D)
                    pe.wait_ge(act_turned, n.up(act_turned))
                    for col in (0, BANK):
                        product(bank_for_act(), AT[q], FT, ws, 2, col, act_full)
                    slot_read(act_full)

                def expert(q, more=True):
                    gate(q)
                    turn_hidden(1 - q)
                    up(q)
                    if more:
                        turn_tokens(1 - q)
                    down(1 - q)

                turn_tokens(0)
                gate(0)
                up(0)
                turn_tokens(1)
                with pe.Fori(0, TURNS) as i:
                    per = {act_full: 5 * EXPERTS_A_TURN, dve_full: 2 * EXPERTS_A_TURN, weights_used: 6 * EXPERTS_A_TURN}
                    per |= {s_: EXPERTS_A_TURN for s_ in (act_ready, act_turned, xt_ready)}
                    per |= {w: 16 * 6 * EXPERTS_A_TURN // SLOTS for w in weights_in}
                    per |= {w: 16 * EXPERTS_A_TURN // 2 for w in xe_in}
                    with n.repeat(i, TURNS, per):
                        for j in range(EXPERTS_A_TURN):
                            expert((1 + j) % 2)
                for e in range(1 + TURNS * EXPERTS_A_TURN, E):
                    expert(e % 2, e < E - 1)
                turn_hidden((E - 1) % 2)
                down((E - 1) % 2)
                for c in range(CHUNKS):
                    from_dve()
                    b = bank_for_dve()
                    for kk in range(DK):
                        mm = pe.transpose(b[:, kk * C:(kk + 1) * C], YG[:, c * D + kk * P:c * D + (kk + 1) * P], ident64)
                    mm.then_inc(dve_full, 1)
                pe.wait_ge(overflow_known, layer + 1)
                with pe.If(pe.value_load(overflow[0:1, layer:layer + 1], min_val=0, max_val=1) > 0):
                    overflow_pass(layer)

            def overflow_pass(layer):
                pe.wait_ge(act_free, n.at(act_full))
                pe.wait_ge(dve_free, n.at(dve_full))
                pe.sem_inc(left_weights_free[layer], 1)
                pe.wait_ge(left_ready[layer], 1)
                for e in range(E):
                    if e == 2 * BANKS:
                        pe.wait_ge(left_banks_free[layer], 1)
                    for c in range(CHUNKS):
                        mm = pe.matmul(psum[e % (2 * BANKS)][:, c * C:(c + 1) * C],
                                       R[:, e * CHUNKS + c:e * CHUNKS + c + 1].to_broadcast([C, P]), ident64, start=True, stop=True)
                    mm.then_inc(left_full[layer], 1)
                with pe.Fori(0, E) as e:
                    pe.wait_ge(left_weights_in[layer], e * 96 + 96)
                    pe.wait_ge(left_banks_free[layer], e + 2)
                    gw, uw, dw = ([slot(2 * i + j).rearrange("p (k n) -> p k n", n=cols) for j in range(2)]
                                  for i, cols in enumerate((BANK, BANK, D)))
                    for f in range(FT):
                        for b, ws in ((psum[f], gw), (psum[BANKS + f], uw)):
                            for kk in range(DK):
                                mm = pe.matmul(b[:, 0:T], ws[kk // 4][:, kk % 4, f * P:(f + 1) * P], h[:, kk * T:(kk + 1) * T],
                                               start=(kk == 0), stop=(kk == DK - 1))
                    mm.then_inc(left_products[layer], 1)
                    pe.wait_ge(left_hidden[layer], e + 1)
                    for dt_ in range(DK):
                        for f in range(FT):
                            mm = pe.matmul(psum[dt_][:, 0:T], dw[f // 2][:, f % 2, dt_ * P:(dt_ + 1) * P], ACTV[:, f * T:(f + 1) * T],
                                           start=(f == 0), stop=(f == FT - 1))
                    mm.then_inc(left_outputs[layer], 1)
                    pe.wait_ge(left_outputs[layer], e + 1)
                    pe.sem_inc(left_weights_free[layer], 1)
                pe.wait_ge(left_banks_free[layer], E + 2)

            pe.wait_ge(consts_in, 48)
            pe.wait_ge(tails_in, 48)
            for layer in range(2):
                conditioning()
                norm_sum()
                from_dve()
                if layer == 0:
                    gdn()
                    hgrn()
                    from_dve()
                    projections(h, DK, 2, bank_for_dve, dve_full)
                else:
                    ssd()
                    from_dve()
                    projections(CO1, SX, 2, bank_for_dve, dve_full)
                norm_sum()
                from_dve()
                experts(layer)
            norm_sum()

        @block.scalar
        def _(act):
            n = Count()

            def bank():
                i = n.n.get(id(act_full), 0)
                n.up(act_full)
                act.wait_ge(act_full, n.at(act_full))
                return psum[i % BANKS]

            def from_dve():
                act.wait_ge(to_act, n.up(to_act))

            def step(ins):
                ins.then_inc(act_step, 1)
                act.wait_ge(act_step, n.up(act_step))

            def tell(what):
                act.sem_inc(what, 1)

            def banks_read():
                act.wait_ge(act_free, n.at(act_full))

            def squares(dst, src):
                from_dve()
                act.activation(dst, src, ACT.Square).then_inc(pe_from_act, 1)

            def conditioning():
                for gq in range(12):
                    b = bank()
                    if gq >= 2:
                        act.wait_ge(cond_turned, n.up(cond_turned))
                    act.activation(cond[0:MODS, (gq % 2) * BANK:(gq % 2 + 1) * BANK], b[0:MODS, :], ACT.Copy).then_inc(act_free, 1)
                    banks_read()
                    tell(pe_from_act)
                n.up(cond_turned, 2)

            def root(scale):
                b = bank()
                act.activation(rs[:, :], b[:, 0:T], ACT.Sqrt, scale=scale, bias=eps).then_inc(act_free, 1)
                act.wait_ge(act_free, n.at(act_full))
                tell(to_dve)

            def softplus(e1, l1, a_exp, a_log, beta=None):
                from_dve()
                if beta is not None:
                    act.activation(beta, beta, ACT.Exp, scale=-1.0)
                act.activation(a_exp, a_log, ACT.Exp)
                step(act.activation(e1, e1, ACT.Exp))
                act.activation(l1, e1, ACT.Ln, bias=one_col[0:C, :]).then_inc(to_dve, 1)

            def conv_inputs(UP, CV, CO, tiles, bias, order):
                done = 0

                def silus(upto):
                    nonlocal done
                    while done < upto:
                        act.wait_ge(conv_ready, n.up(conv_ready))
                        cv = CV[:, (done % 4) * 348:(done % 4) * 348 + 347]
                        bb = {} if bias is None else {"bias": bias[:, done:done + 1]}
                        act.activation(CO[:, done * T:done * T + PROMPT], cv[:, 0:PROMPT], ACT.Silu, **bb)
                        act.activation(CO[:, done * T + PROMPT:(done + 1) * T].rearrange("p (b l) -> p b l", l=SEQ_LEN),
                                       cv[:, PAD + PROMPT:].rearrange("p (b l) -> p b l", l=PAD + SEQ_LEN)[:, :, 0:SEQ_LEN],
                                       ACT.Silu, **bb).then_inc(conv_silu, 1)
                        done += 1

                for f in range(tiles):
                    b = bank()
                    up = UP[:, f * UPW:(f + 1) * UPW]
                    act.activation(up[:, PAD:PAD + PROMPT], b[:, 0:PROMPT], ACT.Copy)
                    act.activation(up[:, PAD + PROMPT:].rearrange("p (b l) -> p b l", l=PAD + SEQ_LEN)[:, :, PAD:],
                                   b[:, PROMPT:T].rearrange("p (b l) -> p b l", l=SEQ_LEN), ACT.Copy).then_inc(act_free, 1)
                    banks_read()
                    tell(conv_in_ready)
                    silus(f - 1)
                silus(tiles)

            def copies(dst, parts, width, banks, last):
                total = dst.shape[-1]
                for i in range(banks):
                    w = min(width, total - i * width)
                    b = bank()
                    act.activation(dst[:, i * width:i * width + w], b[0:parts, 0:w], ACT.Copy).then_inc(act_free, 1)
                act.wait_ge(act_free, n.at(act_full))
                if last:
                    tell(pe_from_act)

            def gdn():
                act.wait_ge(zeroed, 32)
                conv_inputs(UP0, CV0, CO0, AB_CONV, None, None)
                for i in range(4):
                    b = bank()
                    act.activation(zs[:, i * T:(i + 1) * T], b[:, 0:T], ACT.Silu).then_inc(act_free, 1)
                for i in range(4):
                    b = bank()
                    act.activation(hq[:, i * T:(i + 1) * T], b[:, 0:T], ACT.Copy, scale=float(P) ** -0.5).then_inc(act_free, 1)
                for i in range(4):
                    b = bank()
                    act.activation(hf[:, i * T:(i + 1) * T], b[:, 0:T], ACT.Sigmoid)
                    act.activation(hk[:, i * T:(i + 1) * T], b[:, 0:T], ACT.Sigmoid, scale=-1.0).then_inc(act_free, 1)
                for i in range(4):
                    b = bank()
                    act.activation(hv[:, i * T:(i + 1) * T], b[:, 0:T], ACT.Copy).then_inc(act_free, 1)
                for i in range(4):
                    b = bank()
                    act.activation(hg[:, i * T:(i + 1) * T], b[:, 0:T], ACT.Silu).then_inc(act_free, 1)
                softplus(sc[:, 60:80], sc[:, 80:100], sc[:, 100:104], W("gdn_a_log")[0:C, :], sc[:, 200:220])
                from_dve()
                act.activation(sc[:, 160:200], sc[:, 120:160], ACT.Exp).then_inc(to_dve, 1)
                from_dve()
                act.activation(EDEC, EDEC, ACT.Exp)
                act.activation(EGR, GR, ACT.Exp).then_inc(to_dve, 1)
                act.wait_ge(conv_silu, AB_CONV)
                act.wait_ge(weights_used, N_AB)
                act.activation(SQ, CO0[:, 0:2 * B], ACT.Square).then_inc(pe_from_act, 1)
                for i in range(2 * HEADS):
                    b = bank()
                    act.activation(SQ[:, i * T:(i + 1) * T], b[:, 0:T], ACT.Sqrt, bias=eps).then_inc(act_free, 1)
                act.wait_ge(act_free, n.at(act_full))
                tell(to_dve)
                for lv in range(len(LEVELS)):
                    copies(PROD, C, BANK, 3, True)
                copies(UT, P, BANK, 3, False)
                copies(WT, P, BANK, 3, True)
                tell(to_dve)
                for c in range(CHUNKS):
                    b = bank()
                    v = VTOK.rearrange("p (h c n) -> p h c n", h=HEADS, c=CHUNKS)[:, :, c, :]
                    act.activation(v, b[0:C, :].rearrange("p (h n) -> p h n", h=HEADS), ACT.Copy).then_inc(act_free, 1)
                    act.wait_ge(act_free, n.at(act_full))
                    tell(pe_from_act)
                squares(SQ[:, 0:B], OI)
                for i in range(HEADS):
                    b = bank()
                    act.activation(SQ[:, B + i * T:B + (i + 1) * T], b[:, 0:T], ACT.Sqrt, scale=1.0 / P, bias=eps).then_inc(act_free, 1)
                act.wait_ge(act_free, n.at(act_full))
                tell(to_dve)

            def hgrn():
                from_dve()
                act.activation(LB[:, 0:12], LB[:, 0:12], ACT.Exp).then_inc(to_dve, 1)
                from_dve()
                act.activation(LFC, hf, ACT.Ln).then_inc(to_dve, 1)
                for lv, half in enumerate(LEVELS):
                    from_dve()
                    act.activation(ED, ED, ACT.Exp).then_inc(to_dve, 1)
                from_dve()
                act.activation(KE, KE, ACT.Exp)
                act.activation(EC, CUM, ACT.Exp).then_inc(to_dve, 1)
                copies(KENDH, C, BANK, 5, False)
                copies(VTOKH, C, BANK, 5, True)
                tell(to_dve)
                squares(Z[0], OIH)
                for i in range(HEADS):
                    b = bank()
                    act.activation(Z[1][:, i * T:(i + 1) * T], b[:, 0:T], ACT.Sqrt, scale=1.0 / P, bias=eps).then_inc(act_free, 1)
                act.wait_ge(act_free, n.at(act_full))
                tell(to_dve)

            def ssd():
                conv_inputs(UP1, CV1, CO1, SXBC, W("ssd_conv_b"), None)
                for i in range(SX):
                    b = bank()
                    act.activation(zs1[:, i * T:(i + 1) * T], b[:, 0:T], ACT.Silu).then_inc(act_free, 1)
                n5 = SH * CHUNKS
                softplus(sc1[:, 2 * n5:3 * n5], sc1[:, 3 * n5:4 * n5], sc1[:, 5 * n5:5 * n5 + SH], W("ssd_a_log")[0:C, :])
                from_dve()
                act.activation(sc1[:, 3 * n5:4 * n5], sc1[:, 3 * n5:4 * n5], ACT.Exp).then_inc(to_dve, 1)
                from_dve()
                act.activation(DEC, DEC, ACT.Exp).then_inc(to_dve, 1)
                act.wait_ge(conv_silu, SXBC)
                tell(pe_from_act)
                for gi in range(SG):
                    for i in range(2):
                        w = BANK if i == 0 else P
                        b = bank()
                        act.activation(BTOK[:, i * BANK:i * BANK + w], b[0:C, 0:w], ACT.Copy).then_inc(act_free, 1)
                    for j in range(4):
                        b = bank()
                        act.activation(ER[:, j * T:(j + 1) * T], b[:, 0:T], ACT.Exp).then_inc(act_free, 1)
                    act.wait_ge(act_free, n.at(act_full))
                    tell(pe_from_act)
                    tell(to_dve)
                    from_dve()
                    act.activation(EG1, EG1, ACT.Exp).then_inc(to_dve, 1)
                    squares(SQ1, CO1[:, 4 * gi * T:4 * (gi + 1) * T])
                    root(1.0 / BANK)

            def experts(layer):
                for i in range(2 * CHUNKS):
                    b = bank()
                    act.activation(HTOK[:, i * BANK:(i + 1) * BANK], b[0:C, :], ACT.Copy).then_inc(act_free, 1)
                banks_read()
                tell(h_by_token)
                from_dve()
                act.activation(R[:, 100:180], R[:, 100:180], ACT.Sigmoid).then_inc(to_dve, 1)

                def tokens(q):
                    for i in range(2):
                        b = bank()
                        act.activation(XT[q][:, i * BANK:(i + 1) * BANK], b[:, :], ACT.Copy).then_inc(act_free, 1)
                    banks_read()
                    tell(xt_ready)

                def gate(q):
                    b = bank()
                    act.wait_ge(gate_free, n.up(gate_free))
                    act.activation(SILE[q], b[:, :], ACT.Silu).then_inc(act_free, 1)
                    banks_read()
                    tell(gate_silu)

                def outputs(e, q, reuse=True):
                    if reuse:
                        n.up(y_stored[q], 16)
                        act.wait_ge(y_stored[q], n.at(y_stored[q]))
                    for i in range(2):
                        b = bank()
                        act.activation(YE[q][:, i * BANK:(i + 1) * BANK], b[:, :], ACT.Copy).then_inc(act_free, 1)
                    banks_read()
                    act.dma_start(y_rows[bass.ds(e * CAP, CAP), :], YE[q]).then_inc(y_stored[q], 16)

                tokens(0)
                gate(0)
                tokens(1)
                reuse = layer > 0
                gate(1)
                tokens(0)
                outputs(0, 0, reuse)
                gate(0)
                tokens(1)
                outputs(1, 1, reuse)
                with act.Fori(0, TURNS) as i:
                    per = {act_full: 5 * EXPERTS_A_TURN, gate_free: EXPERTS_A_TURN}
                    per |= {y: 16 * EXPERTS_A_TURN // 2 for y in y_stored}
                    with n.repeat(i, TURNS, per):
                        for j in range(EXPERTS_A_TURN):
                            q = (3 + j) % 2
                            gate(q)
                            tokens(1 - q)
                            outputs(i * EXPERTS_A_TURN + (2 + j), 1 - q)
                gate(1)
                outputs(E - 2, 0)
                outputs(E - 1, 1)
                act.wait_ge(overflow_known, layer + 1)
                with act.If(act.value_load(overflow[0:1, layer:layer + 1], min_val=0, max_val=1) > 0):
                    with act.Fori(0, E) as e:
                        act.wait_ge(left_products[layer], e + 1)
                        for f in range(FT):
                            ins = act.activation(SIL[:, f * T:(f + 1) * T], psum[f][:, 0:T], ACT.Silu)
                        ins.then_inc(left_silu[layer], 1)

            act.wait_ge(cond_in, 16)
            act.activation(cs[:, :], cs[:, :], ACT.Silu).then_inc(pe_from_act, 1)
            act.wait_ge(consts_in, 48)
            for layer in range(2):
                if layer:
                    tell(pe_from_act)
                conditioning()
                squares(h[:, :], x[:, :])
                root(1.0 / D)
                if layer == 0:
                    gdn()
                    hgrn()
                else:
                    ssd()
                squares(h[:, :], x[:, :])
                root(1.0 / D)
                experts(layer)
            squares(h[:, :], x[:, :])
            root(1.0 / D)

        @block.vector
        def _(dve):
            n = Count()

            def bank():
                i = n.n.get(id(dve_full), 0)
                n.up(dve_full)
                dve.wait_ge(dve_full, n.at(dve_full))
                return psum[BANKS + i % BANKS]

            def freed(ins):
                ins.then_inc(dve_free, 1)
                dve.wait_ge(dve_free, n.at(dve_full))

            def step(ins):
                ins.then_inc(dve_step, 1)
                dve.wait_ge(dve_step, n.up(dve_step))

            def tell(what):
                dve.sem_inc(what, 1)

            def done(ins, what):
                step(ins)
                tell(what)

            def from_act():
                dve.wait_ge(to_dve, n.up(to_dve))

            tt, ts, stt, cp = dve.tensor_tensor, dve.tensor_scalar, dve.scalar_tensor_tensor, dve.tensor_copy

            def v3(ap, k_):
                return ap.rearrange("p (k n) -> p k n", k=k_)

            modv = mod[:, :].rearrange("p (f m) -> p f m", m=MODS)

            def conditioning(layer):
                bias = W("b_ada")[:, 48 * layer:48 * (layer + 1)]
                for gq in range(12):
                    b = bank()
                    freed(tt(modv[:, 4 * gq:4 * gq + 4, :], v3(b[:, 0:4 * MODS], 4), spread(bias[:, 4 * gq:4 * gq + 4], 2, MODS), ALU.add))
                    tell(cond_turned)
                for first, name in ((8, "norm_mix"), (32, "norm_ffn")):
                    gain = W(name)[:, DK * layer:DK * (layer + 1)]
                    step(stt(modv[:, first:first + DK, :], modv[:, first:first + DK, :], 1.0, spread(gain, 2, MODS), ALU.add, ALU.mult))

            def normalise(first):
                from_act()
                step(dve.reciprocal(rs[:, :], rs[:, :]))
                step(tt(v3(h[:, :], DK), v3(x[:, :], DK), spread(rs[:, :], 1, DK), ALU.mult))
                if first is None:
                    for kk in range(DK):
                        last = ts(h[:, kk * T:(kk + 1) * T], h[:, kk * T:(kk + 1) * T], W("norm_final")[:, kk:kk + 1], None, ALU.mult)
                    done(last, out_ready)
                    return
                hs = v3(h[:, :], DK)[:, :, PROMPT:T].rearrange("p k (b l) -> p k b l", l=SEQ_LEN)
                for kk in range(DK):
                    ts(h[:, kk * T:kk * T + PROMPT], h[:, kk * T:kk * T + PROMPT], modv[:, first + DK + kk, 0:1], modv[:, first + kk, 0:1], ALU.mult, ALU.add)
                step(tt(hs, hs, spread(modv[:, first + DK:first + 2 * DK, 1:MODS], 3, SEQ_LEN), ALU.mult))
                tt(hs, hs, spread(modv[:, first:first + DK, 1:MODS], 3, SEQ_LEN), ALU.add).then_inc(pe_from_dve, 1)

            def residual(src, kk, gate, read):
                m0 = modv[:, gate + kk, 0:1]
                ms = spread(modv[:, gate + kk, 1:MODS], 2, SEQ_LEN)
                xk = x[:, kk * T:(kk + 1) * T]
                stt(xk[:, 0:PROMPT], src[:, 0:PROMPT], m0, xk[:, 0:PROMPT], ALU.mult, ALU.add)
                ins = tt(v3(rs[:, PROMPT:T], SEQS), v3(src[:, PROMPT:T], SEQS), ms, ALU.mult)
                read(ins)
                return tt(xk[:, PROMPT:T], xk[:, PROMPT:T], rs[:, PROMPT:T], ALU.add)

            def conv_states(UP, tiles, layer):
                dve.wait_ge(conv_state_in, 16 * (layer + 1))
                upv = v3(UP, tiles)
                dve.memset(upv[:, :, 0:PAD], 0.0)
                hist = upv[:, :, PAD + PROMPT:].rearrange("p k (b l) -> p k b l", l=PAD + SEQ_LEN)[:, :, :, 0:PAD]
                step(cp(hist, convst[:, 0:tiles * SEQS * PAD].rearrange("p (k b l) -> p k b l", k=tiles, b=SEQS)))

            def convolution(UP, CV, tiles, w):
                for f in range(tiles):
                    dve.wait_ge(conv_in_ready, n.up(conv_in_ready))
                    up = UP[:, f * UPW:(f + 1) * UPW]
                    cv = CV[:, (f % 4) * 348:(f % 4) * 348 + CVW]
                    if f >= 4:
                        dve.wait_ge(conv_silu, n.up(conv_silu))
                    step(ts(cv, up[:, 0:CVW], w[:, f * TAPS:f * TAPS + 1], None, ALU.mult))
                    for j in range(1, TAPS):
                        ins = stt(cv, up[:, j:j + CVW], w[:, f * TAPS + j:f * TAPS + j + 1], cv, ALU.mult, ALU.add)
                        if j < TAPS - 1:
                            step(ins)
                        else:
                            ins.then_inc(conv_ready, 1)
                n.up(conv_silu, 4)
                dve.wait_ge(conv_silu, n.at(conv_silu))
                upv = v3(UP, tiles)
                new = convnew[:, 0:tiles * MODS * PAD].rearrange("p (k m l) -> p k m l", k=tiles, m=MODS)
                cp(new[:, :, 0, :], upv[:, :, PROMPT:PROMPT + PAD])
                hist = upv[:, :, PAD + PROMPT:].rearrange("p k (b l) -> p k b l", l=PAD + SEQ_LEN)[:, :, :, SEQ_LEN:]
                done(cp(new[:, :, 1:, :], hist), out_ready)

            def log_decay(pre, t, e1, l1, nh, a_exp, bias, gl, dt_out):
                def hc(ap):
                    return ap.rearrange("p (h c) -> p h c", c=CHUNKS)
                step(tt(hc(t), pre, spread(bias, 2, CHUNKS), ALU.add))
                step(ts(e1, t, -1.0, None, ALU.mult))
                tt(e1, e1, t, ALU.min).then_inc(to_act, 1)
                from_act()
                step(stt(dt_out, t, 0.0, l1, ALU.max, ALU.add))
                step(ts(e1, dt_out, -1.0, None, ALU.mult))
                tt(hc(gl), hc(e1), spread(a_exp, 2, CHUNKS), ALU.mult).then_inc(pe_from_dve, 1)

            def decay_sums(gam, rem, nh):
                b = bank()
                np_ = nh * PC
                o = nh * CHUNKS
                for dst, at in ((gam, 0), (rem, o)):
                    d = dst.rearrange("p (h c) -> p h c", c=CHUNKS)
                    cp(d[:, :, 0:PC], b[0:C, at:at + np_].rearrange("p (h c) -> p h c", c=PC))
                    last = cp(d[:, :, PC], b[0:C, at + np_:at + o])
                freed(last)

            def each_bank(total, width):
                for i0 in range(0, total, width):
                    yield i0, min(width, total - i0), bank()

            def state_update(Sx, dec, b):
                for hh in range(HEADS):
                    last = stt(Sx[:, hh * P:(hh + 1) * P], Sx[:, hh * P:(hh + 1) * P], dec(hh), b[:, hh * P:(hh + 1) * P], ALU.mult, ALU.add)
                freed(last)

            def head_outputs(o, root_, gain, gate, dst):
                from_act()
                step(dve.reciprocal(root_, root_))
                step(tt(o, o, root_, ALU.mult))
                step(stt(dst, o, gain, gate, ALU.mult, ALU.mult))

            def gdn():
                gl, t, e1, l1 = sc[:, 0:20], sc[:, 20:40], sc[:, 60:80], sc[:, 80:100]
                a_exp, gam, rem = sc[:, 100:104], sc[:, 120:140], sc[:, 140:160]
                egam, erem, beta, ba = sc[:, 160:180], sc[:, 180:200], sc[:, 200:220], sc[:, 240:280]
                bg = sc[:, 220:240]
                QT, KT = CO0[:, 0:B], CO0[:, B:2 * B]
                conv_states(UP0, AB_CONV, 0)
                b = bank()
                freed(cp(rs[0:C, 0:CHUNKS * AB_TAIL], b[0:C, 0:CHUNKS * AB_TAIL]))
                convolution(UP0, CV0, AB_CONV, W("ab_conv_w"))
                dve.wait_ge(weights_used, N_AB)
                step(cp(ba, rs[0:C, 0:CHUNKS * AB_TAIL]))
                bav = ba.rearrange("p (c w) -> p w c", w=AB_TAIL)
                step(cp(beta.rearrange("p (h c) -> p h c", c=CHUNKS), bav[:, 0:HEADS, :]))
                log_decay(bav[:, HEADS:2 * HEADS, :], t, e1, l1, HEADS, a_exp, W("gdn_dt_bias")[0:C, :], gl, sc[:, 40:60])
                decay_sums(gam, rem, HEADS)
                tell(to_act)
                step(ts(beta, beta, 1.0, None, ALU.add))
                step(dve.reciprocal(beta, beta))
                from_act()
                step(tt(bg, beta, egam, ALU.mult))
                glv, bev = (q_.rearrange("p (h c) -> p h c", c=CHUNKS) for q_ in (gl, beta))
                inclv = incl.rearrange("p (c n) -> p c n", n=C)
                v4 = lambda ap: ap.rearrange("p (h c n) -> p h c n", h=HEADS, c=CHUNKS)
                tt(v4(EDEC), spread(inclv, 1, HEADS), spread(glv, 3, C), ALU.mult)
                tt(v4(U), spread(spread(ident64, 1, CHUNKS), 1, HEADS), spread(bev, 3, C), ALU.mult).then_inc(pe_from_dve, 1)
                for i0, w, b in each_bank(B, BANK):
                    freed(cp(GR[:, i0:i0 + w], b[:, 0:w]))
                for i0, w, b in each_bank(B, BANK):
                    freed(cp(BR[:, i0:i0 + w], b[0:C, 0:w]))
                step(tt(v3(EDEC, BLOCKS), v3(GR[0:C, :], BLOCKS), spread(gam, 2, C), ALU.subtract))
                ts(EDEC, EDEC, 0.0, None, ALU.min).then_inc(to_act, 1)
                from_act()
                step(tt(v4(EDEC), v4(EDEC), spread(inclv, 1, HEADS), ALU.mult))
                from_act()
                step(dve.reciprocal(SQ, SQ))
                stt(QT, QT, float(P) ** -0.5, SQ[:, 0:B], ALU.mult, ALU.mult)
                tt(KT, KT, SQ[:, B:2 * B], ALU.mult).then_inc(pe_from_dve, 1)
                for i0, w, b in each_bank(B, BANK):
                    freed(tt(U[:, i0:i0 + w], b[0:C, 0:w], EDEC[:, i0:i0 + w], ALU.mult))
                step(tt(U, U, BR, ALU.mult))
                for i0, w, b in each_bank(B, BANK):
                    freed(tt(QKE[:, i0:i0 + w], b[0:C, 0:w], EDEC[:, i0:i0 + w], ALU.mult))
                for i0, w, b in each_bank(BLOCKS * P, BANK):
                    q0 = i0 // P
                    tt(v3(BK[:, i0:i0 + w], 4), v3(b[0:C, :], 4), spread(bg[:, q0:q0 + 4], 2, P), ALU.mult)
                    freed(tt(v3(KEND[:, i0:i0 + w], 4), v3(b[0:C, :], 4), spread(erem[:, q0:q0 + 4], 2, P), ALU.mult))
                for i0, w, b in each_bank(BLOCKS * P, BANK):
                    q0 = i0 // P
                    freed(tt(v3(BV[:, i0:i0 + w], 4), v3(b[0:C, :], 4), spread(beta[:, q0:q0 + 4], 2, P), ALU.mult))
                cp(v3(M, BLOCKS), spread(ident64, 1, BLOCKS))
                step(cp(v3(MT, BLOCKS), spread(ident64, 1, BLOCKS)))
                dve.wait_ge(levels_in, 16)
                for lv in range(len(LEVELS)):
                    mk = levels.rearrange("p (l n) -> p l n", l=len(LEVELS))[:, len(LEVELS) - 1 - lv, :].rearrange("p (c n) -> p c n", n=C)
                    ct, mt = (CT, MT) if lv % 2 == 0 else (MT, CT)
                    tt(v4(ct), v4(U), spread(mk, 1, HEADS), ALU.mult).then_inc(pe_from_dve, 1)
                    for i0, w, b in each_bank(B, BANK):
                        freed(stt(ct[:, i0:i0 + w], b[0:C, 0:w], -1.0, mt[:, i0:i0 + w], ALU.mult, ALU.add))
                    if lv < len(LEVELS) - 1:
                        for i0, w, b in each_bank(B, BANK):
                            freed(stt(M[:, i0:i0 + w], b[0:C, 0:w], -1.0, M[:, i0:i0 + w], ALU.mult, ALU.add))
                tell(pe_from_dve)
                dve.memset(S, 0.0)
                done(tt(GR, QT, EGR, ALU.mult), pe_from_dve)
                from_act()
                hv4 = lambda ap: ap.rearrange("p (h c n) -> p h c n", h=HEADS, c=CHUNKS)
                egr = EGR.rearrange("p (h t) -> p h t", h=HEADS)
                for c in range(CHUNKS):
                    b = bank()
                    cp(hv4(OI)[:, :, c, :], v3(b[:, 0:HEADS * C], HEADS))
                    freed(tt(v3(VN, HEADS), hv4(UT)[:, :, c, :], v3(b[:, HEADS * C:2 * HEADS * C], HEADS), ALU.subtract))
                    tell(pe_from_dve)
                    if c < PC:
                        b = bank()
                        state_update(S, lambda hh: egr[:, hh, c * C + C - 1:c * C + C], b)
                        if c < PC - 1:
                            tell(pe_from_dve)
                        else:
                            tell(out_ready)
                kv = KEND.rearrange("p (h c n) -> p h c n", h=HEADS, c=CHUNKS)[:, :, PC, :]
                for hh in range(HEADS):
                    last = tt(KENDM.rearrange("p (b h n) -> p b h n", b=SEQS, h=HEADS)[:, :, hh, :], spread(kv[:, hh, :], 1, SEQS), spread(seq, 2, P), ALU.mult)
                done(last, pe_from_dve)
                for s_ in range(SEQS):
                    b = bank()
                    at = PROMPT + s_ * SEQ_LEN + SEQ_LEN - 1
                    state_update(SS[:, s_ * HEADS * P:(s_ + 1) * HEADS * P], lambda hh: egr[:, hh, at:at + 1], b)
                tell(out_ready)
                for i0, w, b in each_bank(B, BANK):
                    freed(tt(OI[:, i0:i0 + w], b[:, 0:w], OI[:, i0:i0 + w], ALU.add))
                tell(to_act)
                head_outputs(OI, SQ[:, B:2 * B], W("gdn_norm"), zs, h[:, 0:B])
                tell(out_ready)

            def hgrn():
                lb = LB.rearrange("p (k n) -> p k n", n=4)
                lg = W("lb_logits")
                dve.wait_ge(stored, 48)
                step(tt(LB[:, 12:16], lg[:, 0:4], lg[:, 4:8], ALU.max))
                step(tt(LB[:, 12:16], LB[:, 12:16], lg[:, 8:12], ALU.max))
                tt(v3(LB[:, 0:12], 3), v3(lg, 3), spread(LB[:, 12:16], 1, 3), ALU.subtract).then_inc(to_act, 1)
                from_act()
                step(tt(LB[:, 16:20], LB[:, 4:8], LB[:, 8:12], ALU.add))
                step(tt(LB[:, 20:24], LB[:, 16:20], LB[:, 0:4], ALU.add))
                step(dve.reciprocal(LB[:, 24:28], LB[:, 20:24]))
                tt(LB[:, 28:32], LB[:, 0:4], LB[:, 24:28], ALU.mult)
                step(tt(LB[:, 32:36], LB[:, 16:20], LB[:, 24:28], ALU.mult))
                for hh in range(HEADS):
                    cols = slice(hh * T, (hh + 1) * T)
                    ts(hf[:, cols], hf[:, cols], LB[:, 32 + hh:33 + hh], LB[:, 28 + hh:29 + hh], ALU.mult, ALU.add)
                    last = ts(hk[:, cols], hk[:, cols], LB[:, 32 + hh:33 + hh], None, ALU.mult)
                done(last, pe_from_dve)
                step(ts(hf, hf, 1e-19, None, ALU.max))
                tell(to_act)
                from_act()
                for hh in range(HEADS):
                    cols = slice(hh * T, (hh + 1) * T)
                    last = dve.tensor_tensor_scan(CUM[:, cols], restart, LFC[:, cols], 0.0, ALU.mult, ALU.add)
                step(last)
                for i0, w, b in each_bank(B, BANK):
                    freed(tt(v3(ATT[0:C, i0:i0 + w], w // C), v3(b[0:C, 0:w], w // C), spread(ident64, 1, w // C), ALU.mult))
                for lv, half in enumerate(LEVELS):
                    nb = T // (2 * half) if half < SEQ_LEN else PROMPT // (2 * half)
                    used = nb * 2 * half
                    zz = Z[lv % 2]

                    def halves(buf, hh):
                        return buf[:, hh * T:hh * T + used].rearrange("p (n two w) -> p n two w", two=2, w=half)
                    for hh in range(HEADS):
                        cu, ed = halves(CUM, hh), halves(ED, hh)
                        mid = spread(cu[:, :, 0, half - 1], 2, half)
                        tt(ed[:, :, 0, :], mid, cu[:, :, 0, :], ALU.subtract)
                        last = tt(ed[:, :, 1, :], cu[:, :, 1, :], mid, ALU.subtract)
                        if used < T:
                            last = dve.memset(ED[:, hh * T + used:(hh + 1) * T], 0.0)
                    done(last, to_act)
                    from_act()
                    for hh in range(HEADS):
                        ed, zv = halves(ED, hh), halves(zz, hh)
                        tt(zv[:, :, 0, :], ed[:, :, 0, :], halves(hk, hh)[:, :, 0, :], ALU.mult)
                        last = tt(zv[:, :, 1, :], ed[:, :, 1, :], halves(hq, hh)[:, :, 1, :], ALU.mult)
                    done(last, pe_from_dve)
                    mk = levels.rearrange("p (l n) -> p l n", l=len(LEVELS))[:, lv, :]
                    for i0, w, b in each_bank(B, BANK):
                        i, end = i0 // C, (i0 + w) // C
                        runs = []
                        while i < end:
                            hh, c = divmod(i, CHUNKS)
                            stop = min(end - i, (CHUNKS if half < SEQ_LEN else PC) - c)
                            if stop > 0:
                                runs.append((i, c, stop))
                            i += max(1, min(end - i, CHUNKS - c))
                        for i, c, m_ in runs:
                            last = dve.copy_predicated(ATT[0:C, i * C:(i + m_) * C], mk[:, c * C:(c + m_) * C].bitcast(U32),
                                                       b[0:C, i * C - i0:(i + m_) * C - i0])
                        freed(last)
                cum4 = CUM.rearrange("p (h t) -> p h t", h=HEADS)
                ke4 = KE.rearrange("p (h t) -> p h t", h=HEADS)
                for hh in range(HEADS):
                    for lo_, hi_, w in ((0, PROMPT, C), (PROMPT, T, SEQ_LEN)):
                        cu = cum4[:, hh, lo_:hi_].rearrange("p (n w) -> p n w", w=w)
                        ke = ke4[:, hh, lo_:hi_].rearrange("p (n w) -> p n w", w=w)
                        last = tt(ke, spread(cu[:, :, w - 1], 2, w), cu, ALU.subtract)
                done(last, to_act)
                from_act()
                step(tt(KE, KE, hk, ALU.mult))
                tell(pe_from_dve)
                dve.memset(SHG, 0.0)
                step(tt(ED, hq, EC, ALU.mult))
                tell(pe_from_dve)
                from_act()
                ov = OIH.rearrange("p (h c n) -> p h c n", h=HEADS, c=CHUNKS)
                ec = EC.rearrange("p (h t) -> p h t", h=HEADS)
                for c in range(PC):
                    b = bank()
                    freed(cp(ov[:, :, c, :], v3(b[:, 0:HEADS * C], HEADS)))
                    b = bank()
                    state_update(SHG, lambda hh: ec[:, hh, c * C + C - 1:c * C + C], b)
                    tell(pe_from_dve if c < PC - 1 else out_ready)
                b = bank()
                freed(cp(ov[:, :, PC, :], v3(b[:, 0:HEADS * C], HEADS)))
                kv = KENDH.rearrange("p (h c n) -> p h c n", h=HEADS, c=CHUNKS)[:, :, PC, :]
                for hh in range(HEADS):
                    last = tt(KENDMH.rearrange("p (b h n) -> p b h n", b=SEQS, h=HEADS)[:, :, hh, :], spread(kv[:, hh, :], 1, SEQS), spread(seq, 2, P), ALU.mult)
                done(last, pe_from_dve)
                for s_ in range(SEQS):
                    b = bank()
                    at = PROMPT + s_ * SEQ_LEN + SEQ_LEN - 1
                    state_update(SSH[:, s_ * HEADS * P:(s_ + 1) * HEADS * P], lambda hh: ec[:, hh, at:at + 1], b)
                tell(out_ready)
                for i0, w, b in each_bank(B, BANK):
                    freed(tt(OIH[:, i0:i0 + w], b[:, 0:w], OIH[:, i0:i0 + w], ALU.add))
                tell(to_act)
                head_outputs(OIH, Z[1], W("hgrn_norm"), hg, h[:, B:2 * B])
                tell(pe_from_dve)
                dve.wait_ge(stored, 80)
                tell(mixer_done)

            def ssd():
                n5 = SH * CHUNKS
                gl, t, e1, l1, dt = (sc1[:, i * n5:(i + 1) * n5] for i in range(5))
                gam, rem = e1, l1
                a_exp = sc1[:, 5 * n5:5 * n5 + SH]
                conv_states(UP1, SXBC, 1)
                b = bank()
                freed(cp(rs[0:C, 0:n5], b[0:C, 0:n5]))
                convolution(UP1, CV1, SXBC, W("ssd_conv_w"))
                dve.wait_ge(weights_used, N_SSD)
                log_decay(rs[0:C, 0:n5].rearrange("p (c h) -> p h c", c=CHUNKS), t, e1, l1, SH, a_exp, W("ssd_dt_bias")[0:C, :], gl, dt)
                decay_sums(gam, rem, SH)
                tell(to_act)
                glv = gl.rearrange("p (h c) -> p c h", c=CHUNKS)
                tt(GS.rearrange("p (b h) -> p b h", b=SEQS), spread(glv[:, PC, :], 1, SEQS), spread(seq, 2, SH), ALU.mult).then_inc(pe_from_dve, 1)
                from_act()
                b = bank()
                freed(cp(DEC, b[:, 0:(PC + SEQS) * SH]))
                tell(to_act)
                from_act()
                dve.memset(ST, 0.0)
                decv = DEC.rearrange("p (c h) -> p c h", h=SH)
                inclv = incl.rearrange("p (c n) -> p c n", n=C)
                for gi in range(SG):
                    hs = slice(gi * SHPG * CHUNKS, (gi + 1) * SHPG * CHUNKS)

                    def g8(ap):
                        return ap[:, hs].rearrange("p (h c) -> p h c", c=CHUNKS)
                    b = bank()
                    freed(tt(CBM, b[0:C, 0:T], incl, ALU.mult))
                    v4 = lambda ap: ap.rearrange("p (h c n) -> p h c n", h=SHPG, c=CHUNKS)
                    tt(v4(GM1), spread(inclv, 1, SHPG), spread(g8(gl), 3, C), ALU.mult)
                    cp(GBC.rearrange("p (c h n) -> p c h n", c=CHUNKS, h=SHPG), spread(g8(gl).rearrange("p h c -> p c h"), 3, C)).then_inc(pe_from_dve, 1)
                    for i0, w, b in each_bank(SHPG * T, BANK):
                        q0 = gi * SHPG * CHUNKS + i0 // C
                        freed(tt(v3(EG1[:, i0:i0 + w], 8), v3(b[0:C, :], 8), spread(gam[:, q0:q0 + 8], 2, C), ALU.subtract))
                    step(ts(EG1, EG1, 0.0, None, ALU.min))
                    xdt = XDT.rearrange("p (c h n) -> p c h n", c=CHUNKS, h=SHPG)
                    xend = XEND.rearrange("p (c h n) -> p c h n", c=CHUNKS, h=SHPG)
                    for c in range(CHUNKS):
                        b = bank()
                        freed(tt(xdt[:, c], v3(b[0:C, :], SHPG), spread(g8(dt)[:, :, c], 2, C), ALU.mult))
                    for c in range(CHUNKS):
                        last = tt(xend[:, c], xdt[:, c], spread(g8(rem)[:, :, c], 2, C), ALU.mult)
                    step(last)
                    tell(pe_from_dve)
                    from_act()
                    tell(to_act)
                    yi = YI.rearrange("p (j c n) -> p j c n", j=4, c=CHUNKS)
                    er = ER.rearrange("p (j c n) -> p j c n", j=4, c=CHUNKS)
                    stg = ST[:, gi * BANK:(gi + 1) * BANK]
                    for c in range(PC):
                        b = bank()
                        freed(tt(yi[:, :, c, :], v3(b[:, 0:4 * C], 4), er[:, :, c, :], ALU.mult))
                        b = bank()
                        step(tt(v3(stg, SHPG), v3(stg, SHPG), spread(decv[:, c, gi * SHPG:(gi + 1) * SHPG], 2, C), ALU.mult))
                        freed(tt(stg, b[:, :], stg, ALU.add))
                        if c < PC - 1:
                            tell(pe_from_dve)
                    b = bank()
                    freed(tt(yi[:, :, PC, :], v3(b[:, 0:4 * C], 4), er[:, :, PC, :], ALU.mult))
                    tt(v3(BM, SEQS), spread(BTOK[:, PC * P:CHUNKS * P], 1, SEQS), spread(seq, 2, P), ALU.mult).then_inc(pe_from_dve, 1)
                    for s_ in range(SEQS):
                        b = bank()
                        st = SSS[gi % 2][:, s_ * BANK:(s_ + 1) * BANK]
                        step(tt(v3(st, SHPG), v3(st, SHPG), spread(decv[:, PC + s_, gi * SHPG:(gi + 1) * SHPG], 2, C), ALU.mult))
                        freed(tt(st, b[:, :], st, ALU.add))
                    tell(out_ready)
                    from_act()
                    step(tt(v4(EG1), v4(EG1), spread(CBM.rearrange("p (c n) -> p c n", n=C), 1, SHPG), ALU.mult))
                    tell(pe_from_dve)
                    for j in range(4):
                        q = 4 * gi + j
                        xt, yt = CO1[:, q * T:(q + 1) * T], YI[:, j * T:(j + 1) * T]
                        step(stt(yt, xt, W("ssd_d")[:, q:q + 1], yt, ALU.mult, ALU.add))
                        b = bank()
                        freed(tt(yt, b[:, 0:T], yt, ALU.add))
                        step(tt(xt, yt, zs1[:, q * T:(q + 1) * T], ALU.mult))
                    tell(to_act)
                    from_act()
                    step(dve.reciprocal(rs[:, :], rs[:, :]))
                    for j in range(4):
                        q = 4 * gi + j
                        xt = CO1[:, q * T:(q + 1) * T]
                        step(stt(xt, xt, W("ssd_norm")[:, q:q + 1], rs[:, :], ALU.mult, ALU.mult))
                tell(pe_from_dve)
                tell(out_ready)
                dve.wait_ge(stored, 112)
                for i in range(2):
                    dve.wait_ge(stored_state[i], 16 * SG // 2)
                tell(mixer_done)

            def route(layer):
                sg, bi = R[:, 100:180], R[:, 180:260]
                b = bank()
                freed(cp(sg, b[0:C, 0:CHUNKS * E]))
                tell(to_act)
                from_act()
                step(tt(v3(bi, CHUNKS), v3(sg, CHUNKS), spread(W("router_b")[0:C, :], 1, CHUNKS), ALU.add))
                v = bi.rearrange("p (g e) -> p g e", e=EPG)
                NG = CHUNKS * EG
                t = [R[:, 300 + 20 * i:320 + 20 * i] for i in range(20)]
                hi1, lo1, hi2, lo2, mid, m1, m2, gs, gsel = t[:9]
                tt(hi1, v[:, :, 0], v[:, :, 1], ALU.max)
                tt(lo1, v[:, :, 0], v[:, :, 1], ALU.min)
                tt(hi2, v[:, :, 2], v[:, :, 3], ALU.max)
                step(tt(lo2, v[:, :, 2], v[:, :, 3], ALU.min))
                tt(m1, hi1, hi2, ALU.max)
                tt(mid, hi1, hi2, ALU.min)
                step(tt(m2, lo1, lo2, ALU.max))
                step(tt(m2, m2, mid, ALU.max))
                step(tt(gs, m1, m2, ALU.add))
                gmax, nf = R[:, 800:805], R[:, 810:815]
                gv, sv = (q.rearrange("p (c g) -> p c g", g=EG) for q in (gs, gsel))
                dve.memset(nf, 1.0)
                step(dve.tensor_reduce(gmax, gv, AX.X, ALU.max))
                for g_ in range(EG):
                    step(tt(sv[:, :, g_], gv[:, :, g_], gmax, ALU.is_equal))
                    step(tt(sv[:, :, g_], sv[:, :, g_], nf, ALU.mult))
                    step(tt(nf, nf, sv[:, :, g_], ALU.subtract))
                cmpv = R[:, 900:900 + NG * EPG * 3].rearrange("p (g e j) -> p g e j", g=NG, e=EPG)
                for e in range(EPG):
                    for q, j in enumerate([j for j in range(EPG) if j != e]):
                        last = tt(cmpv[:, :, e, q], v[:, :, j], v[:, :, e], ALU.is_ge if j < e else ALU.is_gt)
                step(last)
                cnt = R[:, 1200:1200 + NG * EPG]
                step(dve.tensor_reduce(cnt, R[:, 900:900 + NG * EPG * 3].rearrange("p (g j) -> p g j", j=3), AX.X, ALU.add))
                step(ts(cnt, cnt, 1.5, None, ALU.is_lt))
                cg = cnt.rearrange("p (g e) -> p g e", e=EPG)
                step(tt(cg, cg, spread(gsel, 2, EPG), ALU.mult))
                tell(pe_from_dve)
                ce = lambda ap: ap.rearrange("p (c e) -> p c e", e=E)
                w, tot = R[:, 1600:1680], R[:, 820:825]
                step(tt(w, cnt, sg, ALU.mult))
                step(dve.tensor_reduce(tot, ce(w), AX.X, ALU.add))
                step(dve.reciprocal(tot, tot))
                step(tt(ce(w), ce(w), spread(tot, 2, E), ALU.mult))
                order, pick = R[:, 1280:1360], R[:, 1360:1520]
                og = order.rearrange("p (g e) -> p g e", e=EPG)
                step(cp(og[:, :, 0], cg[:, :, 0]))
                for e in range(1, EPG):
                    step(tt(og[:, :, e], og[:, :, e - 1], cg[:, :, e], ALU.add))
                for k_ in range(2):
                    stt(pick[:, k_ * 80:(k_ + 1) * 80], order, float(k_ + 1), cnt, ALU.is_equal, ALU.mult)
                upto, row = R[:, 1980:2060], R[:, 1520:1600]
                fits, prod = R[:, 1870:1950], R[:, 1680:1840]
                b = bank()
                cp(R[:, 2060:2076], b[0:C, 0:E])
                freed(cp(upto, b[0:C, E:E + CHUNKS * E]))
                step(ts(fits, upto, CAP + 0.5, None, ALU.is_lt))
                step(tt(ce(row), ce(upto), spread(K("row0", C), 1, CHUNKS), ALU.add))
                step(tt(v3(pick, 2), v3(pick, 2), spread(fits, 1, 2), ALU.mult))
                kce = lambda ap: ap.rearrange("p (k c e) -> p (k c) e", k=2, c=CHUNKS)
                rows, placed, wk, spare = R[:, 1840:1850], R[:, 1860:1870], R[:, 1850:1860], K("spare", C)
                step(dve.tensor_reduce(placed, kce(pick), AX.X, ALU.add))
                step(tt(v3(prod, 2), v3(pick, 2), spread(row, 1, 2), ALU.mult))
                step(dve.tensor_reduce(rows, kce(prod), AX.X, ALU.add))
                step(tt(v3(prod, 2), v3(pick, 2), spread(w, 1, 2), ALU.mult))
                step(dve.tensor_reduce(wk, kce(prod), AX.X, ALU.add))
                step(tt(placed, placed, spare, ALU.mult))
                step(tt(rows, rows, placed, ALU.subtract))
                step(tt(rows, rows, spare, ALU.add))
                done(cp(R[:, 1960:1970].bitcast(mybir.dt.uint32), rows), rows_ready)
                most = R[0:1, 2076:2077]
                step(dve.tensor_reduce(most, R[0:1, 2060:2076], AX.X, ALU.max))
                step(ts(most, most, CAP + 0.5, None, ALU.is_gt))
                done(cp(overflow[0:1, layer:layer + 1], most), overflow_known)

            def experts(layer):
                route(layer)
                wk = R[:, 1850:1860]

                def hidden_turned(q):
                    b = bank()
                    freed(cp(AT[q], b[:, :]))
                    tell(act_turned)

                def hidden(q):
                    b = bank()
                    dve.wait_ge(gate_silu, n.up(gate_silu))
                    freed(tt(ACTS[q], b[:, :], SILE[q], ALU.mult))
                    tell(act_ready)
                    tell(gate_free)

                hidden(0)
                with dve.Fori(0, TURNS) as i:
                    with n.repeat(i, TURNS, {dve_full: 2 * EXPERTS_A_TURN, gate_silu: EXPERTS_A_TURN}):
                        for j in range(EXPERTS_A_TURN):
                            q = (1 + j) % 2
                            hidden_turned(1 - q)
                            hidden(q)
                for e in range(1 + TURNS * EXPERTS_A_TURN, E):
                    hidden_turned(1 - e % 2)
                    hidden(e % 2)
                hidden_turned((E - 1) % 2)
                dve.wait_ge(gathered, 16 * 2 * CHUNKS * (layer + 1))
                xv = v3(x[:, :], DK)
                for c in range(CHUNKS):
                    y0, y1 = YG[:, c * D:(c + 1) * D], YG[:, (CHUNKS + c) * D:(CHUNKS + c + 1) * D]
                    step(ts(y0, y0, wk[:, c:c + 1], None, ALU.mult))
                    done(stt(y0, y1, wk[:, CHUNKS + c:CHUNKS + c + 1], y0, ALU.mult, ALU.add), pe_from_dve)
                for c in range(CHUNKS):
                    b = bank()
                    if c < PC:
                        freed(tt(v3(TMP, DK), v3(b[:, :], DK), spread(modv[:, 40:48, 0], 2, C), ALU.mult))
                    else:
                        four = lambda ap: ap.rearrange("p (k b l) -> p k b l", k=DK, b=SEQS)
                        freed(tt(four(TMP), four(b[:, :]), spread(modv[:, 40:48, 1:MODS], 3, SEQ_LEN), ALU.mult))
                    xc = xv[:, :, c * C:(c + 1) * C]
                    step(tt(xc, xc, v3(TMP, DK), ALU.add))
                with dve.If(dve.value_load(overflow[0:1, layer:layer + 1], min_val=0, max_val=1) > 0):
                    overflow_pass(layer)

            def overflow_pass(layer):
                m = Count()
                own = left_step[layer]

                def step(ins):
                    ins.then_inc(own, 1)
                    dve.wait_ge(own, m.up(own))

                w, fits, left = R[:, 1600:1680], R[:, 1870:1950], R[:, 1680:1760]
                step(tt(left, w, fits, ALU.mult))
                step(tt(left, w, left, ALU.subtract))
                cp(R[:, 0:80].rearrange("p (e c) -> p e c", c=CHUNKS), left.rearrange("p (c e) -> p e c", e=E)).then_inc(left_ready[layer], 1)
                step(dve.memset(YACC, 0.0))
                for e in range(E):
                    dve.wait_ge(left_full[layer], e + 1)
                    step(cp(COMB[:, e * T:(e + 1) * T], psum[e % (2 * BANKS)][:, 0:T]))
                    if e % (2 * BANKS) == 2 * BANKS - 1:
                        dve.sem_inc(left_banks_free[layer], 1)
                with dve.Fori(0, E) as e:
                    with m.repeat(e, E, {own: 2 * FT + DK}):
                        dve.wait_ge(left_silu[layer], e + 1)
                        for f in range(FT):
                            dst = ACTV[:, f * T:(f + 1) * T]
                            step(tt(dst, psum[BANKS + f][:, 0:T], SIL[:, f * T:(f + 1) * T], ALU.mult))
                            step(tt(dst, dst, COMB[:, bass.ds(e * T, T)], ALU.mult))
                        dve.sem_inc(left_hidden[layer], 1)
                        dve.wait_ge(left_outputs[layer], e + 1)
                        for dt_ in range(DK):
                            y = YACC[:, dt_ * T:(dt_ + 1) * T]
                            step(tt(y, psum[dt_][:, 0:T], y, ALU.add))
                        dve.sem_inc(left_banks_free[layer], 1)
                for kk in range(DK):
                    step(residual(YACC[:, kk * T:(kk + 1) * T], kk, 40, step))

            dve.wait_ge(consts_in, 48)
            dve.sem_inc(gate_free, 2)
            for layer in range(2):
                tell(to_act)
                conditioning(layer)
                normalise(0)
                if layer == 0:
                    gdn()
                    hgrn()
                else:
                    ssd()
                for kk in range(DK):
                    b = bank()
                    step(residual(b, kk, 16, freed))
                tell(to_act)
                normalise(24)
                experts(layer)
            tell(to_act)
            normalise(None)


_WEIGHTS = ("w_ada", "ab_w_in", "ab_w_out", "ssd_w_in", "ssd_w_out", "moe_w_gate", "moe_w_up", "moe_w_down")


def _constants():
    def put(a, name, v):
        at, cols = CONST[name]
        a[:v.shape[0], at:at + cols] = v.reshape(v.shape[0], cols)

    a = np.zeros((P, CONST_COLS), np.float32)
    s, t = np.arange(C)[:, None], np.arange(C)[None, :]
    same = s // SEQ_LEN == t // SEQ_LEN
    put(a, "ones", np.ones((P, P), np.float32))
    put(a, "ident", np.eye(P, dtype=np.float32))
    put(a, "incl", np.stack([s <= t] * PC + [(s <= t) & same], 1).astype(np.float32))
    put(a, "after", np.stack([s > t, (s > t) & same], 1).astype(np.float32))
    put(a, "seq", (s // SEQ_LEN == np.arange(SEQS)[None, :]).astype(np.float32))
    tok = np.arange(T)
    first = np.where(tok < PROMPT, tok % C == 0, (tok - PROMPT) % SEQ_LEN == 0)
    put(a, "restart", np.broadcast_to(1.0 - first.astype(np.float32), (P, T)))
    put(a, "eps", np.full((P, 1), EPS, np.float32))
    put(a, "row0", np.broadcast_to(np.arange(E, dtype=np.float32) * CAP - 1, (P, E)))
    token = np.arange(C)[:, None, None] + C * np.arange(CHUNKS)[None, None, :]
    put(a, "spare", (SPARE + 2 * token + np.arange(2)[None, :, None]).astype(np.float32))
    levels = []
    for half in LEVELS:
        m = (s // (2 * half) == t // (2 * half)) & (s // half % 2 == 0) & (t // half % 2 == 1)
        levels.append(np.stack([m] * PC + [m & (half < SEQ_LEN)], 1))
    return a, np.stack(levels, 1).astype(np.float32).reshape(C, -1)


def _small(v):
    a = np.zeros((P, SMALL_COLS), np.float32)

    def put(name, x):
        at, cols = SMALL[name]
        a[:, at:at + cols] = x

    def features(x):
        x = np.asarray(x)
        return x.reshape(-1, P).T

    def taps(w):
        return np.asarray(w).reshape(TAPS, -1, P).transpose(2, 1, 0).reshape(P, -1)

    for name in ("norm_mix", "norm_ffn", "norm_final", "b_ada", "gdn_norm", "hgrn_norm", "ssd_conv_b", "ssd_norm"):
        put(name, features(v[name]))
    put("lb_logits", features(v["hgrn_lb_logits"]))
    put("ab_conv_w", taps(v["ab_conv_w"]))
    put("ssd_conv_w", taps(v["ssd_conv_w"]))
    put("ssd_d", features(np.repeat(np.asarray(v["ssd_d"]).reshape(-1), C)))
    for name in ("gdn_a_log", "gdn_dt_bias", "ssd_a_log", "ssd_dt_bias", "router_b"):
        put(name, np.broadcast_to(np.asarray(v[name]).reshape(1, -1), (P, SMALL[name][1])))
    return a


def kernel(**v):
    import concourse.bacc as bacc
    from concourse.bass_utils import run_bass_kernel_spmd

    v = {name: np.asarray(x) for name, x in v.items()}

    def conv_t(st):
        return st[0].reshape(SEQS, PAD, -1, P).transpose(3, 2, 0, 1).reshape(P, -1)

    consts, levels = _constants()
    arrays = {
        "consts": consts, "levels": levels, "small": _small(v),
        "x_t": np.concatenate([v["x_prompt"].reshape(-1, D), v["x_sample"].reshape(-1, D)]).T,
        "c_t": np.concatenate([v["c_prompt"], v["c_sample"]]).T,
        "router_w": v["router_w"],
        "gdn_conv_t": conv_t(v["state_gdn_conv"]), "ssd_conv_t": conv_t(v["state_ssd_conv"]),
        "gdn_state": v["state_gdn"][0].transpose(2, 0, 1, 3).reshape(P, -1),
        "hgrn_state": v["state_hgrn"][0].transpose(2, 0, 1, 3).reshape(P, -1),
        "ssd_state": v["state_ssd"][0].transpose(3, 0, 1, 2).reshape(P, SEQS, -1),
    }
    arrays |= {name: v[name] for name in _WEIGHTS}
    arrays = {name: np.ascontiguousarray(x) for name, x in arrays.items()}
    shapes = {"y": (D, T), "gdn_p": (P, HEADS * P), "gdn_s": (P, SEQS * HEADS * P), "gdn_conv": (P, AB_CONV * MODS * PAD),
              "hgrn_p": (P, HEADS * P), "hgrn_s": (P, SEQS * HEADS * P), "ssd_p": (P, SH * C), "ssd_s": (P, SEQS, SH * C),
              "ssd_conv": (P, SXBC * MODS * PAD)}
    nc = bacc.Bacc("TRN2", target_bir_lowering=False, num_devices=1)
    a = {name: nc.dram_tensor(name + "_in", x.shape, F32, kind="ExternalInput").ap() for name, x in arrays.items()}
    out = {name: nc.dram_tensor(name + "_out", shape, F32, kind="ExternalOutput").ap() for name, shape in shapes.items()}
    trunk_program(nc, a, out)
    r = run_bass_kernel_spmd(nc, [{name + "_in": x for name, x in arrays.items()}], core_ids=[0]).results[0]
    r = {name: r[name + "_out"] for name in shapes}

    def conv_out(m):
        m = m.reshape(P, -1, MODS, PAD).transpose(2, 3, 1, 0).reshape(1, MODS, PAD, -1)
        return m[:, 0:1], m[:, 1:]

    y = r["y"].T
    gc, sc_ = conv_out(r["gdn_conv"]), conv_out(r["ssd_conv"])
    heads = lambda m: m.reshape(P, -1, HEADS, P).transpose(1, 2, 0, 3)[None]
    got = (y[:PROMPT].reshape(1, PROMPT, D), y[PROMPT:].reshape(SEQS, SEQ_LEN, D),
           heads(r["gdn_p"]), gc[0], heads(r["hgrn_p"]), r["ssd_p"].reshape(P, 1, SH, C).transpose(1, 2, 3, 0)[None], sc_[0],
           heads(r["gdn_s"]), gc[1], heads(r["hgrn_s"]), r["ssd_s"].reshape(P, SEQS, SH, C).transpose(1, 2, 3, 0)[None], sc_[1])
    return tuple(np.ascontiguousarray(g) for g in got)
```

```python
from contextlib import ExitStack, contextmanager

import numpy as np

import concourse.bass as bass
from concourse import mybir

ALU = mybir.AluOpType
ACT = mybir.ActivationFunctionType
AX = mybir.AxisListType
F32 = mybir.dt.float32
U32 = mybir.dt.uint32

P = 128
D = 1024
DK = D // P
PROMPT = 256
SEQS, SEQ_LEN = 8, 8
T = PROMPT + SEQS * SEQ_LEN
C = 64
PC = PROMPT // C
CHUNKS = PC + 1
MODS = 1 + SEQS
TAPS = 4
PAD = TAPS - 1
UPW = PAD + PROMPT + SEQS * (PAD + SEQ_LEN)
CVW = UPW - PAD
EPS = 1e-6

HEADS = 4
BLOCKS = HEADS * CHUNKS
AB_CONV = 12
AB_TAIL = 2 * HEADS
AB_TAIL_AT = 2048

SX = 16
SG = 4
SHPG = 8
SH = SG * SHPG
SXBC = 24
SSD_IN = 5152

E = 16
EG, EPG = 4, 4
FT = 4
FE = FT * P

SLOT = 2048
SLOTS = 8
BANKS = 4
BANK = 512

COND_FIRST = ([(0, g) for g in range(4)], [])
COND_NORM = ([(0, g) for g in range(4, 8)], [(1, 6), (1, 7)])
COND_MIXED = ([(0, 8), (0, 9)], [(1, 8), (1, 9)])
COND_AGAIN = ([(0, 10)], [(1, 10)])
COND_ROUTE = ([(0, 11)], [(1, 11)])
COND_MOVE = ([(1, 0), (1, 1), (1, 2)], [])
COND_BACK = ([(1, 3), (1, 4), (1, 5)], [])
N_AB = 2 * 8 + 2 * 8
N_SSD = N_AB + 2 * (2 + 1 + 1 + 3 + 3 + 2) + 2 * 2 + 6 * E + 2 * 10
EXPERTS_A_TURN = 4
TURNS = 3
CAP = 128
SPARE = E * CAP
ROWS = SPARE + 2 * T

SMALL = {}
_at = 0
for _name, _n in (("norm_mix", 16), ("norm_ffn", 16), ("norm_final", 8), ("b_ada", 96),
                  ("ab_conv_w", 48), ("gdn_norm", 1), ("hgrn_norm", 1), ("lb_logits", 12),
                  ("ssd_conv_w", 96), ("ssd_conv_b", 24), ("ssd_norm", 16), ("ssd_d", 16),
                  ("gdn_a_log", 4), ("gdn_dt_bias", 4), ("ssd_a_log", 32), ("ssd_dt_bias", 32),
                  ("router_b", 16)):
    SMALL[_name] = (_at, _n)
    _at += _n
SMALL_COLS = _at

LEVELS = (32, 16, 8, 4, 2, 1)
CONST = {}
_at = 0
for _name, _n in (("ones", P), ("ident", P), ("incl", CHUNKS * C), ("after", 2 * C), ("seq", SEQS),
                  ("restart", T), ("eps", 1), ("row0", E), ("spare", 2 * CHUNKS)):
    CONST[_name] = (_at, _n)
    _at += _n
CONST_COLS = _at


class Count:

    def __init__(self):
        self.n, self.turn = {}, {}

    def at(self, sem, more=0):
        v = self.n.get(id(sem), 0) + more
        if id(sem) in self.turn:
            i, per = self.turn[id(sem)]
            v = i * per + v
        return v

    def up(self, sem, k=1):
        self.n[id(sem)] = self.n.get(id(sem), 0) + k
        return self.at(sem)

    @contextmanager
    def repeat(self, i, turns, per):
        start = {id(s): self.n.get(id(s), 0) for s in per}
        self.turn = {id(s): (i, k) for s, k in per.items()}
        yield
        for s, k in per.items():
            assert self.n[id(s)] - start[id(s)] == k, (self.n[id(s)] - start[id(s)], k)
            self.n[id(s)] = start[id(s)] + turns * k
        self.turn = {}


def spread(ap, axis, n):
    ap = ap.unsqueeze(axis)
    shape = list(ap.shape)
    shape[axis] = n
    return ap.to_broadcast(shape)


def trunk_program(nc, a, out):
    with ExitStack() as ctx:
        def sb(name, cols, parts=P):
            return ctx.enter_context(nc.sbuf_tensor(name, [parts, cols], F32))

        def sem(name):
            return ctx.enter_context(nc.semaphore(name))

        const = sb("const", CONST_COLS)
        small = sb("small", SMALL_COLS)
        x = sb("x", DK * T)
        h = sb("h", DK * T)
        cs = sb("cs", DK * MODS)
        mod0 = sb("mod0", 48 * MODS)
        router = sb("router", DK * E)
        ab_tail = sb("ab_tail", DK * AB_TAIL)
        dt_tail = sb("dt_tail", DK * SH)
        cond = sb("cond", 2 * BANK)
        convst = sb("convst", SXBC * SEQS * PAD)
        convnew = sb("convnew", SXBC * MODS * PAD)
        rs = sb("rs", T)
        overflow = ctx.enter_context(nc.sbuf_tensor("overflow", [1, 2], mybir.dt.int32))
        pool_cols = (nc.sbuf_usable_end - nc.sbuf_base) // 4 - 64
        pool = sb("pool", pool_cols)
        RING = pool_cols - SLOTS * SLOT

        def K(name, parts=P):
            at, n = CONST[name]
            return const[0:parts, at:at + n]

        def W(name):
            at, n = SMALL[name]
            return small[:, at:at + n]

        ones, ident = K("ones"), K("ident")
        ident64 = const[0:C, CONST["ident"][0]:CONST["ident"][0] + C]
        ones64 = const[0:C, CONST["ones"][0]:CONST["ones"][0] + P]
        incl = K("incl", C)
        incl_p, incl_s = incl[:, 0:C], incl[:, PC * C:CHUNKS * C]
        after = K("after", C)
        after_p, after_s = after[:, 0:C], after[:, C:2 * C]
        seq = K("seq", C)
        restart = K("restart")
        eps = K("eps")
        one_col = ones[:, 0:1]

        psum = [ctx.enter_context(nc.psum_tensor(f"bank{i}", [P, BANK], F32)) for i in range(2 * BANKS)]

        def area(at, cols, parts=P):
            return pool[0:parts, at:at + cols]

        def slot(n):
            at = RING + (n % SLOTS) * SLOT
            return pool[:, at:at + SLOT]

        class Plan:
            def __init__(self, *free):
                self.free = [list(f) for f in free]

            def __call__(self, cols, parts=P):
                for f in self.free:
                    if f[1] - f[0] >= cols:
                        f[0] += cols
                        return area(f[0] - cols, cols, parts)
                raise MemoryError((cols, self.free, pool_cols, RING))

        lo = Plan((0, RING))
        UP0 = lo(AB_CONV * UPW)
        CV0 = lo(4 * 348)
        ab_free = AB_CONV * UPW + 4 * 348
        CO0 = lo(AB_CONV * T)
        zs, hq, hk, hf, hv, hg = (lo(HEADS * T) for _ in range(6))
        ab_lo_end = lo.free[0][0]
        B = BLOCKS * C
        g = Plan((0, ab_free), (ab_lo_end, pool_cols))
        levels = g(len(LEVELS) * CHUNKS * C, C)
        SQG = g(3 * B)
        SQ, GR = SQG[:, 0:2 * B], SQG[:, 2 * B:3 * B]
        UT, WT = SQ[:, 0:B], SQ[:, B:2 * B]
        BK, KEND, BV, VTOK = (g(BLOCKS * P, C) for _ in range(4))
        EDEC, U, QKE = (g(B, C) for _ in range(3))
        MM = g(4 * B)
        M, MT, PROD, CT = (MM[0:C, i * B:(i + 1) * B] for i in range(4))
        BR = CT
        KENDM = MM[0:C, 0:SEQS * HEADS * P]
        EGR = g(B)
        SS = g(SEQS * HEADS * P)
        OI = CO0[:, 2 * B:3 * B]
        VN = g(HEADS * C)
        S = g(HEADS * P)
        sc = g(288, C)
        k = Plan((0, ab_free), (ab_lo_end, pool_cols))
        assert k(len(LEVELS) * CHUNKS * C, C).offset == levels.offset
        ED1, CUM, ED0, EC, KE, OIH = (k(B) for _ in range(6))
        ATT = k(B, C)
        Z = [k(B), k(B)]
        SHG = k(HEADS * P)
        LB = cond[:, 0:40]
        k(RING - (ab_lo_end + 7 * B))
        KENDMH, KENDH = k(SEQS * HEADS * P, C), k(BLOCKS * P, C)
        SSH = k(SEQS * HEADS * P)
        VTOKH = k(BLOCKS * P, C)
        lo = Plan((0, RING))
        UP1 = lo(SXBC * UPW)
        CV1 = lo(4 * 348)
        ssd_free = lo.free[0][0]
        CO1 = lo(SXBC * T)
        zs1 = lo(SX * T)
        MOD1_AT = lo.free[0][0]
        MOD1 = area(MOD1_AT, 48 * MODS)
        s = Plan((0, ssd_free), (MOD1_AT + 48 * MODS, pool_cols))
        ST = s(SH * C)
        SSS = [s(SEQS * SHPG * C)]
        XDT = s(CHUNKS * SHPG * C, C)
        sc1 = s(832, C)
        EG1, CBM = s(SHPG * T, C), s(CHUNKS * C, C)
        DEC = s((PC + SEQS) * SH)
        s(RING - s.free[1][0])
        XEND = s(CHUNKS * SHPG * C, C)
        BTOK = [s(CHUNKS * P, C), s(CHUNKS * P, C)]
        BM = s(SEQS * P, C)
        SEL = s(SH * C, SH)
        G = s(T, SH)
        GS = s(SEQS * SH, C)
        ER = [s(4 * T), s(4 * T)]
        SSS.append(s(SEQS * SHPG * C))
        YI = s(4 * T)
        m = Plan((0, MOD1_AT))
        HY = m(2 * CHUNKS * D, C)
        HTOK = HY[:, 0:CHUNKS * D]
        YG = HY
        XE = [m(D), m(D)]
        XT = [m(DK * CAP), m(DK * CAP)]
        SILE = [m(FE), m(FE)]
        ACTS = [m(FE), m(FE)]
        AT = [m(FE), m(FE)]
        YE = [m(D), m(D)]
        TMP = m(BANK)
        R = m(2100, C)
        o = Plan((0, MOD1_AT - 2100))
        COMB = o(E * T)
        SIL, ACTV = o(FT * T), o(FT * T)
        YACC = o(DK * T)
        x_rows = nc.dram_tensor("x_rows", [ROWS, D], F32, kind="Internal").ap()
        y_rows = nc.dram_tensor("y_rows", [ROWS, D], F32, kind="Internal").ap()
        ZERO = area(ab_lo_end, D)

        consts_in = sem("consts_in")
        cond_in = sem("cond_in")
        x_in = sem("x_in")
        tails_in = sem("tails_in")
        conv_state_in = sem("conv_state_in")
        levels_in = sem("levels_in")
        gdn_state_in = sem("gdn_state_in")
        hgrn_state_in = sem("hgrn_state_in")
        ssd_state_in = [sem("ssd_state_in0"), sem("ssd_state_in1")]
        weights_in = [sem(f"weights_in{i}") for i in range(SLOTS)]
        weights_used = sem("weights_used")
        act_full, act_free = sem("act_full"), sem("act_free")
        dve_full, dve_free = sem("dve_full"), sem("dve_free")
        act_step, dve_step = sem("act_step"), sem("dve_step")
        ring_opens = sem("ring_opens")
        mixer_done = sem("mixer_done")
        to_act = sem("to_act")
        to_dve = sem("to_dve")
        pe_from_dve = sem("pe_from_dve")
        pe_from_act = sem("pe_from_act")
        conv_in_ready = sem("conv_in_ready")
        conv_ready = sem("conv_ready")
        conv_silu = sem("conv_silu")
        gate_silu = sem("gate_silu")
        cond_turned = sem("cond_turned")
        gate_free = sem("gate_free")
        act_ready = sem("act_ready")
        act_turned = sem("act_turned")
        xt_ready = sem("xt_ready")
        xe_turned = sem("xe_turned")
        xe_in = [sem("xe_in0"), sem("xe_in1")]
        zeroed = sem("zeroed")
        zero_made = sem("zero_made")
        h_by_token = sem("h_by_token")
        rows_ready = sem("rows_ready")
        scattered = sem("scattered")
        y_stored = [sem("y_stored0"), sem("y_stored1")]
        gathered = sem("gathered")
        out_ready = sem("out_ready")
        stored = sem("stored")
        stored_state = [sem("stored_state0"), sem("stored_state1")]
        overflow_known = sem("overflow_known")
        by_layer = lambda name: [sem(f"{name}{layer}") for layer in range(2)]
        left_ready = by_layer("left_ready")
        left_full = by_layer("left_full")
        left_banks_free = by_layer("left_banks_free")
        left_weights_in = by_layer("left_weights_in")
        left_weights_free = by_layer("left_weights_free")
        left_products = by_layer("left_products")
        left_silu = by_layer("left_silu")
        left_hidden = by_layer("left_hidden")
        left_outputs = by_layer("left_outputs")
        left_step = by_layer("left_step")

        block = ctx.enter_context(nc.Block())

        @block.sync
        def _(sp):
            n = Count()

            def load(src):
                i = n.n.get(id(weights_used), 0)
                if i >= SLOTS:
                    sp.wait_ge(weights_used, n.at(weights_used, 1 - SLOTS))
                n.up(weights_used)
                sp.dma_start(slot(i).rearrange("p (k n) -> p k n", n=src.shape[-1]), src) \
                    .then_inc(weights_in[i % SLOTS], 16)

            def load_cond(groups):
                for layer, g_ in groups:
                    load_square(a["w_ada"][layer], [g_ * BANK], DK)

            def load_square(w, cols, nk):
                wk = w.rearrange("(k p) n -> p k n", p=P)
                for c0 in cols:
                    for k0 in range(0, nk, 4):
                        load(wk[:, k0:k0 + 4, c0:c0 + BANK])

            def experts(layer):
                wg, wu, wd = a["moe_w_gate"][layer], a["moe_w_up"][layer], a["moe_w_down"][layer]

                def gate_up(e):
                    for w in (wg, wu):
                        wk = w[bass.ds(e, 1)].rearrange("o (k p) n -> p (o k) n", p=P)
                        for k0 in (0, 4):
                            load(wk[:, k0:k0 + 4, :])

                def down(e):
                    wk = wd[bass.ds(e, 1)].rearrange("o (k p) n -> p (o k) n", p=P)
                    for k0 in (0, 2):
                        load(wk[:, k0:k0 + 2, :])

                def tokens(e, b, reuse=True):
                    if reuse:
                        n.up(xe_turned)
                        sp.wait_ge(xe_turned, n.at(xe_turned))
                    sp.dma_start(XE[b], x_rows[bass.ds(e * CAP, CAP), :]).then_inc(xe_in[b], 16)

                load_cond(COND_AGAIN[layer] + COND_ROUTE[layer] + COND_MOVE[layer])
                gate_up(0)
                sp.wait_ge(scattered, 16 * 2 * CHUNKS * (layer + 1))
                tokens(0, 0, False)
                tokens(1, 1, False)
                gate_up(1)
                down(0)
                with sp.Fori(0, TURNS) as i:
                    with n.repeat(i, TURNS, {weights_used: 6 * EXPERTS_A_TURN, xe_turned: EXPERTS_A_TURN}):
                        for j in range(EXPERTS_A_TURN):
                            e = i * EXPERTS_A_TURN + (2 + j)
                            tokens(e, j % 2)
                            gate_up(e)
                            down(i * EXPERTS_A_TURN + (1 + j))
                for e in range(2 + TURNS * EXPERTS_A_TURN, E):
                    tokens(e, e % 2)
                    gate_up(e)
                    down(e - 1)
                down(E - 1)
                n.up(xe_turned, 2)
                load_cond(COND_BACK[layer])
                sp.wait_ge(overflow_known, layer + 1)
                with sp.If(sp.value_load(overflow[0:1, layer:layer + 1], min_val=0, max_val=1) > 0):
                    with sp.Fori(0, E) as e:
                        sp.wait_ge(left_weights_free[layer], e + 1)
                        for i, w in enumerate((wg, wg, wu, wu, wd, wd)):
                            wk = w[bass.ds(e, 1)].rearrange("o (k p) n -> p (o k) n", p=P)
                            nk = wk.shape[1] // 2
                            sp.dma_start(slot(i).rearrange("p (k n) -> p k n", k=nk), wk[:, i % 2 * nk:(i % 2 + 1) * nk, :]) \
                                .then_inc(left_weights_in[layer], 16)
                    sp.wait_ge(left_weights_free[layer], E + 1)

            sp.dma_start(cs[:, :].rearrange("p (k n) -> p k n", k=DK), a["c_t"].rearrange("(k p) n -> p k n", p=P)).then_inc(cond_in, 16)
            load_cond(COND_FIRST[0][:1])
            for dst, src in ((const, a["consts"]), (small, a["small"])):
                sp.dma_start(dst[:, :], src).then_inc(consts_in, 16)
            load_cond(COND_FIRST[0][1:])
            sp.dma_start(x[:, :].rearrange("p (k n) -> p k n", k=DK), a["x_t"].rearrange("(k p) n -> p k n", p=P)).then_inc(x_in, 16)
            for dst, src, k_ in ((router, a["router_w"], DK), (ab_tail, a["ab_w_in"][0][:, AB_TAIL_AT:AB_TAIL_AT + AB_TAIL], DK),
                                 (dt_tail, a["ssd_w_in"][0][:, SSD_IN - SH:SSD_IN], DK)):
                sp.dma_start(dst[:, :].rearrange("p (k n) -> p k n", k=k_), src.rearrange("(k p) n -> p k n", p=P)).then_inc(tails_in, 16)
            load_cond(COND_NORM[0])
            load_square(a["ab_w_in"][0], [0, 512, 1024, 1536] + [AB_TAIL_AT + AB_TAIL + BANK * i for i in range(4)], DK)
            for layer, w_out, nk in ((0, a["ab_w_out"][0], DK), (1, a["ssd_w_out"][0], SX)):
                if layer == 1:
                    load_cond(COND_NORM[1])
                    load_square(a["ssd_w_in"][0], [BANK * i for i in range(4, 10)] + [BANK * i for i in range(4)], DK)
                sp.wait_ge(ring_opens, layer + 1)
                if layer == 0:
                    load_cond(COND_MIXED[0][:1])
                    load_square(a["w_ada"][0][0:BANK], [COND_MIXED[0][1][1] * BANK], DK // 2)
                    sp.wait_ge(mixer_done, 1)
                    load_square(a["w_ada"][0][BANK:D], [COND_MIXED[0][1][1] * BANK], DK // 2)
                else:
                    load_cond(COND_MIXED[1])
                    sp.wait_ge(mixer_done, 2)
                load_square(w_out, (0, BANK), nk)
                experts(layer)

        @block.gpsimd
        def _(pool_eng):
            n = Count()

            def store(dst, src):
                pool_eng.wait_ge(out_ready, n.up(out_ready))
                n.up(stored, 16)
                pool_eng.dma_start(dst, src).then_inc(stored, 16)

            pool_eng.dma_start(convst[:, 0:AB_CONV * SEQS * PAD], a["gdn_conv_t"]).then_inc(conv_state_in, 16)
            pool_eng.memset(ZERO, 0.0).then_inc(zero_made, 1)
            pool_eng.wait_ge(zero_made, 1)
            pool_eng.wait_ge(conv_in_ready, 1)
            pool_eng.dma_start(x_rows[0:SPARE, :].rearrange("(i p) d -> p i d", p=P), spread(ZERO, 1, E)).then_inc(zeroed, 16)
            pool_eng.dma_start(y_rows[SPARE:ROWS, :].rearrange("(i p) d -> p i d", p=P), spread(ZERO, 1, 2 * T // P)).then_inc(zeroed, 16)

            def exchange(layer):
                rows = R[:, 1960:1960 + 2 * CHUNKS].bitcast(mybir.dt.uint32)
                pool_eng.wait_ge(rows_ready, layer + 1)
                pool_eng.wait_ge(h_by_token, layer + 1)
                for k_ in range(2):
                    for c in range(CHUNKS):
                        i = k_ * CHUNKS + c
                        pool_eng.indirect_dma_start(x_rows[:, :], bass.IndirectOffsetOnAxis(rows[:, i:i + 1], 0),
                                                    HTOK[:, c * D:(c + 1) * D], None).then_inc(scattered, 16)
                for q in range(2):
                    pool_eng.wait_ge(y_stored[q], 16 * E // 2 * (layer + 1))
                for k_ in range(2):
                    for c in range(CHUNKS):
                        i = k_ * CHUNKS + c
                        pool_eng.indirect_dma_start(YG[:, i * D:(i + 1) * D], None, y_rows[:, :],
                                                    bass.IndirectOffsetOnAxis(rows[:, i:i + 1], 0)).then_inc(gathered, 16)

            store(out["gdn_conv"], convnew[:, 0:AB_CONV * MODS * PAD])
            pool_eng.dma_start(convst[:, :], a["ssd_conv_t"]).then_inc(conv_state_in, 16)
            pool_eng.wait_ge(weights_used, N_AB)
            pool_eng.wait_ge(conv_silu, AB_CONV)
            pool_eng.dma_start(levels, a["levels"]).then_inc(levels_in, 16)
            pool_eng.dma_start(SS.rearrange("p (b n) -> p b n", b=SEQS), a["gdn_state"].rearrange("p (b n) -> p b n", b=SEQS)).then_inc(gdn_state_in, 16)
            store(out["gdn_p"], S)
            store(out["gdn_s"], SS)
            pool_eng.wait_ge(out_ready, n.up(out_ready))
            pool_eng.wait_ge(stored, n.at(stored))
            pool_eng.dma_start(SSH.rearrange("p (b n) -> p b n", b=SEQS), a["hgrn_state"].rearrange("p (b n) -> p b n", b=SEQS)).then_inc(hgrn_state_in, 16)
            store(out["hgrn_p"], SHG)
            store(out["hgrn_s"], SSH)
            pool_eng.wait_ge(stored, n.at(stored))
            exchange(0)
            store(out["ssd_conv"], convnew[:, :])
            pool_eng.wait_ge(weights_used, N_SSD)
            pool_eng.wait_ge(conv_silu, AB_CONV + SXBC)
            for gi in range(SG):
                if gi >= 2:
                    pool_eng.wait_ge(stored_state[gi % 2], 16 * (gi // 2))
                pool_eng.dma_start(SSS[gi % 2].rearrange("p (b n) -> p b n", b=SEQS),
                                   a["ssd_state"][:, :, gi * SHPG * C:(gi + 1) * SHPG * C]).then_inc(ssd_state_in[gi % 2], 16)
                if gi >= 1:
                    q = gi - 1
                    pool_eng.wait_ge(out_ready, n.up(out_ready))
                    pool_eng.dma_start(out["ssd_s"][:, :, q * SHPG * C:(q + 1) * SHPG * C],
                                       SSS[q % 2].rearrange("p (b n) -> p b n", b=SEQS)).then_inc(stored_state[q % 2], 16)
            q = SG - 1
            pool_eng.wait_ge(out_ready, n.up(out_ready))
            pool_eng.dma_start(out["ssd_s"][:, :, q * SHPG * C:(q + 1) * SHPG * C],
                               SSS[q % 2].rearrange("p (b n) -> p b n", b=SEQS)).then_inc(stored_state[q % 2], 16)
            store(out["ssd_p"], ST)
            exchange(1)
            store(out["y"].rearrange("(k p) n -> p k n", p=P), h[:, :].rearrange("p (k n) -> p k n", k=DK))
            pool_eng.wait_ge(stored, n.at(stored))
            for i in range(2):
                pool_eng.wait_ge(stored_state[i], 16 * SG // 2)

        @block.tensor
        def _(pe):
            n = Count()

            def bank_for_act():
                i = n.n.get(id(act_full), 0)
                if i >= BANKS:
                    pe.wait_ge(act_free, n.at(act_full, 1 - BANKS))
                n.up(act_full)
                return psum[i % BANKS]

            def bank_for_dve():
                i = n.n.get(id(dve_full), 0)
                if i >= BANKS:
                    pe.wait_ge(dve_free, n.at(dve_full, 1 - BANKS))
                n.up(dve_full)
                return psum[BANKS + i % BANKS]

            def slot_read(full):
                pe.wait_ge(full, n.at(full))
                pe.sem_inc(weights_used, 1)

            def next_slot():
                i = n.n.get(id(weights_used), 0)
                n.up(weights_used)
                n.up(weights_in[i % SLOTS], 16)
                pe.wait_ge(weights_in[i % SLOTS], n.at(weights_in[i % SLOTS]))
                return slot(i)

            def from_dve():
                pe.wait_ge(pe_from_dve, n.up(pe_from_dve))

            def from_act():
                pe.wait_ge(pe_from_act, n.up(pe_from_act))

            def projections(rhs, nk, groups, bank, full):
                for _g in range(groups):
                    ws = [next_slot().rearrange("p (k n) -> p k n", n=BANK) for _ in range(nk // 4)]
                    for mt in range(4):
                        b = bank()
                        for kk in range(nk):
                            mm = pe.matmul(b[:, 0:T], ws[kk // 4][:, kk % 4, mt * P:(mt + 1) * P],
                                           rhs[:, kk * T:(kk + 1) * T], start=(kk == 0), stop=(kk == nk - 1))
                            if mt == 3 and kk % 4 == 3 and kk < nk - 1:
                                mm.then_inc(weights_used, 1)
                        mm.then_inc(full, 1)
                    slot_read(full)

            def conditioning(groups):
                def turn(at):
                    from_act()
                    b = bank_for_dve()
                    for mt in range(4):
                        mm = pe.transpose(b[:, mt * MODS:(mt + 1) * MODS], cond[0:MODS, at * BANK + mt * P:at * BANK + (mt + 1) * P],
                                          ident[0:MODS, 0:MODS])
                    mm.then_inc(dve_full, 1)

                for i in range(len(groups)):
                    at = n.n.get(id(cond_turned), 0) % 2
                    n.up(cond_turned)
                    b = bank_for_act()
                    for k0 in (0, 4):
                        w = next_slot().rearrange("p (k n) -> p k n", n=BANK)
                        for kk in range(4):
                            mm = pe.matmul(b[0:MODS, :], cs[:, (k0 + kk) * MODS:(k0 + kk + 1) * MODS], w[:, kk, :],
                                           start=(k0 + kk == 0), stop=(k0 + kk == DK - 1))
                        if k0 == 0:
                            mm.then_inc(weights_used, 1)
                    mm.then_inc(act_full, 1)
                    slot_read(act_full)
                    if i:
                        turn(1 - at)
                if groups:
                    turn(at)

            def norm_sum():
                from_act()
                b = bank_for_act()
                for kk in range(DK):
                    mm = pe.matmul(b[:, 0:T], ones, h[:, kk * T:(kk + 1) * T], start=(kk == 0), stop=(kk == DK - 1))
                mm.then_inc(act_full, 1)

            def token_scalars(tail, width):
                b = bank_for_dve()
                for c in range(CHUNKS):
                    for kk in range(DK):
                        mm = pe.matmul(b[0:C, c * width:(c + 1) * width], h[:, kk * T + c * C:kk * T + (c + 1) * C],
                                       tail[:, kk * width:(kk + 1) * width], start=(kk == 0), stop=(kk == DK - 1))
                mm.then_inc(dve_full, 1)

            def decay_sums(gt, nh):
                gp = gt.rearrange("p (h c) -> p h c", c=CHUNKS)
                b = bank_for_dve()
                np_, ns_ = nh * PC, nh
                pe.matmul(b[0:C, 0:np_], incl_p, gp[:, :, 0:PC], start=True, stop=True)
                pe.matmul(b[0:C, np_:np_ + ns_], incl_s, gp[:, :, PC], start=True, stop=True)
                o = np_ + ns_
                pe.matmul(b[0:C, o:o + np_], after_p, gp[:, :, 0:PC], start=True, stop=True)
                pe.matmul(b[0:C, o + np_:o + np_ + ns_], after_s, gp[:, :, PC], start=True, stop=True).then_inc(dve_full, 1)

            def blocks(bank, full, lhs, rhs, count, parts, width):
                per = BANK // width
                for i0 in range(0, count, per):
                    b = bank()
                    for i in range(i0, min(i0 + per, count)):
                        mm = pe.matmul(b[0:parts, (i - i0) * width:(i - i0 + 1) * width], lhs(i), rhs(i), start=True, stop=True)
                    mm.then_inc(full, 1)

            def turned(bank, full, src, count):
                for i0 in range(0, count, 4):
                    b = bank()
                    for i in range(i0, min(i0 + 4, count)):
                        mm = pe.transpose(b[0:C, (i - i0) * P:(i - i0 + 1) * P], src(i), ident)
                    mm.then_inc(full, 1)

            def c64(buf):
                return lambda i: buf[:, i * C:(i + 1) * C]

            def c128(buf):
                return lambda i: buf[:, i * P:(i + 1) * P]

            def head_norm_sum(sq, count):
                for i0 in range(0, count, 4):
                    b = bank_for_act()
                    for i in range(4):
                        mm = pe.matmul(b[32 * i:32 * i + 32, 0:T], ones[:, 0:32], sq[:, (i0 + i) * T:(i0 + i + 1) * T], start=True, stop=True)
                    mm.then_inc(act_full, 1)

            def head_norms(norms, count):
                from_dve()
                for i in range(count):
                    b = bank_for_dve()
                    r = slice(32 * (i % 4), 32 * (i % 4) + 1)
                    pe.matmul(b[:, 0:T], ones[r, :], norms[r, i // 4 * T:(i // 4 + 1) * T], start=True, stop=True).then_inc(dve_full, 1)

            def read_state(b, at, st, q, cols):
                n_ = cols.stop - cols.start
                if q.shape[-1] == B:
                    return pe.matmul(b[:, at:at + n_], st, q[:, cols], start=True, stop=True)
                both = q.rearrange("p (two n) -> p two n", two=2)[:, :, cols]
                out2 = b[:, 0:2 * HEADS * C].rearrange("p (two n) -> p two n", two=2)[:, :, at:at + n_]
                return pe.matmul(out2, st, both, start=True, stop=True)

            def state_chunk(Sx, QG, c):
                b = bank_for_dve()
                for hh in range(HEADS):
                    st = Sx[:, hh * P:(hh + 1) * P]
                    cols = slice(hh * T + c * C, hh * T + (c + 1) * C)
                    mm = read_state(b, hh * C, st, QG, cols)
                mm.then_inc(dve_full, 1)

            def state_samples(b, SSx, QG, seqs=range(SEQS)):
                for s_ in seqs:
                    for hh in range(HEADS):
                        st = SSx[:, (s_ * HEADS + hh) * P:(s_ * HEADS + hh + 1) * P]
                        cols = slice(hh * T + PROMPT + s_ * SEQ_LEN, hh * T + PROMPT + (s_ + 1) * SEQ_LEN)
                        o = hh * C + s_ * SEQ_LEN
                        mm = read_state(b, o, st, QG, cols)
                return mm

            def update_chunk(kend, vtok, c):
                b = bank_for_dve()
                for hh in range(HEADS):
                    i = hh * CHUNKS + c
                    mm = pe.matmul(b[:, hh * P:(hh + 1) * P], kend[:, i * P:(i + 1) * P], vtok[:, i * P:(i + 1) * P], start=True, stop=True)
                mm.then_inc(dve_full, 1)

            def update_samples(kendm, vtok):
                for s_ in range(SEQS):
                    b = bank_for_dve()
                    for hh in range(HEADS):
                        i = hh * CHUNKS + PC
                        j = s_ * HEADS + hh
                        mm = pe.matmul(b[:, hh * P:(hh + 1) * P], kendm[:, j * P:(j + 1) * P], vtok[:, i * P:(i + 1) * P], start=True, stop=True)
                    mm.then_inc(dve_full, 1)

            def gdn():
                QT, KT, VT = CO0[:, 0:B], CO0[:, B:2 * B], CO0[:, 2 * B:3 * B]
                token_scalars(ab_tail, AB_TAIL)
                projections(h, DK, 8, bank_for_act, act_full)
                from_dve()
                decay_sums(sc[:, 0:BLOCKS], HEADS)
                from_dve()
                for i0 in range(0, B, BANK):
                    b = bank_for_dve()
                    w = min(BANK, B - i0)
                    pe.matmul(b[:, 0:w], ones64, EDEC[:, i0:i0 + w], start=True, stop=True).then_inc(dve_full, 1)
                for i0 in range(0, B, BANK):
                    b = bank_for_dve()
                    w = min(BANK, B - i0)
                    pe.matmul(b[0:C, 0:w], ones64[:, 0:C], U[:, i0:i0 + w], start=True, stop=True).then_inc(dve_full, 1)
                from_act()
                head_norm_sum(SQ, 2 * HEADS)
                head_norms(SQ, 2 * HEADS)
                from_dve()
                blocks(bank_for_dve, dve_full, c64(KT), c64(KT), BLOCKS, C, C)
                blocks(bank_for_dve, dve_full, c64(KT), c64(QT), BLOCKS, C, C)
                turned(bank_for_dve, dve_full, c64(KT), BLOCKS)
                turned(bank_for_dve, dve_full, c64(VT), BLOCKS)
                for lv in range(len(LEVELS)):
                    ct, mt = (CT, MT) if lv % 2 == 0 else (MT, CT)
                    from_dve()
                    if lv == 0:
                        blocks(bank_for_dve, dve_full, c64(ct), c64(M), BLOCKS, C, C)
                        continue
                    blocks(bank_for_act, act_full, c64(ct), c64(M), BLOCKS, C, C)
                    from_act()
                    blocks(bank_for_dve, dve_full, c64(PROD), c64(mt), BLOCKS, C, C)
                    if lv < len(LEVELS) - 1:
                        blocks(bank_for_dve, dve_full, c64(mt), c64(PROD), BLOCKS, C, C)
                from_dve()
                blocks(bank_for_act, act_full, c128(BV), c64(MT), BLOCKS, P, C)
                blocks(bank_for_act, act_full, c128(BK), c64(MT), BLOCKS, P, C)
                from_act()
                from_dve()
                for c in range(PC):
                    if c:
                        from_dve()
                    state_chunk(S, SQG[:, B:3 * B], c)
                    from_dve()
                    b = bank_for_act()
                    for hh in range(HEADS):
                        mm = pe.transpose(b[0:C, hh * P:(hh + 1) * P], VN[:, hh * C:(hh + 1) * C], ident)
                    mm.then_inc(act_full, 1)
                    from_act()
                    update_chunk(KEND, VTOK, c)
                pe.wait_ge(gdn_state_in, 16)
                state_samples(bank_for_dve(), SS, SQG[:, B:3 * B]).then_inc(dve_full, 1)
                from_dve()
                b = bank_for_act()
                for hh in range(HEADS):
                    mm = pe.transpose(b[0:C, hh * P:(hh + 1) * P], VN[:, hh * C:(hh + 1) * C], ident)
                mm.then_inc(act_full, 1)
                from_act()
                from_dve()
                update_samples(KENDM, VTOK)
                blocks(bank_for_dve, dve_full, c128(VTOK), c64(QKE), BLOCKS, P, C)
                from_act()
                head_norm_sum(SQ, HEADS)
                head_norms(SQ[:, B:2 * B], HEADS)

            def hgrn():
                blocks(bank_for_dve, dve_full, c64(hk), c64(hq), BLOCKS, C, C)
                for lv, half in enumerate(LEVELS):
                    from_dve()
                    zz = Z[lv % 2]
                    cs_ = [i for i in range(BLOCKS) if half < SEQ_LEN or i % CHUNKS < PC]
                    per = BANK // C
                    for i0 in range(0, BLOCKS, per):
                        b = bank_for_dve()
                        for i in range(i0, min(i0 + per, BLOCKS)):
                            if i in cs_:
                                mm = pe.matmul(b[0:C, (i - i0) * C:(i - i0 + 1) * C], zz[:, i * C:(i + 1) * C], zz[:, i * C:(i + 1) * C], start=True, stop=True)
                        mm.then_inc(dve_full, 1)
                from_dve()
                turned(bank_for_act, act_full, c64(KE), BLOCKS)
                turned(bank_for_act, act_full, c64(hv), BLOCKS)
                from_act()
                from_dve()
                pe.wait_ge(hgrn_state_in, 16)
                reads = bank_for_act()
                for c in range(PC):
                    if c:
                        from_dve()
                    state_chunk(SHG, ED0, c)
                    update_chunk(KENDH, VTOKH, c)
                    mm = state_samples(reads, SSH, ED0, range(c * SEQS // PC, (c + 1) * SEQS // PC))
                mm.then_inc(act_full, 1)
                from_dve()
                update_samples(KENDMH, VTOKH)
                blocks(bank_for_dve, dve_full, c128(VTOKH), c64(ATT), BLOCKS, P, C)
                from_act()
                head_norm_sum(Z[0], HEADS)
                head_norms(Z[1], HEADS)

            def ssd():
                token_scalars(dt_tail, SH)
                projections(h, DK, 10, bank_for_act, act_full)
                from_dve()
                gl = sc1[:, 0:SH * CHUNKS].rearrange("p (h c) -> p h c", c=CHUNKS)
                decay_sums(sc1[:, 0:SH * CHUNKS], SH)
                b = bank_for_dve()
                for c in range(CHUNKS):
                    mm = pe.matmul(b[0:SH, c * C:(c + 1) * C], gl[:, :, c], incl_p if c < PC else incl_s, start=True, stop=True)
                mm.then_inc(dve_full, 1)
                from_dve()
                b = bank_for_dve()
                pe.matmul(b[:, 0:PC * SH], ones64, gl.rearrange("p h c -> p c h")[:, 0:PC, :], start=True, stop=True)
                pe.matmul(b[:, PC * SH:(PC + SEQS) * SH], ones64, GS, start=True, stop=True).then_inc(dve_full, 1)
                from_act()

                def norm_of_group(gi):
                    from_act()
                    b = bank_for_act()
                    for j in range(4):
                        mm = pe.matmul(b[:, 0:T], ones, zs1[:, (4 * gi + j) * T:(4 * gi + j + 1) * T], start=(j == 0), stop=(j == 3))
                    mm.then_inc(act_full, 1)

                for gi in range(SG):
                    Bf = CO1[:, (SX + gi) * T:(SX + gi + 1) * T]
                    Cf = CO1[:, (SX + SG + gi) * T:(SX + SG + gi + 1) * T]
                    btok, states = BTOK[gi % 2], SSS[gi % 2]
                    blocks(bank_for_dve, dve_full, c64(Bf), c64(Cf), CHUNKS, C, C)
                    turned(bank_for_act, act_full, c64(Bf), CHUNKS)
                    for j in range(4):
                        at = (gi * SHPG + 2 * j) * C
                        b = bank_for_act()
                        pe.matmul(b[:, 0:T], SEL[:, at:at + 2 * C], G, start=True, stop=True).then_inc(act_full, 1)
                    for hh in range(SHPG):
                        b = bank_for_dve()
                        pe.matmul(b[0:C, 0:T], SEL[:, (gi * SHPG + hh) * C:(gi * SHPG + hh + 1) * C], G,
                                  start=True, stop=True).then_inc(dve_full, 1)
                    for c in range(CHUNKS):
                        b = bank_for_dve()
                        for j in range(4):
                            mm = pe.transpose(b[0:C, j * P:(j + 1) * P], CO1[:, (4 * gi + j) * T + c * C:(4 * gi + j) * T + (c + 1) * C], ident)
                        mm.then_inc(dve_full, 1)
                    from_act()
                    if gi:
                        norm_of_group(gi - 1)
                    pe.wait_ge(ssd_state_in[gi % 2], 16 * (gi // 2 + 1))
                    reads = bank_for_act()
                    for c in range(PC):
                        from_dve()
                        b = bank_for_dve()
                        for j in range(4):
                            mm = pe.matmul(b[:, j * C:(j + 1) * C], ST[:, (4 * gi + j) * P:(4 * gi + j + 1) * P], Cf[:, c * C:(c + 1) * C], start=True, stop=True)
                        mm.then_inc(dve_full, 1)
                        b = bank_for_dve()
                        pe.matmul(b[:, :], btok[:, c * P:(c + 1) * P], XEND[:, c * BANK:(c + 1) * BANK], start=True, stop=True).then_inc(dve_full, 1)
                        for s_ in range(c * SEQS // PC, (c + 1) * SEQS // PC):
                            for j in range(4):
                                o = j * C + s_ * SEQ_LEN
                                mm = pe.matmul(reads[:, o:o + SEQ_LEN], states[:, s_ * BANK + j * P:s_ * BANK + (j + 1) * P],
                                               Cf[:, PROMPT + s_ * SEQ_LEN:PROMPT + (s_ + 1) * SEQ_LEN], start=True, stop=True)
                    mm.then_inc(act_full, 1)
                    for s_ in range(SEQS):
                        b = bank_for_dve()
                        pe.matmul(b[:, :], BM[:, s_ * P:(s_ + 1) * P], XEND[:, PC * BANK:CHUNKS * BANK], start=True, stop=True).then_inc(dve_full, 1)
                    from_dve()
                    for j in range(4):
                        b = bank_for_dve()
                        for c in range(CHUNKS):
                            for o in range(2):
                                hh = 2 * j + o
                                mm = pe.matmul(b[o * C:(o + 1) * C, c * C:(c + 1) * C], XDT[:, c * BANK + hh * C:c * BANK + (hh + 1) * C],
                                               EG1[:, (hh * CHUNKS + c) * C:(hh * CHUNKS + c + 1) * C], start=True, stop=True)
                        mm.then_inc(dve_full, 1)
                norm_of_group(SG - 1)

            def experts(layer):
                token_scalars(router, E)
                for c in range(CHUNKS):
                    for k0 in (0, 4):
                        b = bank_for_act()
                        for kk in range(k0, k0 + 4):
                            mm = pe.transpose(b[0:C, (kk - k0) * P:(kk - k0 + 1) * P], h[:, kk * T + c * C:kk * T + (c + 1) * C], ident)
                        mm.then_inc(act_full, 1)
                conditioning(COND_ROUTE[layer])
                from_dve()
                chosen = R[:, 1200:1280]
                b = bank_for_dve()
                for c in range(CHUNKS):
                    pe.matmul(b[0:C, 0:E], ones64[:, 0:C], chosen[:, c * E:(c + 1) * E], start=(c == 0), stop=(c == CHUNKS - 1))
                pe.matmul(b[0:C, E:E + CHUNKS * E], incl_p, chosen, start=True, stop=False)
                for c in range(CHUNKS - 1):
                    later = CHUNKS - 1 - c
                    mm = pe.matmul(b[0:C, E + (c + 1) * E:E + CHUNKS * E], ones64[:, 0:C], spread(chosen[:, c * E:(c + 1) * E], 1, later),
                                   start=False, stop=(c == CHUNKS - 2))
                mm.then_inc(dve_full, 1)

                def turn_tokens(q):
                    n.up(xe_in[q], 16)
                    pe.wait_ge(xe_in[q], n.at(xe_in[q]))
                    for k0 in (0, 4):
                        b = bank_for_act()
                        for kk in range(k0, k0 + 4):
                            mm = pe.transpose(b[:, (kk - k0) * P:(kk - k0 + 1) * P], XE[q][:, kk * P:(kk + 1) * P], ident)
                        mm.then_inc(act_full, 1)
                    pe.wait_ge(act_full, n.at(act_full))
                    pe.sem_inc(xe_turned, 1)

                def product(b, lhs, nk, ws, per, col, full):
                    for kk in range(nk):
                        mm = pe.matmul(b[:, :], lhs[:, kk * CAP:(kk + 1) * CAP], ws[kk // per][:, kk % per, col:col + BANK],
                                       start=(kk == 0), stop=(kk == nk - 1))
                        if kk == per - 1 and kk < nk - 1 and col + BANK == ws[0].shape[-1]:
                            mm.then_inc(weights_used, 1)
                    mm.then_inc(full, 1)

                def wide(ws_cols):
                    return [next_slot().rearrange("p (k n) -> p k n", n=ws_cols) for _ in range(2)]

                def gate(q):
                    pe.wait_ge(xt_ready, n.up(xt_ready))
                    product(bank_for_act(), XT[q], DK, wide(BANK), 4, 0, act_full)
                    slot_read(act_full)

                def up(q):
                    product(bank_for_dve(), XT[q], DK, wide(BANK), 4, 0, dve_full)
                    slot_read(dve_full)

                def turn_hidden(q):
                    pe.wait_ge(act_ready, n.up(act_ready))
                    b = bank_for_dve()
                    for f in range(FT):
                        mm = pe.transpose(b[:, f * CAP:(f + 1) * CAP], ACTS[q][:, f * P:(f + 1) * P], ident)
                    mm.then_inc(dve_full, 1)

                def down(q):
                    ws = wide(D)
                    pe.wait_ge(act_turned, n.up(act_turned))
                    for col in (0, BANK):
                        product(bank_for_act(), AT[q], FT, ws, 2, col, act_full)
                    slot_read(act_full)

                def expert(q, more=True):
                    gate(q)
                    turn_hidden(1 - q)
                    up(q)
                    if more:
                        turn_tokens(1 - q)
                    down(1 - q)

                conditioning(COND_MOVE[layer])
                turn_tokens(0)
                gate(0)
                up(0)
                turn_tokens(1)
                with pe.Fori(0, TURNS) as i:
                    per = {act_full: 5 * EXPERTS_A_TURN, dve_full: 2 * EXPERTS_A_TURN, weights_used: 6 * EXPERTS_A_TURN}
                    per |= {s_: EXPERTS_A_TURN for s_ in (act_ready, act_turned, xt_ready)}
                    per |= {w: 16 * 6 * EXPERTS_A_TURN // SLOTS for w in weights_in}
                    per |= {w: 16 * EXPERTS_A_TURN // 2 for w in xe_in}
                    with n.repeat(i, TURNS, per):
                        for j in range(EXPERTS_A_TURN):
                            expert((1 + j) % 2)
                for e in range(1 + TURNS * EXPERTS_A_TURN, E):
                    expert(e % 2, e < E - 1)
                turn_hidden((E - 1) % 2)
                down((E - 1) % 2)
                conditioning(COND_BACK[layer])
                for c in range(CHUNKS):
                    from_dve()
                    b = bank_for_dve()
                    for kk in range(DK):
                        mm = pe.transpose(b[:, kk * C:(kk + 1) * C], YG[:, c * D + kk * P:c * D + (kk + 1) * P], ident64)
                    mm.then_inc(dve_full, 1)
                pe.wait_ge(overflow_known, layer + 1)
                with pe.If(pe.value_load(overflow[0:1, layer:layer + 1], min_val=0, max_val=1) > 0):
                    overflow_pass(layer)

            def overflow_pass(layer):
                pe.wait_ge(act_free, n.at(act_full))
                pe.wait_ge(dve_free, n.at(dve_full))
                pe.sem_inc(left_weights_free[layer], 1)
                pe.wait_ge(left_ready[layer], 1)
                for e in range(E):
                    if e == 2 * BANKS:
                        pe.wait_ge(left_banks_free[layer], 1)
                    for c in range(CHUNKS):
                        mm = pe.matmul(psum[e % (2 * BANKS)][:, c * C:(c + 1) * C],
                                       R[:, e * CHUNKS + c:e * CHUNKS + c + 1].to_broadcast([C, P]), ident64, start=True, stop=True)
                    mm.then_inc(left_full[layer], 1)
                with pe.Fori(0, E) as e:
                    pe.wait_ge(left_weights_in[layer], e * 96 + 96)
                    pe.wait_ge(left_banks_free[layer], e + 2)
                    gw, uw, dw = ([slot(2 * i + j).rearrange("p (k n) -> p k n", n=cols) for j in range(2)]
                                  for i, cols in enumerate((BANK, BANK, D)))
                    for f in range(FT):
                        for b, ws in ((psum[f], gw), (psum[BANKS + f], uw)):
                            for kk in range(DK):
                                mm = pe.matmul(b[:, 0:T], ws[kk // 4][:, kk % 4, f * P:(f + 1) * P], h[:, kk * T:(kk + 1) * T],
                                               start=(kk == 0), stop=(kk == DK - 1))
                    mm.then_inc(left_products[layer], 1)
                    pe.wait_ge(left_hidden[layer], e + 1)
                    for dt_ in range(DK):
                        for f in range(FT):
                            mm = pe.matmul(psum[dt_][:, 0:T], dw[f // 2][:, f % 2, dt_ * P:(dt_ + 1) * P], ACTV[:, f * T:(f + 1) * T],
                                           start=(f == 0), stop=(f == FT - 1))
                    mm.then_inc(left_outputs[layer], 1)
                    pe.wait_ge(left_outputs[layer], e + 1)
                    pe.sem_inc(left_weights_free[layer], 1)
                pe.wait_ge(left_banks_free[layer], E + 2)

            pe.wait_ge(consts_in, 32)
            from_act()
            for layer in range(2):
                conditioning(COND_FIRST[layer])
                if layer == 0:
                    pe.wait_ge(tails_in, 48)
                norm_sum()
                conditioning(COND_NORM[layer])
                from_dve()
                if layer == 0:
                    gdn()
                    hgrn()
                else:
                    ssd()
                conditioning(COND_MIXED[layer])
                from_dve()
                projections(h if layer == 0 else CO1, DK if layer == 0 else SX, 2, bank_for_dve, dve_full)
                norm_sum()
                conditioning(COND_AGAIN[layer])
                from_dve()
                experts(layer)
            norm_sum()

        @block.scalar
        def _(act):
            n = Count()

            def bank():
                i = n.n.get(id(act_full), 0)
                n.up(act_full)
                act.wait_ge(act_full, n.at(act_full))
                return psum[i % BANKS]

            def from_dve():
                act.wait_ge(to_act, n.up(to_act))

            def step(ins):
                ins.then_inc(act_step, 1)
                act.wait_ge(act_step, n.up(act_step))

            def tell(what):
                act.sem_inc(what, 1)

            def banks_read():
                act.wait_ge(act_free, n.at(act_full))

            def squares(dst, src):
                from_dve()
                act.activation(dst, src, ACT.Square).then_inc(pe_from_act, 1)

            def conditioning(groups):
                for _ in groups:
                    b = bank()
                    i = n.n.get(id(cond_turned), 0)
                    n.up(cond_turned)
                    if i >= 2:
                        act.wait_ge(cond_turned, i - 1)
                    act.activation(cond[0:MODS, (i % 2) * BANK:(i % 2 + 1) * BANK], b[0:MODS, :], ACT.Copy).then_inc(act_free, 1)
                    banks_read()
                    tell(pe_from_act)

            def root(scale):
                b = bank()
                act.activation(rs[:, :], b[:, 0:T], ACT.Sqrt, scale=scale, bias=eps).then_inc(act_free, 1)
                act.wait_ge(act_free, n.at(act_full))
                tell(to_dve)

            def softplus(e1, l1, a_exp, a_log, beta=None):
                from_dve()
                if beta is not None:
                    act.activation(beta, beta, ACT.Exp, scale=-1.0)
                act.activation(a_exp, a_log, ACT.Exp)
                step(act.activation(e1, e1, ACT.Exp))
                act.activation(l1, e1, ACT.Ln, bias=one_col[0:C, :]).then_inc(to_dve, 1)

            def conv_inputs(UP, CV, CO, tiles, bias):
                done = 0

                def silus(upto):
                    nonlocal done
                    while done < upto:
                        act.wait_ge(conv_ready, n.up(conv_ready))
                        cv = CV[:, (done % 4) * 348:(done % 4) * 348 + 347]
                        bb = {} if bias is None else {"bias": bias[:, done:done + 1]}
                        act.activation(CO[:, done * T:done * T + PROMPT], cv[:, 0:PROMPT], ACT.Silu, **bb)
                        act.activation(CO[:, done * T + PROMPT:(done + 1) * T].rearrange("p (b l) -> p b l", l=SEQ_LEN),
                                       cv[:, PAD + PROMPT:].rearrange("p (b l) -> p b l", l=PAD + SEQ_LEN)[:, :, 0:SEQ_LEN],
                                       ACT.Silu, **bb).then_inc(conv_silu, 1)
                        done += 1

                for f in range(tiles):
                    b = bank()
                    up = UP[:, f * UPW:(f + 1) * UPW]
                    act.activation(up[:, PAD:PAD + PROMPT], b[:, 0:PROMPT], ACT.Copy)
                    act.activation(up[:, PAD + PROMPT:].rearrange("p (b l) -> p b l", l=PAD + SEQ_LEN)[:, :, PAD:],
                                   b[:, PROMPT:T].rearrange("p (b l) -> p b l", l=SEQ_LEN), ACT.Copy).then_inc(act_free, 1)
                    banks_read()
                    tell(conv_in_ready)
                    silus(f - 1)
                silus(tiles)

            def copies(dst, parts, width, banks, last):
                total = dst.shape[-1]
                for i in range(banks):
                    w = min(width, total - i * width)
                    b = bank()
                    act.activation(dst[:, i * width:i * width + w], b[0:parts, 0:w], ACT.Copy).then_inc(act_free, 1)
                act.wait_ge(act_free, n.at(act_full))
                if last:
                    tell(pe_from_act)

            def gdn():
                conv_inputs(UP0, CV0, CO0, AB_CONV, None)
                for i in range(4):
                    b = bank()
                    act.activation(zs[:, i * T:(i + 1) * T], b[:, 0:T], ACT.Silu).then_inc(act_free, 1)
                for i in range(4):
                    b = bank()
                    act.activation(hq[:, i * T:(i + 1) * T], b[:, 0:T], ACT.Copy, scale=float(P) ** -0.5).then_inc(act_free, 1)
                for i in range(4):
                    b = bank()
                    act.activation(hf[:, i * T:(i + 1) * T], b[:, 0:T], ACT.Sigmoid)
                    act.activation(hk[:, i * T:(i + 1) * T], b[:, 0:T], ACT.Sigmoid, scale=-1.0).then_inc(act_free, 1)
                for i in range(4):
                    b = bank()
                    act.activation(hv[:, i * T:(i + 1) * T], b[:, 0:T], ACT.Copy).then_inc(act_free, 1)
                for i in range(4):
                    b = bank()
                    act.activation(hg[:, i * T:(i + 1) * T], b[:, 0:T], ACT.Silu).then_inc(act_free, 1)
                softplus(sc[:, 60:80], sc[:, 80:100], sc[:, 100:104], W("gdn_a_log")[0:C, :], sc[:, 200:220])
                from_dve()
                act.activation(sc[:, 160:200], sc[:, 120:160], ACT.Exp).then_inc(to_dve, 1)
                from_dve()
                act.activation(EDEC, EDEC, ACT.Exp)
                act.activation(EGR, GR, ACT.Exp).then_inc(to_dve, 1)
                act.wait_ge(conv_silu, AB_CONV)
                act.wait_ge(weights_used, N_AB)
                act.wait_ge(zeroed, 32)
                act.activation(SQ, CO0[:, 0:2 * B], ACT.Square).then_inc(pe_from_act, 1)
                for i in range(2 * HEADS // 4):
                    b = bank()
                    act.activation(SQ[:, i * T:(i + 1) * T], b[:, 0:T], ACT.Sqrt, bias=eps).then_inc(act_free, 1)
                act.wait_ge(act_free, n.at(act_full))
                tell(to_dve)
                for lv in range(1, len(LEVELS)):
                    copies(PROD, C, BANK, 3, True)
                from_dve()
                act.activation(LB[:, 0:12], LB[:, 0:12], ACT.Exp).then_inc(to_dve, 1)
                copies(UT, P, BANK, 3, False)
                copies(WT, P, BANK, 3, True)
                tell(to_dve)
                from_dve()
                act.activation(hf, hf, ACT.Ln)
                for c in range(CHUNKS):
                    b = bank()
                    v = VTOK.rearrange("p (h c n) -> p h c n", h=HEADS, c=CHUNKS)[:, :, c, :]
                    act.activation(v, b[0:C, :].rearrange("p (h n) -> p h n", h=HEADS), ACT.Copy).then_inc(act_free, 1)
                    act.wait_ge(act_free, n.at(act_full))
                    tell(pe_from_act)
                squares(SQ[:, 0:B], OI)
                for i in range(HEADS // 4):
                    b = bank()
                    act.activation(SQ[:, B + i * T:B + (i + 1) * T], b[:, 0:T], ACT.Sqrt, scale=1.0 / P, bias=eps).then_inc(act_free, 1)
                act.wait_ge(act_free, n.at(act_full))
                tell(to_dve)

            def hgrn():
                for lv, half in enumerate(LEVELS):
                    ed = (ED0, ED1)[lv % 2]
                    from_dve()
                    act.activation(ed, ed, ACT.Exp).then_inc(to_dve, 1)
                from_dve()
                act.activation(KE, KE, ACT.Exp)
                act.activation(EC, CUM, ACT.Exp).then_inc(to_dve, 1)
                copies(KENDH, C, BANK, 5, False)
                copies(VTOKH, C, BANK, 5, True)
                tell(to_dve)
                b = bank()
                act.activation(OIH.rearrange("p (h t) -> p h t", h=HEADS)[:, :, PROMPT:T], b[:, 0:HEADS * C].rearrange("p (h t) -> p h t", h=HEADS), ACT.Copy) \
                    .then_inc(act_free, 1)
                banks_read()
                tell(to_dve)
                squares(Z[0], OIH)
                for i in range(HEADS // 4):
                    b = bank()
                    act.activation(Z[1][:, i * T:(i + 1) * T], b[:, 0:T], ACT.Sqrt, scale=1.0 / P, bias=eps).then_inc(act_free, 1)
                act.wait_ge(act_free, n.at(act_full))
                tell(to_dve)

            def ssd():
                conv_inputs(UP1, CV1, CO1, SXBC, W("ssd_conv_b"))
                for i in range(SX):
                    b = bank()
                    act.activation(zs1[:, i * T:(i + 1) * T], b[:, 0:T], ACT.Silu).then_inc(act_free, 1)
                n5 = SH * CHUNKS
                softplus(sc1[:, 2 * n5:3 * n5], sc1[:, 3 * n5:4 * n5], sc1[:, 5 * n5:5 * n5 + SH], W("ssd_a_log")[0:C, :])
                from_dve()
                act.activation(sc1[:, 3 * n5:4 * n5], sc1[:, 3 * n5:4 * n5], ACT.Exp).then_inc(to_dve, 1)
                from_dve()
                act.activation(DEC, DEC, ACT.Exp).then_inc(to_dve, 1)
                act.wait_ge(conv_silu, AB_CONV + SXBC)
                tell(pe_from_act)

                def norm_of_group(gi):
                    squares(zs1[:, 4 * gi * T:4 * (gi + 1) * T], CO1[:, 4 * gi * T:4 * (gi + 1) * T])
                    root(1.0 / BANK)

                for gi in range(SG):
                    btok, er = BTOK[gi % 2], ER[gi % 2]
                    for i in range(2):
                        w = BANK if i == 0 else P
                        b = bank()
                        act.activation(btok[:, i * BANK:i * BANK + w], b[0:C, 0:w], ACT.Copy).then_inc(act_free, 1)
                    for j in range(4):
                        b = bank()
                        act.activation(er[:, j * T:(j + 1) * T], b[:, 0:T], ACT.Exp).then_inc(act_free, 1)
                    banks_read()
                    tell(pe_from_act)
                    tell(to_dve)
                    if gi:
                        norm_of_group(gi - 1)
                    from_dve()
                    act.activation(EG1, EG1, ACT.Exp).then_inc(to_dve, 1)
                    b = bank()
                    act.activation(YI.rearrange("p (j t) -> p j t", j=4)[:, :, PROMPT:T], b[:, 0:4 * C].rearrange("p (j t) -> p j t", j=4), ACT.Copy) \
                        .then_inc(act_free, 1)
                    banks_read()
                    tell(to_dve)
                norm_of_group(SG - 1)

            def experts(layer):
                for i in range(2 * CHUNKS):
                    b = bank()
                    act.activation(HTOK[:, i * BANK:(i + 1) * BANK], b[0:C, :], ACT.Copy).then_inc(act_free, 1)
                banks_read()
                tell(h_by_token)
                from_dve()
                act.activation(R[:, 100:180], R[:, 100:180], ACT.Sigmoid).then_inc(to_dve, 1)
                conditioning(COND_ROUTE[layer] + COND_MOVE[layer])

                def tokens(q):
                    for i in range(2):
                        b = bank()
                        act.activation(XT[q][:, i * BANK:(i + 1) * BANK], b[:, :], ACT.Copy).then_inc(act_free, 1)
                    banks_read()
                    tell(xt_ready)

                def gate(q):
                    b = bank()
                    act.wait_ge(gate_free, n.up(gate_free))
                    act.activation(SILE[q], b[:, :], ACT.Silu).then_inc(act_free, 1)
                    banks_read()
                    tell(gate_silu)

                def outputs(e, q, reuse=True):
                    if reuse:
                        n.up(y_stored[q], 16)
                        act.wait_ge(y_stored[q], n.at(y_stored[q]))
                    for i in range(2):
                        b = bank()
                        act.activation(YE[q][:, i * BANK:(i + 1) * BANK], b[:, :], ACT.Copy).then_inc(act_free, 1)
                    banks_read()
                    act.dma_start(y_rows[bass.ds(e * CAP, CAP), :], YE[q]).then_inc(y_stored[q], 16)

                tokens(0)
                gate(0)
                tokens(1)
                reuse = layer > 0
                gate(1)
                tokens(0)
                outputs(0, 0, reuse)
                gate(0)
                tokens(1)
                outputs(1, 1, reuse)
                with act.Fori(0, TURNS) as i:
                    per = {act_full: 5 * EXPERTS_A_TURN, gate_free: EXPERTS_A_TURN}
                    per |= {y: 16 * EXPERTS_A_TURN // 2 for y in y_stored}
                    with n.repeat(i, TURNS, per):
                        for j in range(EXPERTS_A_TURN):
                            q = (3 + j) % 2
                            gate(q)
                            tokens(1 - q)
                            outputs(i * EXPERTS_A_TURN + (2 + j), 1 - q)
                gate(1)
                outputs(E - 2, 0)
                outputs(E - 1, 1)
                conditioning(COND_BACK[layer])
                act.wait_ge(overflow_known, layer + 1)
                with act.If(act.value_load(overflow[0:1, layer:layer + 1], min_val=0, max_val=1) > 0):
                    with act.Fori(0, E) as e:
                        act.wait_ge(left_products[layer], e + 1)
                        for f in range(FT):
                            ins = act.activation(SIL[:, f * T:(f + 1) * T], psum[f][:, 0:T], ACT.Silu)
                        ins.then_inc(left_silu[layer], 1)

            act.wait_ge(cond_in, 16)
            act.activation(cs[:, :], cs[:, :], ACT.Silu).then_inc(pe_from_act, 1)
            act.wait_ge(consts_in, 32)
            for layer in range(2):
                conditioning(COND_FIRST[layer])
                act.wait_ge(x_in, 16)
                squares(h[:, :], x[:, :])
                root(1.0 / D)
                conditioning(COND_NORM[layer])
                if layer == 0:
                    gdn()
                    hgrn()
                else:
                    ssd()
                conditioning(COND_MIXED[layer])
                squares(h[:, :], x[:, :])
                root(1.0 / D)
                conditioning(COND_AGAIN[layer])
                experts(layer)
            squares(h[:, :], x[:, :])
            root(1.0 / D)

        @block.vector
        def _(dve):
            n = Count()

            def bank():
                i = n.n.get(id(dve_full), 0)
                n.up(dve_full)
                dve.wait_ge(dve_full, n.at(dve_full))
                return psum[BANKS + i % BANKS]

            def freed(ins):
                ins.then_inc(dve_free, 1)
                dve.wait_ge(dve_free, n.at(dve_full))

            def step(ins):
                ins.then_inc(dve_step, 1)
                dve.wait_ge(dve_step, n.up(dve_step))

            def tell(what):
                dve.sem_inc(what, 1)

            def done(ins, what):
                step(ins)
                tell(what)

            def from_act():
                dve.wait_ge(to_dve, n.up(to_dve))

            tt, ts, stt, cp = dve.tensor_tensor, dve.tensor_scalar, dve.scalar_tensor_tensor, dve.tensor_copy

            def v3(ap, k_):
                return ap.rearrange("p (k n) -> p k n", k=k_)

            mods = [m_.rearrange("p (f m) -> p f m", m=MODS) for m_ in (mod0[:, :], MOD1)]
            modv = mods[0]

            def conditioning(groups):
                for layer, g_ in groups:
                    mv = mods[layer]
                    bias = W("b_ada")[:, 48 * layer + 4 * g_:48 * layer + 4 * g_ + 4]
                    b = bank()
                    freed(tt(mv[:, 4 * g_:4 * g_ + 4, :], v3(b[:, 0:4 * MODS], 4), spread(bias, 2, MODS), ALU.add))
                    tell(cond_turned)
                    if g_ in (3, 9):
                        first, name = (8, "norm_mix") if g_ == 3 else (32, "norm_ffn")
                        gain = W(name)[:, DK * layer:DK * (layer + 1)]
                        step(stt(mv[:, first:first + DK, :], mv[:, first:first + DK, :], 1.0, spread(gain, 2, MODS), ALU.add, ALU.mult))

            def normalise(first):
                from_act()
                step(dve.reciprocal(rs[:, :], rs[:, :]))
                step(tt(v3(h[:, :], DK), v3(x[:, :], DK), spread(rs[:, :], 1, DK), ALU.mult))
                if first is None:
                    for kk in range(DK):
                        last = ts(h[:, kk * T:(kk + 1) * T], h[:, kk * T:(kk + 1) * T], W("norm_final")[:, kk:kk + 1], None, ALU.mult)
                    done(last, out_ready)
                    return
                hs = v3(h[:, :], DK)[:, :, PROMPT:T].rearrange("p k (b l) -> p k b l", l=SEQ_LEN)
                for kk in range(DK):
                    ts(h[:, kk * T:kk * T + PROMPT], h[:, kk * T:kk * T + PROMPT], modv[:, first + DK + kk, 0:1], modv[:, first + kk, 0:1], ALU.mult, ALU.add)
                step(tt(hs, hs, spread(modv[:, first + DK:first + 2 * DK, 1:MODS], 3, SEQ_LEN), ALU.mult))
                tt(hs, hs, spread(modv[:, first:first + DK, 1:MODS], 3, SEQ_LEN), ALU.add).then_inc(pe_from_dve, 1)

            def residual(src, kk, gate, read):
                m0 = modv[:, gate + kk, 0:1]
                ms = spread(modv[:, gate + kk, 1:MODS], 2, SEQ_LEN)
                xk = x[:, kk * T:(kk + 1) * T]
                stt(xk[:, 0:PROMPT], src[:, 0:PROMPT], m0, xk[:, 0:PROMPT], ALU.mult, ALU.add)
                ins = tt(v3(rs[:, PROMPT:T], SEQS), v3(src[:, PROMPT:T], SEQS), ms, ALU.mult)
                read(ins)
                return tt(xk[:, PROMPT:T], xk[:, PROMPT:T], rs[:, PROMPT:T], ALU.add)

            def conv_states(UP, tiles, layer):
                dve.wait_ge(conv_state_in, 16 * (layer + 1))
                upv = v3(UP, tiles)
                dve.memset(upv[:, :, 0:PAD], 0.0)
                hist = upv[:, :, PAD + PROMPT:].rearrange("p k (b l) -> p k b l", l=PAD + SEQ_LEN)[:, :, :, 0:PAD]
                step(cp(hist, convst[:, 0:tiles * SEQS * PAD].rearrange("p (k b l) -> p k b l", k=tiles, b=SEQS)))

            def convolution(UP, CV, tiles, w):
                for f in range(tiles):
                    dve.wait_ge(conv_in_ready, n.up(conv_in_ready))
                    up = UP[:, f * UPW:(f + 1) * UPW]
                    cv = CV[:, (f % 4) * 348:(f % 4) * 348 + CVW]
                    if f >= 4:
                        dve.wait_ge(conv_silu, n.up(conv_silu))
                    step(ts(cv, up[:, 0:CVW], w[:, f * TAPS:f * TAPS + 1], None, ALU.mult))
                    for j in range(1, TAPS):
                        ins = stt(cv, up[:, j:j + CVW], w[:, f * TAPS + j:f * TAPS + j + 1], cv, ALU.mult, ALU.add)
                        if j < TAPS - 1:
                            step(ins)
                        else:
                            ins.then_inc(conv_ready, 1)
                n.up(conv_silu, 4)
                dve.wait_ge(conv_silu, n.at(conv_silu))
                upv = v3(UP, tiles)
                new = convnew[:, 0:tiles * MODS * PAD].rearrange("p (k m l) -> p k m l", k=tiles, m=MODS)
                cp(new[:, :, 0, :], upv[:, :, PROMPT:PROMPT + PAD])
                hist = upv[:, :, PAD + PROMPT:].rearrange("p k (b l) -> p k b l", l=PAD + SEQ_LEN)[:, :, :, SEQ_LEN:]
                done(cp(new[:, :, 1:, :], hist), out_ready)

            def log_decay(pre, t, e1, l1, nh, a_exp, bias, gl, dt_out):
                def hc(ap):
                    return ap.rearrange("p (h c) -> p h c", c=CHUNKS)
                step(tt(hc(t), pre, spread(bias, 2, CHUNKS), ALU.add))
                step(ts(e1, t, -1.0, None, ALU.mult))
                tt(e1, e1, t, ALU.min).then_inc(to_act, 1)
                from_act()
                step(stt(dt_out, t, 0.0, l1, ALU.max, ALU.add))
                step(ts(e1, dt_out, -1.0, None, ALU.mult))
                tt(hc(gl), hc(e1), spread(a_exp, 2, CHUNKS), ALU.mult).then_inc(pe_from_dve, 1)

            def decay_sums(gam, rem, nh):
                b = bank()
                np_ = nh * PC
                o = nh * CHUNKS
                for dst, at in ((gam, 0), (rem, o)):
                    d = dst.rearrange("p (h c) -> p h c", c=CHUNKS)
                    cp(d[:, :, 0:PC], b[0:C, at:at + np_].rearrange("p (h c) -> p h c", c=PC))
                    last = cp(d[:, :, PC], b[0:C, at + np_:at + o])
                freed(last)

            def each_bank(total, width):
                for i0 in range(0, total, width):
                    yield i0, min(width, total - i0), bank()

            def state_update(Sx, dec, b):
                for hh in range(HEADS):
                    last = stt(Sx[:, hh * P:(hh + 1) * P], Sx[:, hh * P:(hh + 1) * P], dec(hh), b[:, hh * P:(hh + 1) * P], ALU.mult, ALU.add)
                freed(last)

            def head_outputs(o, root_, gain, gate, dst):
                from_act()
                done(dve.reciprocal(root_[:, 0:T], root_[:, 0:T]), pe_from_dve)
                for i in range(HEADS):
                    b = bank()
                    freed(tt(o[:, i * T:(i + 1) * T], o[:, i * T:(i + 1) * T], b[:, 0:T], ALU.mult))
                step(stt(dst, o, gain, gate, ALU.mult, ALU.mult))

            def gdn():
                gl, t, e1, l1 = sc[:, 0:20], sc[:, 20:40], sc[:, 60:80], sc[:, 80:100]
                a_exp, gam, rem = sc[:, 100:104], sc[:, 120:140], sc[:, 140:160]
                egam, erem, beta, ba = sc[:, 160:180], sc[:, 180:200], sc[:, 200:220], sc[:, 240:280]
                bg = sc[:, 220:240]
                QT, KT = CO0[:, 0:B], CO0[:, B:2 * B]
                conv_states(UP0, AB_CONV, 0)
                b = bank()
                freed(cp(rs[0:C, 0:CHUNKS * AB_TAIL], b[0:C, 0:CHUNKS * AB_TAIL]))
                convolution(UP0, CV0, AB_CONV, W("ab_conv_w"))
                dve.wait_ge(weights_used, N_AB)
                dve.wait_ge(zeroed, 32)
                step(cp(ba, rs[0:C, 0:CHUNKS * AB_TAIL]))
                bav = ba.rearrange("p (c w) -> p w c", w=AB_TAIL)
                step(cp(beta.rearrange("p (h c) -> p h c", c=CHUNKS), bav[:, 0:HEADS, :]))
                log_decay(bav[:, HEADS:2 * HEADS, :], t, e1, l1, HEADS, a_exp, W("gdn_dt_bias")[0:C, :], gl, sc[:, 40:60])
                decay_sums(gam, rem, HEADS)
                tell(to_act)
                step(ts(beta, beta, 1.0, None, ALU.add))
                step(dve.reciprocal(beta, beta))
                from_act()
                step(tt(bg, beta, egam, ALU.mult))
                glv, bev = (q_.rearrange("p (h c) -> p h c", c=CHUNKS) for q_ in (gl, beta))
                inclv = incl.rearrange("p (c n) -> p c n", n=C)
                v4 = lambda ap: ap.rearrange("p (h c n) -> p h c n", h=HEADS, c=CHUNKS)
                tt(v4(EDEC), spread(inclv, 1, HEADS), spread(glv, 3, C), ALU.mult)
                tt(v4(U), spread(spread(ident64, 1, CHUNKS), 1, HEADS), spread(bev, 3, C), ALU.mult).then_inc(pe_from_dve, 1)
                for i0, w, b in each_bank(B, BANK):
                    freed(cp(GR[:, i0:i0 + w], b[:, 0:w]))
                for i0, w, b in each_bank(B, BANK):
                    freed(cp(BR[:, i0:i0 + w], b[0:C, 0:w]))
                step(tt(v3(EDEC, BLOCKS), v3(GR[0:C, :], BLOCKS), spread(gam, 2, C), ALU.subtract))
                ts(EDEC, EDEC, 0.0, None, ALU.min).then_inc(to_act, 1)
                from_act()
                step(tt(v4(EDEC), v4(EDEC), spread(inclv, 1, HEADS), ALU.mult))
                from_act()
                done(dve.reciprocal(SQ[:, 0:2 * T], SQ[:, 0:2 * T]), pe_from_dve)
                for i in range(2 * HEADS):
                    b = bank()
                    qk = CO0[:, i * T:(i + 1) * T]
                    freed(stt(qk, qk, float(P) ** -0.5 if i < HEADS else 1.0, b[:, 0:T], ALU.mult, ALU.mult))
                tell(pe_from_dve)
                for i0, w, b in each_bank(B, BANK):
                    freed(tt(U[:, i0:i0 + w], b[0:C, 0:w], EDEC[:, i0:i0 + w], ALU.mult))
                step(tt(U, U, BR, ALU.mult))
                for i0, w, b in each_bank(B, BANK):
                    freed(tt(QKE[:, i0:i0 + w], b[0:C, 0:w], EDEC[:, i0:i0 + w], ALU.mult))
                for i0, w, b in each_bank(BLOCKS * P, BANK):
                    q0 = i0 // P
                    tt(v3(BK[:, i0:i0 + w], 4), v3(b[0:C, :], 4), spread(bg[:, q0:q0 + 4], 2, P), ALU.mult)
                    freed(tt(v3(KEND[:, i0:i0 + w], 4), v3(b[0:C, :], 4), spread(erem[:, q0:q0 + 4], 2, P), ALU.mult))
                for i0, w, b in each_bank(BLOCKS * P, BANK):
                    q0 = i0 // P
                    freed(tt(v3(BV[:, i0:i0 + w], 4), v3(b[0:C, :], 4), spread(beta[:, q0:q0 + 4], 2, P), ALU.mult))
                cp(v3(M, BLOCKS), spread(ident64, 1, BLOCKS))
                step(cp(v3(MT, BLOCKS), spread(ident64, 1, BLOCKS)))
                dve.wait_ge(levels_in, 16)
                for lv in range(len(LEVELS)):
                    mk = levels.rearrange("p (l n) -> p l n", l=len(LEVELS))[:, len(LEVELS) - 1 - lv, :].rearrange("p (c n) -> p c n", n=C)
                    ct, mt = (CT, MT) if lv % 2 == 0 else (MT, CT)
                    tt(v4(ct), v4(U), spread(mk, 1, HEADS), ALU.mult).then_inc(pe_from_dve, 1)
                    if lv == 0:
                        for i0, w, b in each_bank(B, BANK):
                            freed(tt(M[:, i0:i0 + w], M[:, i0:i0 + w], b[0:C, 0:w], ALU.subtract))
                        step(tt(ct, mt, ct, ALU.subtract))
                        continue
                    for i0, w, b in each_bank(B, BANK):
                        freed(stt(ct[:, i0:i0 + w], b[0:C, 0:w], -1.0, mt[:, i0:i0 + w], ALU.mult, ALU.add))
                    if lv < len(LEVELS) - 1:
                        for i0, w, b in each_bank(B, BANK):
                            freed(stt(M[:, i0:i0 + w], b[0:C, 0:w], -1.0, M[:, i0:i0 + w], ALU.mult, ALU.add))
                tell(pe_from_dve)
                dve.memset(S, 0.0)
                done(tt(GR, QT, EGR, ALU.mult), pe_from_dve)
                lg = W("lb_logits")
                step(tt(LB[:, 12:16], lg[:, 0:4], lg[:, 4:8], ALU.max))
                step(tt(LB[:, 12:16], LB[:, 12:16], lg[:, 8:12], ALU.max))
                tt(v3(LB[:, 0:12], 3), v3(lg, 3), spread(LB[:, 12:16], 1, 3), ALU.subtract).then_inc(to_act, 1)
                from_act()
                step(tt(LB[:, 16:20], LB[:, 4:8], LB[:, 8:12], ALU.add))
                step(tt(LB[:, 20:24], LB[:, 16:20], LB[:, 0:4], ALU.add))
                step(dve.reciprocal(LB[:, 24:28], LB[:, 20:24]))
                tt(LB[:, 28:32], LB[:, 0:4], LB[:, 24:28], ALU.mult)
                step(tt(LB[:, 32:36], LB[:, 16:20], LB[:, 24:28], ALU.mult))
                for hh in range(HEADS):
                    cols = slice(hh * T, (hh + 1) * T)
                    ts(hf[:, cols], hf[:, cols], LB[:, 32 + hh:33 + hh], LB[:, 28 + hh:29 + hh], ALU.mult, ALU.add)
                    last = ts(hk[:, cols], hk[:, cols], LB[:, 32 + hh:33 + hh], None, ALU.mult)
                step(last)
                step(ts(hf, hf, 1e-19, None, ALU.max))
                tell(to_act)
                from_act()
                hv4 = lambda ap: ap.rearrange("p (h c n) -> p h c n", h=HEADS, c=CHUNKS)
                egr = EGR.rearrange("p (h t) -> p h t", h=HEADS)
                for c in range(CHUNKS):
                    b = bank()
                    cp(hv4(OI)[:, :, c, :], v3(b[:, HEADS * C:2 * HEADS * C], HEADS))
                    freed(tt(v3(VN, HEADS), hv4(UT)[:, :, c, :], v3(b[:, 0:HEADS * C], HEADS), ALU.subtract))
                    tell(pe_from_dve)
                    if c < PC:
                        b = bank()
                        state_update(S, lambda hh: egr[:, hh, c * C + C - 1:c * C + C], b)
                        if c < PC - 1:
                            tell(pe_from_dve)
                        else:
                            tell(out_ready)
                kv = KEND.rearrange("p (h c n) -> p h c n", h=HEADS, c=CHUNKS)[:, :, PC, :]
                for hh in range(HEADS):
                    last = tt(KENDM.rearrange("p (b h n) -> p b h n", b=SEQS, h=HEADS)[:, :, hh, :], spread(kv[:, hh, :], 1, SEQS), spread(seq, 2, P), ALU.mult)
                done(last, pe_from_dve)
                for s_ in range(SEQS):
                    b = bank()
                    at = PROMPT + s_ * SEQ_LEN + SEQ_LEN - 1
                    state_update(SS[:, s_ * HEADS * P:(s_ + 1) * HEADS * P], lambda hh: egr[:, hh, at:at + 1], b)
                tell(out_ready)
                for i0, w, b in each_bank(B, BANK):
                    freed(tt(OI[:, i0:i0 + w], b[:, 0:w], OI[:, i0:i0 + w], ALU.add))
                tell(to_act)
                head_outputs(OI, SQ[:, B:2 * B], W("gdn_norm"), zs, h[:, 0:B])
                tell(out_ready)

            def hgrn():
                dve.wait_ge(stored, 48)
                for hh in range(HEADS):
                    cols = slice(hh * T, (hh + 1) * T)
                    last = dve.tensor_tensor_scan(CUM[:, cols], restart, hf[:, cols], 0.0, ALU.mult, ALU.add)
                step(last)
                for i0, w, b in each_bank(B, BANK):
                    freed(tt(v3(ATT[0:C, i0:i0 + w], w // C), v3(b[0:C, 0:w], w // C), spread(ident64, 1, w // C), ALU.mult))
                def halves(buf, hh, half):
                    used = T if half < SEQ_LEN else PROMPT
                    return buf[:, hh * T:hh * T + used].rearrange("p (n two w) -> p n two w", two=2, w=half)

                def distances(lv, half):
                    eds = (ED0, ED1)[lv % 2]
                    for hh in range(HEADS):
                        cu, ed = halves(CUM, hh, half), halves(eds, hh, half)
                        mid = spread(cu[:, :, 0, half - 1], 2, half)
                        tt(ed[:, :, 0, :], mid, cu[:, :, 0, :], ALU.subtract)
                        last = tt(ed[:, :, 1, :], cu[:, :, 1, :], mid, ALU.subtract)
                        if half >= SEQ_LEN:
                            last = dve.memset(eds[:, hh * T + PROMPT:(hh + 1) * T], 0.0)
                    done(last, to_act)

                def merge(lv, half):
                    mk = levels.rearrange("p (l n) -> p l n", l=len(LEVELS))[:, lv, :]
                    for i0, w, b in each_bank(B, BANK):
                        i, end = i0 // C, (i0 + w) // C
                        runs = []
                        while i < end:
                            hh, c = divmod(i, CHUNKS)
                            stop = min(end - i, (CHUNKS if half < SEQ_LEN else PC) - c)
                            if stop > 0:
                                runs.append((i, c, stop))
                            i += max(1, min(end - i, CHUNKS - c))
                        for i, c, m_ in runs:
                            last = dve.copy_predicated(ATT[0:C, i * C:(i + m_) * C], mk[:, c * C:(c + m_) * C].bitcast(U32),
                                                       b[0:C, i * C - i0:(i + m_) * C - i0])
                        freed(last)

                distances(0, LEVELS[0])
                for lv, half in enumerate(LEVELS):
                    if lv + 1 < len(LEVELS):
                        distances(lv + 1, LEVELS[lv + 1])
                    from_act()
                    zz = Z[lv % 2]
                    for hh in range(HEADS):
                        ed, zv = halves((ED0, ED1)[lv % 2], hh, half), halves(zz, hh, half)
                        tt(zv[:, :, 0, :], ed[:, :, 0, :], halves(hk, hh, half)[:, :, 0, :], ALU.mult)
                        last = tt(zv[:, :, 1, :], ed[:, :, 1, :], halves(hq, hh, half)[:, :, 1, :], ALU.mult)
                    done(last, pe_from_dve)
                    if lv:
                        merge(lv - 1, LEVELS[lv - 1])
                merge(len(LEVELS) - 1, LEVELS[-1])
                cum4 = CUM.rearrange("p (h t) -> p h t", h=HEADS)
                ke4 = KE.rearrange("p (h t) -> p h t", h=HEADS)
                for hh in range(HEADS):
                    for lo_, hi_, w in ((0, PROMPT, C), (PROMPT, T, SEQ_LEN)):
                        cu = cum4[:, hh, lo_:hi_].rearrange("p (n w) -> p n w", w=w)
                        ke = ke4[:, hh, lo_:hi_].rearrange("p (n w) -> p n w", w=w)
                        last = tt(ke, spread(cu[:, :, w - 1], 2, w), cu, ALU.subtract)
                done(last, to_act)
                from_act()
                step(tt(KE, KE, hk, ALU.mult))
                tell(pe_from_dve)
                dve.memset(SHG, 0.0)
                step(tt(ED0, hq, EC, ALU.mult))
                tell(pe_from_dve)
                from_act()
                ov = OIH.rearrange("p (h c n) -> p h c n", h=HEADS, c=CHUNKS)
                ec = EC.rearrange("p (h t) -> p h t", h=HEADS)
                for c in range(PC):
                    b = bank()
                    freed(cp(ov[:, :, c, :], v3(b[:, 0:HEADS * C], HEADS)))
                    b = bank()
                    state_update(SHG, lambda hh: ec[:, hh, c * C + C - 1:c * C + C], b)
                    tell(pe_from_dve if c < PC - 1 else out_ready)
                kv = KENDH.rearrange("p (h c n) -> p h c n", h=HEADS, c=CHUNKS)[:, :, PC, :]
                for hh in range(HEADS):
                    last = tt(KENDMH.rearrange("p (b h n) -> p b h n", b=SEQS, h=HEADS)[:, :, hh, :], spread(kv[:, hh, :], 1, SEQS), spread(seq, 2, P), ALU.mult)
                done(last, pe_from_dve)
                from_act()
                for s_ in range(SEQS):
                    b = bank()
                    at = PROMPT + s_ * SEQ_LEN + SEQ_LEN - 1
                    state_update(SSH[:, s_ * HEADS * P:(s_ + 1) * HEADS * P], lambda hh: ec[:, hh, at:at + 1], b)
                tell(out_ready)
                tell(ring_opens)
                for i0, w, b in each_bank(B, BANK):
                    freed(tt(OIH[:, i0:i0 + w], b[:, 0:w], OIH[:, i0:i0 + w], ALU.add))
                tell(to_act)
                head_outputs(OIH, Z[1], W("hgrn_norm"), hg, h[:, B:2 * B])
                tell(pe_from_dve)
                dve.wait_ge(stored, 80)
                tell(mixer_done)

            def ssd():
                n5 = SH * CHUNKS
                gl, t, e1, l1, dt = (sc1[:, i * n5:(i + 1) * n5] for i in range(5))
                gam, rem = e1, l1
                a_exp = sc1[:, 5 * n5:5 * n5 + SH]
                conv_states(UP1, SXBC, 1)
                b = bank()
                freed(cp(rs[0:C, 0:n5], b[0:C, 0:n5]))
                convolution(UP1, CV1, SXBC, W("ssd_conv_w"))
                dve.wait_ge(weights_used, N_SSD)
                log_decay(rs[0:C, 0:n5].rearrange("p (c h) -> p h c", c=CHUNKS), t, e1, l1, SH, a_exp, W("ssd_dt_bias")[0:C, :], gl, dt)
                decay_sums(gam, rem, SH)
                tell(to_act)
                b = bank()
                freed(cp(G, b[0:SH, 0:T]))
                cp(v3(SEL, SH), spread(ident[0:SH, 0:SH], 2, C))
                glv = gl.rearrange("p (h c) -> p c h", c=CHUNKS)
                tt(GS.rearrange("p (b h) -> p b h", b=SEQS), spread(glv[:, PC, :], 1, SEQS), spread(seq, 2, SH), ALU.mult).then_inc(pe_from_dve, 1)
                from_act()
                b = bank()
                freed(cp(DEC, b[:, 0:(PC + SEQS) * SH]))
                tell(to_act)
                from_act()
                dve.memset(ST, 0.0)
                decv = DEC.rearrange("p (c h) -> p c h", h=SH)

                def norm_of_group(gi):
                    step(dve.reciprocal(rs[:, :], rs[:, :]))
                    for j in range(4):
                        q = 4 * gi + j
                        xt = CO1[:, q * T:(q + 1) * T]
                        last = stt(xt, xt, W("ssd_norm")[:, q:q + 1], rs[:, :], ALU.mult, ALU.mult)
                    step(last)

                for gi in range(SG):
                    hs = slice(gi * SHPG * CHUNKS, (gi + 1) * SHPG * CHUNKS)

                    def g8(ap):
                        return ap[:, hs].rearrange("p (h c) -> p h c", c=CHUNKS)
                    er = ER[gi % 2].rearrange("p (j c n) -> p j c n", j=4, c=CHUNKS)
                    b = bank()
                    freed(tt(CBM, b[0:C, 0:T], incl, ALU.mult))
                    v4 = lambda ap: ap.rearrange("p (h c n) -> p h c n", h=SHPG, c=CHUNKS)
                    for hh in range(SHPG):
                        b = bank()
                        freed(tt(v4(EG1)[:, hh], v3(b[0:C, 0:T], CHUNKS), spread(g8(gam)[:, hh], 2, C), ALU.subtract))
                    ts(EG1, EG1, 0.0, None, ALU.min).then_inc(to_act, 1)
                    xdt = XDT.rearrange("p (c h n) -> p c h n", c=CHUNKS, h=SHPG)
                    xend = XEND.rearrange("p (c h n) -> p c h n", c=CHUNKS, h=SHPG)
                    for c in range(CHUNKS):
                        b = bank()
                        freed(tt(xdt[:, c], v3(b[0:C, :], SHPG), spread(g8(dt)[:, :, c], 2, C), ALU.mult))
                    for c in range(CHUNKS):
                        tt(xend[:, c], xdt[:, c], spread(g8(rem)[:, :, c], 2, C), ALU.mult)
                    from_act()
                    tt(v3(BM, SEQS), spread(BTOK[gi % 2][:, PC * P:CHUNKS * P], 1, SEQS), spread(seq, 2, P), ALU.mult).then_inc(pe_from_dve, 1)
                    yi = YI.rearrange("p (j c n) -> p j c n", j=4, c=CHUNKS)
                    stg = ST[:, gi * BANK:(gi + 1) * BANK]
                    for c in range(PC):
                        b = bank()
                        freed(tt(yi[:, :, c, :], v3(b[:, 0:4 * C], 4), er[:, :, c, :], ALU.mult))
                        step(tt(v3(stg, SHPG), v3(stg, SHPG), spread(decv[:, c, gi * SHPG:(gi + 1) * SHPG], 2, C), ALU.mult))
                        b = bank()
                        freed(tt(stg, b[:, :], stg, ALU.add))
                        if c < PC - 1:
                            tell(pe_from_dve)
                    if gi:
                        from_act()
                    from_act()
                    tt(v4(EG1), v4(EG1), spread(CBM.rearrange("p (c n) -> p c n", n=C), 1, SHPG), ALU.mult).then_inc(pe_from_dve, 1)
                    from_act()
                    tt(yi[:, :, PC, :], yi[:, :, PC, :], er[:, :, PC, :], ALU.mult)
                    for s_ in range(SEQS):
                        st = SSS[gi % 2][:, s_ * BANK:(s_ + 1) * BANK]
                        step(tt(v3(st, SHPG), v3(st, SHPG), spread(decv[:, PC + s_, gi * SHPG:(gi + 1) * SHPG], 2, C), ALU.mult))
                        b = bank()
                        freed(tt(st, b[:, :], st, ALU.add))
                    tell(out_ready)
                    if gi == SG - 1:
                        tell(ring_opens)
                    for j in range(4):
                        q = 4 * gi + j
                        xt, yt = CO1[:, q * T:(q + 1) * T], YI[:, j * T:(j + 1) * T]
                        step(stt(yt, xt, W("ssd_d")[:, q:q + 1], yt, ALU.mult, ALU.add))
                        b = bank()
                        freed(tt(yt, b[:, 0:T], yt, ALU.add))
                        last = tt(xt, yt, zs1[:, q * T:(q + 1) * T], ALU.mult)
                    step(last)
                    if gi:
                        norm_of_group(gi - 1)
                    tell(to_act)
                from_act()
                norm_of_group(SG - 1)
                tell(pe_from_dve)
                tell(out_ready)
                dve.wait_ge(stored, 112)
                for i in range(2):
                    dve.wait_ge(stored_state[i], 16 * SG // 2)
                tell(mixer_done)

            def route(layer):
                sg, bi = R[:, 100:180], R[:, 180:260]
                b = bank()
                freed(cp(sg, b[0:C, 0:CHUNKS * E]))
                tell(to_act)
                from_act()
                step(tt(v3(bi, CHUNKS), v3(sg, CHUNKS), spread(W("router_b")[0:C, :], 1, CHUNKS), ALU.add))
                v = bi.rearrange("p (g e) -> p g e", e=EPG)
                NG = CHUNKS * EG
                t = [R[:, 300 + 20 * i:320 + 20 * i] for i in range(20)]
                hi1, lo1, hi2, lo2, mid, m1, m2, gs, gsel = t[:9]
                tt(hi1, v[:, :, 0], v[:, :, 1], ALU.max)
                tt(lo1, v[:, :, 0], v[:, :, 1], ALU.min)
                tt(hi2, v[:, :, 2], v[:, :, 3], ALU.max)
                step(tt(lo2, v[:, :, 2], v[:, :, 3], ALU.min))
                tt(m1, hi1, hi2, ALU.max)
                tt(mid, hi1, hi2, ALU.min)
                step(tt(m2, lo1, lo2, ALU.max))
                step(tt(m2, m2, mid, ALU.max))
                step(tt(gs, m1, m2, ALU.add))
                gmax, nf = R[:, 800:805], R[:, 810:815]
                gv, sv = (q.rearrange("p (c g) -> p c g", g=EG) for q in (gs, gsel))
                dve.memset(nf, 1.0)
                step(dve.tensor_reduce(gmax, gv, AX.X, ALU.max))
                for g_ in range(EG):
                    step(tt(sv[:, :, g_], gv[:, :, g_], gmax, ALU.is_equal))
                    step(tt(sv[:, :, g_], sv[:, :, g_], nf, ALU.mult))
                    step(tt(nf, nf, sv[:, :, g_], ALU.subtract))
                cmpv = R[:, 900:900 + NG * EPG * 3].rearrange("p (g e j) -> p g e j", g=NG, e=EPG)
                for e in range(EPG):
                    for q, j in enumerate([j for j in range(EPG) if j != e]):
                        last = tt(cmpv[:, :, e, q], v[:, :, j], v[:, :, e], ALU.is_ge if j < e else ALU.is_gt)
                step(last)
                cnt = R[:, 1200:1200 + NG * EPG]
                step(dve.tensor_reduce(cnt, R[:, 900:900 + NG * EPG * 3].rearrange("p (g j) -> p g j", j=3), AX.X, ALU.add))
                step(ts(cnt, cnt, 1.5, None, ALU.is_lt))
                cg = cnt.rearrange("p (g e) -> p g e", e=EPG)
                step(tt(cg, cg, spread(gsel, 2, EPG), ALU.mult))
                tell(pe_from_dve)
                ce = lambda ap: ap.rearrange("p (c e) -> p c e", e=E)
                w, tot = R[:, 1600:1680], R[:, 820:825]
                step(tt(w, cnt, sg, ALU.mult))
                step(dve.tensor_reduce(tot, ce(w), AX.X, ALU.add))
                step(dve.reciprocal(tot, tot))
                step(tt(ce(w), ce(w), spread(tot, 2, E), ALU.mult))
                order, pick = R[:, 1280:1360], R[:, 1360:1520]
                og = order.rearrange("p (g e) -> p g e", e=EPG)
                step(cp(og[:, :, 0], cg[:, :, 0]))
                for e in range(1, EPG):
                    step(tt(og[:, :, e], og[:, :, e - 1], cg[:, :, e], ALU.add))
                for k_ in range(2):
                    stt(pick[:, k_ * 80:(k_ + 1) * 80], order, float(k_ + 1), cnt, ALU.is_equal, ALU.mult)
                upto, row = R[:, 1980:2060], R[:, 1520:1600]
                fits, prod = R[:, 1870:1950], R[:, 1680:1840]
                conditioning(COND_ROUTE[layer])
                b = bank()
                cp(R[:, 2060:2076], b[0:C, 0:E])
                freed(cp(upto, b[0:C, E:E + CHUNKS * E]))
                step(ts(fits, upto, CAP + 0.5, None, ALU.is_lt))
                step(tt(ce(row), ce(upto), spread(K("row0", C), 1, CHUNKS), ALU.add))
                step(tt(v3(pick, 2), v3(pick, 2), spread(fits, 1, 2), ALU.mult))
                kce = lambda ap: ap.rearrange("p (k c e) -> p (k c) e", k=2, c=CHUNKS)
                rows, placed, wk, spare = R[:, 1840:1850], R[:, 1860:1870], R[:, 1850:1860], K("spare", C)
                step(dve.tensor_reduce(placed, kce(pick), AX.X, ALU.add))
                step(tt(v3(prod, 2), v3(pick, 2), spread(row, 1, 2), ALU.mult))
                step(dve.tensor_reduce(rows, kce(prod), AX.X, ALU.add))
                step(tt(v3(prod, 2), v3(pick, 2), spread(w, 1, 2), ALU.mult))
                step(dve.tensor_reduce(wk, kce(prod), AX.X, ALU.add))
                step(tt(placed, placed, spare, ALU.mult))
                step(tt(rows, rows, placed, ALU.subtract))
                step(tt(rows, rows, spare, ALU.add))
                done(cp(R[:, 1960:1970].bitcast(mybir.dt.uint32), rows), rows_ready)
                most = R[0:1, 2076:2077]
                step(dve.tensor_reduce(most, R[0:1, 2060:2076], AX.X, ALU.max))
                step(ts(most, most, CAP + 0.5, None, ALU.is_gt))
                done(cp(overflow[0:1, layer:layer + 1], most), overflow_known)

            def experts(layer):
                route(layer)
                conditioning(COND_MOVE[layer])
                wk = R[:, 1850:1860]

                def hidden_turned(q):
                    b = bank()
                    freed(cp(AT[q], b[:, :]))
                    tell(act_turned)

                def hidden(q):
                    b = bank()
                    dve.wait_ge(gate_silu, n.up(gate_silu))
                    freed(tt(ACTS[q], b[:, :], SILE[q], ALU.mult))
                    tell(act_ready)
                    tell(gate_free)

                hidden(0)
                with dve.Fori(0, TURNS) as i:
                    with n.repeat(i, TURNS, {dve_full: 2 * EXPERTS_A_TURN, gate_silu: EXPERTS_A_TURN}):
                        for j in range(EXPERTS_A_TURN):
                            q = (1 + j) % 2
                            hidden_turned(1 - q)
                            hidden(q)
                for e in range(1 + TURNS * EXPERTS_A_TURN, E):
                    hidden_turned(1 - e % 2)
                    hidden(e % 2)
                hidden_turned((E - 1) % 2)
                conditioning(COND_BACK[layer])
                dve.wait_ge(gathered, 16 * 2 * CHUNKS * (layer + 1))
                xv = v3(x[:, :], DK)
                for c in range(CHUNKS):
                    y0, y1 = YG[:, c * D:(c + 1) * D], YG[:, (CHUNKS + c) * D:(CHUNKS + c + 1) * D]
                    step(ts(y0, y0, wk[:, c:c + 1], None, ALU.mult))
                    done(stt(y0, y1, wk[:, CHUNKS + c:CHUNKS + c + 1], y0, ALU.mult, ALU.add), pe_from_dve)
                for c in range(CHUNKS):
                    b = bank()
                    if c < PC:
                        freed(tt(v3(TMP, DK), v3(b[:, :], DK), spread(modv[:, 40:48, 0], 2, C), ALU.mult))
                    else:
                        four = lambda ap: ap.rearrange("p (k b l) -> p k b l", k=DK, b=SEQS)
                        freed(tt(four(TMP), four(b[:, :]), spread(modv[:, 40:48, 1:MODS], 3, SEQ_LEN), ALU.mult))
                    xc = xv[:, :, c * C:(c + 1) * C]
                    step(tt(xc, xc, v3(TMP, DK), ALU.add))
                with dve.If(dve.value_load(overflow[0:1, layer:layer + 1], min_val=0, max_val=1) > 0):
                    overflow_pass(layer)

            def overflow_pass(layer):
                m = Count()
                own = left_step[layer]

                def step(ins):
                    ins.then_inc(own, 1)
                    dve.wait_ge(own, m.up(own))

                w, fits, left = R[:, 1600:1680], R[:, 1870:1950], R[:, 1680:1760]
                step(tt(left, w, fits, ALU.mult))
                step(tt(left, w, left, ALU.subtract))
                cp(R[:, 0:80].rearrange("p (e c) -> p e c", c=CHUNKS), left.rearrange("p (c e) -> p e c", e=E)).then_inc(left_ready[layer], 1)
                step(dve.memset(YACC, 0.0))
                for e in range(E):
                    dve.wait_ge(left_full[layer], e + 1)
                    step(cp(COMB[:, e * T:(e + 1) * T], psum[e % (2 * BANKS)][:, 0:T]))
                    if e % (2 * BANKS) == 2 * BANKS - 1:
                        dve.sem_inc(left_banks_free[layer], 1)
                with dve.Fori(0, E) as e:
                    with m.repeat(e, E, {own: 2 * FT + DK}):
                        dve.wait_ge(left_silu[layer], e + 1)
                        for f in range(FT):
                            dst = ACTV[:, f * T:(f + 1) * T]
                            step(tt(dst, psum[BANKS + f][:, 0:T], SIL[:, f * T:(f + 1) * T], ALU.mult))
                            step(tt(dst, dst, COMB[:, bass.ds(e * T, T)], ALU.mult))
                        dve.sem_inc(left_hidden[layer], 1)
                        dve.wait_ge(left_outputs[layer], e + 1)
                        for dt_ in range(DK):
                            y = YACC[:, dt_ * T:(dt_ + 1) * T]
                            step(tt(y, psum[dt_][:, 0:T], y, ALU.add))
                        dve.sem_inc(left_banks_free[layer], 1)
                for kk in range(DK):
                    step(residual(YACC[:, kk * T:(kk + 1) * T], kk, 40, step))

            dve.wait_ge(consts_in, 32)
            dve.sem_inc(gate_free, 2)
            for layer in range(2):
                tell(to_act)
                modv = mods[layer]
                conditioning(COND_FIRST[layer])
                normalise(0)
                conditioning(COND_NORM[layer])
                if layer == 0:
                    gdn()
                    hgrn()
                else:
                    ssd()
                conditioning(COND_MIXED[layer])
                for kk in range(DK):
                    b = bank()
                    step(residual(b, kk, 16, freed))
                tell(to_act)
                normalise(24)
                conditioning(COND_AGAIN[layer])
                experts(layer)
            tell(to_act)
            normalise(None)


_WEIGHTS = ("w_ada", "ab_w_in", "ab_w_out", "ssd_w_in", "ssd_w_out", "moe_w_gate", "moe_w_up", "moe_w_down")


def _constants():
    def put(a, name, v):
        at, cols = CONST[name]
        a[:v.shape[0], at:at + cols] = v.reshape(v.shape[0], cols)

    a = np.zeros((P, CONST_COLS), np.float32)
    s, t = np.arange(C)[:, None], np.arange(C)[None, :]
    same = s // SEQ_LEN == t // SEQ_LEN
    put(a, "ones", np.ones((P, P), np.float32))
    put(a, "ident", np.eye(P, dtype=np.float32))
    put(a, "incl", np.stack([s <= t] * PC + [(s <= t) & same], 1).astype(np.float32))
    put(a, "after", np.stack([s > t, (s > t) & same], 1).astype(np.float32))
    put(a, "seq", (s // SEQ_LEN == np.arange(SEQS)[None, :]).astype(np.float32))
    tok = np.arange(T)
    first = np.where(tok < PROMPT, tok % C == 0, (tok - PROMPT) % SEQ_LEN == 0)
    put(a, "restart", np.broadcast_to(1.0 - first.astype(np.float32), (P, T)))
    put(a, "eps", np.full((P, 1), EPS, np.float32))
    put(a, "row0", np.broadcast_to(np.arange(E, dtype=np.float32) * CAP - 1, (P, E)))
    token = np.arange(C)[:, None, None] + C * np.arange(CHUNKS)[None, None, :]
    put(a, "spare", (SPARE + 2 * token + np.arange(2)[None, :, None]).astype(np.float32))
    levels = []
    for half in LEVELS:
        m = (s // (2 * half) == t // (2 * half)) & (s // half % 2 == 0) & (t // half % 2 == 1)
        levels.append(np.stack([m] * PC + [m & (half < SEQ_LEN)], 1))
    return a, np.stack(levels, 1).astype(np.float32).reshape(C, -1)


def _small(v):
    a = np.zeros((P, SMALL_COLS), np.float32)

    def put(name, x):
        at, cols = SMALL[name]
        a[:, at:at + cols] = x

    def features(x):
        x = np.asarray(x)
        return x.reshape(-1, P).T

    def taps(w):
        return np.asarray(w).reshape(TAPS, -1, P).transpose(2, 1, 0).reshape(P, -1)

    for name in ("norm_mix", "norm_ffn", "norm_final", "b_ada", "gdn_norm", "hgrn_norm", "ssd_conv_b", "ssd_norm"):
        put(name, features(v[name]))
    put("lb_logits", features(v["hgrn_lb_logits"]))
    put("ab_conv_w", taps(v["ab_conv_w"]))
    put("ssd_conv_w", taps(v["ssd_conv_w"]))
    put("ssd_d", features(np.repeat(np.asarray(v["ssd_d"]).reshape(-1), C)))
    for name in ("gdn_a_log", "gdn_dt_bias", "ssd_a_log", "ssd_dt_bias", "router_b"):
        put(name, np.broadcast_to(np.asarray(v[name]).reshape(1, -1), (P, SMALL[name][1])))
    return a


def kernel(**v):
    import concourse.bacc as bacc
    from concourse.bass_utils import run_bass_kernel_spmd

    v = {name: np.asarray(x) for name, x in v.items()}

    def conv_t(st):
        return st[0].reshape(SEQS, PAD, -1, P).transpose(3, 2, 0, 1).reshape(P, -1)

    consts, levels = _constants()
    arrays = {
        "consts": consts, "levels": levels, "small": _small(v),
        "x_t": np.concatenate([v["x_prompt"].reshape(-1, D), v["x_sample"].reshape(-1, D)]).T,
        "c_t": np.concatenate([v["c_prompt"], v["c_sample"]]).T,
        "router_w": v["router_w"],
        "gdn_conv_t": conv_t(v["state_gdn_conv"]), "ssd_conv_t": conv_t(v["state_ssd_conv"]),
        "gdn_state": v["state_gdn"][0].transpose(2, 0, 1, 3).reshape(P, -1),
        "hgrn_state": v["state_hgrn"][0].transpose(2, 0, 1, 3).reshape(P, -1),
        "ssd_state": v["state_ssd"][0].transpose(3, 0, 1, 2).reshape(P, SEQS, -1),
    }
    arrays |= {name: v[name] for name in _WEIGHTS}
    arrays = {name: np.ascontiguousarray(x) for name, x in arrays.items()}
    shapes = {"y": (D, T), "gdn_p": (P, HEADS * P), "gdn_s": (P, SEQS * HEADS * P), "gdn_conv": (P, AB_CONV * MODS * PAD),
              "hgrn_p": (P, HEADS * P), "hgrn_s": (P, SEQS * HEADS * P), "ssd_p": (P, SH * C), "ssd_s": (P, SEQS, SH * C),
              "ssd_conv": (P, SXBC * MODS * PAD)}
    nc = bacc.Bacc("TRN2", target_bir_lowering=False, num_devices=1)
    a = {name: nc.dram_tensor(name + "_in", x.shape, F32, kind="ExternalInput").ap() for name, x in arrays.items()}
    out = {name: nc.dram_tensor(name + "_out", shape, F32, kind="ExternalOutput").ap() for name, shape in shapes.items()}
    trunk_program(nc, a, out)
    r = run_bass_kernel_spmd(nc, [{name + "_in": x for name, x in arrays.items()}], core_ids=[0]).results[0]
    r = {name: r[name + "_out"] for name in shapes}

    def conv_out(m):
        m = m.reshape(P, -1, MODS, PAD).transpose(2, 3, 1, 0).reshape(1, MODS, PAD, -1)
        return m[:, 0:1], m[:, 1:]

    y = r["y"].T
    gc, sc_ = conv_out(r["gdn_conv"]), conv_out(r["ssd_conv"])
    heads = lambda m: m.reshape(P, -1, HEADS, P).transpose(1, 2, 0, 3)[None]
    got = (y[:PROMPT].reshape(1, PROMPT, D), y[PROMPT:].reshape(SEQS, SEQ_LEN, D),
           heads(r["gdn_p"]), gc[0], heads(r["hgrn_p"]), r["ssd_p"].reshape(P, 1, SH, C).transpose(1, 2, 3, 0)[None], sc_[0],
           heads(r["gdn_s"]), gc[1], heads(r["hgrn_s"]), r["ssd_s"].reshape(P, SEQS, SH, C).transpose(1, 2, 3, 0)[None], sc_[1])
    return tuple(np.ascontiguousarray(g) for g in got)
```
